# Optimizing a Trainium2 kernel written in Bass

```python
import jax, jax.numpy as jnp
from jax import lax
import numpy as np
import jax
import jax.numpy as jnp

D_MODEL = 1024
BATCH = 1
SEQ = 1024
DEPTH = 1

MIX_WIDTH = 512
N_BRANCH = 4
MLA_HEADS = 8
QK_NOPE = 64
QK_ROPE = 32
V_HEAD = 64
Q_LORA = 384
KV_LORA = 256
ROPE_THETA = 10000.0
Q_BLOCK = 128
POOL_WINDOWS = (2, 4, 8, 16)
POOL_GROUP = MIX_WIDTH // 4
SSD_HEADS = 8
SSD_HEADDIM = 64
SSD_GROUPS = 2
SSD_STATE = 64
SSD_CHUNK = 128
CONV_WIDTH = 4
SSD_XBC = SSD_HEADS * SSD_HEADDIM + 2 * SSD_GROUPS * SSD_STATE
LRU_BLOCKS = 8
LRU_BLOCK = MIX_WIDTH // LRU_BLOCKS
LRU_C = 8.0
D_FF = 4 * D_MODEL
PLE_DIM = 256
EPS = 1e-6

SPLIT_SIZES = (Q_LORA, KV_LORA, QK_ROPE,
               MIX_WIDTH,
               MIX_WIDTH, SSD_XBC, SSD_HEADS,
               MIX_WIDTH, MIX_WIDTH,
               N_BRANCH * D_MODEL)
IN_COLS = sum(SPLIT_SIZES)


def _split_points():
    pts, acc = [], 0
    for s in SPLIT_SIZES[:-1]:
        acc += s
        pts.append(acc)
    return pts

def rmsnorm(x, g):
    x32 = x.astype(jnp.float32)
    y = x32 * lax.rsqrt(jnp.mean(x32 * x32, axis=-1, keepdims=True) + EPS)
    return (y * g.astype(jnp.float32)).astype(x.dtype)

def causal_dwconv(x, w, b):
    c = x.shape[-1]
    y = lax.conv_general_dilated(x, w[:, None, :].astype(x.dtype), window_strides=(1,),
                                 padding=[(CONV_WIDTH - 1, 0)],
                                 dimension_numbers=('NWC', 'WIO', 'NWC'),
                                 feature_group_count=c)
    return y + b.astype(x.dtype)

def rope_tables(positions):
    inv = 1.0 / (ROPE_THETA ** (jnp.arange(0, QK_ROPE, 2, dtype=jnp.float32) / QK_ROPE))
    ang = positions.astype(jnp.float32)[..., None] * inv
    return jnp.cos(ang), jnp.sin(ang)

def apply_rope(x, cos, sin):
    x32 = x.astype(jnp.float32)
    x1, x2 = jnp.split(x32, 2, axis=-1)
    out = jnp.concatenate([x1 * cos - x2 * sin, x2 * cos + x1 * sin], axis=-1)
    return out.astype(x.dtype)

def mla_mixer(c_q, c_kv, k_r, cos, sin, q_norm, w_uq, kv_norm, w_ukv):
    b, s, _ = c_q.shape
    q = (rmsnorm(c_q, q_norm) @ w_uq).reshape(b, s, MLA_HEADS, QK_NOPE + QK_ROPE)
    q_nope = q[..., :QK_NOPE]
    q_rope = apply_rope(q[..., QK_NOPE:], cos[:, :, None], sin[:, :, None])
    kv = (rmsnorm(c_kv, kv_norm) @ w_ukv).reshape(b, s, MLA_HEADS, QK_NOPE + V_HEAD)
    k_nope, v = kv[..., :QK_NOPE], kv[..., QK_NOPE:]
    k_rope = apply_rope(k_r, cos, sin)
    scale = (QK_NOPE + QK_ROPE) ** -0.5
    outs = []
    for blk in range(s // Q_BLOCK):
        q0, kend = blk * Q_BLOCK, (blk + 1) * Q_BLOCK
        sc = (jnp.einsum('bqhd,bkhd->bhqk', q_nope[:, q0:kend], k_nope[:, :kend])
              + jnp.einsum('bqhd,bkd->bhqk', q_rope[:, q0:kend], k_rope[:, :kend]))
        sc = sc.astype(jnp.float32) * scale
        qi = q0 + jnp.arange(Q_BLOCK)[:, None]
        ki = jnp.arange(kend)[None, :]
        sc = jnp.where(ki <= qi, sc, -jnp.inf)
        pr = jax.nn.softmax(sc, axis=-1).astype(v.dtype)
        outs.append(jnp.einsum('bhqk,bkhd->bqhd', pr, v[:, :kend]))
    o = jnp.concatenate(outs, axis=1)
    return o.reshape(b, s, MLA_HEADS * V_HEAD)

def pool_mixer(u, w_pool, pool_scale):
    b, s, _ = u.shape
    u32 = u.astype(jnp.float32)
    maxw = max(POOL_WINDOWS)
    cs = jnp.pad(jnp.cumsum(u32, axis=1), ((0, 0), (maxw, 0), (0, 0)))
    t = jnp.arange(s)
    groups = []
    for g, w in enumerate(POOL_WINDOWS):
        sl = slice(g * POOL_GROUP, (g + 1) * POOL_GROUP)
        win_sum = cs[:, maxw:, sl] - cs[:, maxw - w:maxw - w + s, sl]
        count = jnp.minimum(t + 1, w).astype(jnp.float32)[None, :, None]
        groups.append(win_sum / count - u32[..., sl])
    d = jnp.stack(groups, axis=2).astype(u.dtype)
    y = jnp.einsum('bsgc,gcd->bsgd', d, w_pool).reshape(b, s, MIX_WIDTH)
    return y * pool_scale

def segsum(a):
    t = a.shape[-1]
    cs = jnp.cumsum(a, axis=-1)
    diff = cs[..., :, None] - cs[..., None, :]
    mask = jnp.tril(jnp.ones((t, t), dtype=bool))
    return jnp.where(mask, diff, -jnp.inf)

def ssd_mixer(z, xbc, dt, conv_w, conv_b, dt_bias, a_log, d_skip, norm_g):
    b, s, _ = z.shape
    nc, lc, g, r, n, hp = s // SSD_CHUNK, SSD_CHUNK, SSD_GROUPS, SSD_HEADS // SSD_GROUPS, SSD_STATE, SSD_HEADDIM
    xbc = jax.nn.silu(causal_dwconv(xbc, conv_w, conv_b)).astype(jnp.float32)
    xs = xbc[..., :MIX_WIDTH]
    bm = xbc[..., MIX_WIDTH:MIX_WIDTH + g * n].reshape(b, nc, lc, g, n)
    cm = xbc[..., MIX_WIDTH + g * n:].reshape(b, nc, lc, g, n)
    dt = jax.nn.softplus(dt.astype(jnp.float32) + dt_bias.astype(jnp.float32))
    a_head = -jnp.exp(a_log.astype(jnp.float32))
    x = xs.reshape(b, nc, lc, g, r, hp)
    xdt = x * dt.reshape(b, nc, lc, g, r)[..., None]
    a = (dt * a_head).reshape(b, nc, lc, g, r).transpose(0, 3, 4, 1, 2)
    a_cs = jnp.cumsum(a, axis=-1)
    lmat = jnp.exp(segsum(a))
    cb = jnp.einsum('bclgn,bcsgn->bgcls', cm, bm)
    y_diag = jnp.einsum('bgrcls,bcsgrp->bclgrp', cb[:, :, None] * lmat, xdt)
    decay_states = jnp.exp(a_cs[..., -1:] - a_cs)
    states = jnp.einsum('bclgn,bgrcl,bclgrp->bcgrpn', bm, decay_states, xdt)
    states = jnp.concatenate([jnp.zeros_like(states[:, :1]), states], axis=1)
    chunk_a = jnp.pad(a_cs[..., -1], ((0, 0), (0, 0), (0, 0), (1, 0)))
    decay_chunk = jnp.exp(segsum(chunk_a))
    states = jnp.einsum('bgrzc,bcgrpn->bzgrpn', decay_chunk, states)[:, :-1]
    y_off = jnp.einsum('bclgn,bcgrpn,bgrcl->bclgrp', cm, states, jnp.exp(a_cs))
    y = (y_diag + y_off).reshape(b, s, SSD_HEADS, hp) \
        + xs.reshape(b, s, SSD_HEADS, hp) * d_skip.astype(jnp.float32)[:, None]
    y = y.reshape(b, s, MIX_WIDTH) * jax.nn.silu(z.astype(jnp.float32))
    return rmsnorm(y, norm_g).astype(z.dtype)

def rglru_mixer(gate_in, x_in, conv_w, conv_b, w_a, b_a, w_i, b_i, lam):
    b, s, _ = x_in.shape
    gate = jax.nn.gelu(gate_in)
    xc = causal_dwconv(x_in, conv_w, conv_b)
    xb = xc.reshape(b, s, LRU_BLOCKS, LRU_BLOCK)
    r_t = jax.nn.sigmoid((jnp.einsum('bshi,hij->bshj', xb, w_a).reshape(b, s, MIX_WIDTH) + b_a).astype(jnp.float32))
    i_t = jax.nn.sigmoid((jnp.einsum('bshi,hij->bshj', xb, w_i).reshape(b, s, MIX_WIDTH) + b_i).astype(jnp.float32))
    log_a = -LRU_C * r_t * jax.nn.softplus(-lam.astype(jnp.float32))
    a_t = jnp.exp(log_a)
    mult = jnp.sqrt(-jnp.expm1(2.0 * log_a))
    u = xc.astype(jnp.float32) * i_t * mult

    def combine(lhs, rhs):
        a1, b1 = lhs
        a2, b2 = rhs
        return a1 * a2, a2 * b1 + b2

    _, h = lax.associative_scan(combine, (a_t, u), axis=1)
    return h.astype(x_in.dtype) * gate

def first_inputs(seed: int = 0) -> dict:
    key = jax.random.key(seed)
    ks = iter(jax.random.split(key, 48))
    f32 = jnp.float32

    def nrm(shape, fan_in):
        return jax.random.normal(next(ks), shape, f32) * (fan_in ** -0.5)

    def gain(shape):
        return 1.0 + 0.05 * jax.random.normal(next(ks), shape, f32)

    def small(shape):
        return 0.01 * jax.random.normal(next(ks), shape, f32)

    L = DEPTH
    x = jax.random.normal(next(ks), (BATCH, SEQ, D_MODEL), f32)
    p = jax.random.normal(next(ks), (DEPTH, BATCH, SEQ, PLE_DIM), f32)
    offs = jax.random.randint(next(ks), (BATCH, 1), 0, 1024, dtype=jnp.int32)
    positions = (offs + jnp.arange(SEQ, dtype=jnp.int32)[None, :]).astype(jnp.int32)
    dt0 = jnp.exp(jax.random.uniform(next(ks), (L, SSD_HEADS), f32, np.log(1e-3), np.log(1e-1)))
    dt_bias = dt0 + jnp.log(-jnp.expm1(-dt0))
    a_log = jnp.log(jax.random.uniform(next(ks), (L, SSD_HEADS), f32, 1.0, 16.0))
    a_pow = jax.random.uniform(next(ks), (L, MIX_WIDTH), f32, 0.9, 0.999) ** (1.0 / LRU_C)
    lam = jnp.log(a_pow) - jnp.log1p(-a_pow)
    return {
        "x": x,
        "p": p,
        "positions": positions,
        "g_mix": gain((L, D_MODEL)),
        "w_in": nrm((L, D_MODEL, IN_COLS), D_MODEL),
        "q_norm": gain((L, Q_LORA)),
        "w_uq": nrm((L, Q_LORA, MLA_HEADS * (QK_NOPE + QK_ROPE)), Q_LORA),
        "kv_norm": gain((L, KV_LORA)),
        "w_ukv": nrm((L, KV_LORA, MLA_HEADS * (QK_NOPE + V_HEAD)), KV_LORA),
        "w_pool": nrm((L, 4, POOL_GROUP, POOL_GROUP), POOL_GROUP),
        "pool_scale": 1.0 + 0.1 * jax.random.normal(next(ks), (L, MIX_WIDTH), f32),
        "ssd_conv_w": nrm((L, CONV_WIDTH, SSD_XBC), CONV_WIDTH),
        "ssd_conv_b": small((L, SSD_XBC)),
        "ssd_dt_bias": dt_bias,
        "ssd_a_log": a_log,
        "ssd_d": gain((L, SSD_HEADS)),
        "ssd_norm": gain((L, MIX_WIDTH)),
        "lru_conv_w": nrm((L, CONV_WIDTH, MIX_WIDTH), CONV_WIDTH),
        "lru_conv_b": small((L, MIX_WIDTH)),
        "lru_w_a": nrm((L, LRU_BLOCKS, LRU_BLOCK, LRU_BLOCK), LRU_BLOCK),
        "lru_b_a": small((L, MIX_WIDTH)),
        "lru_w_i": nrm((L, LRU_BLOCKS, LRU_BLOCK, LRU_BLOCK), LRU_BLOCK),
        "lru_b_i": small((L, MIX_WIDTH)),
        "lru_lambda": lam,
        "w_branch": nrm((L, N_BRANCH, MIX_WIDTH, D_MODEL), MIX_WIDTH),
        "w_out": nrm((L, D_MODEL, D_MODEL), D_MODEL),
        "g_mlp": gain((L, D_MODEL)),
        "w_ff1": nrm((L, D_MODEL, D_FF), D_MODEL),
        "w_ff2": nrm((L, D_FF, D_MODEL), D_FF),
        "g_ple": gain((L, D_MODEL)),
        "w_ple_gate": nrm((L, D_MODEL, D_MODEL), D_MODEL),
        "w_ple": nrm((L, PLE_DIM, D_MODEL), PLE_DIM),
        "g_final": gain((D_MODEL,)),
    }

def first_block(x, p, positions, g_mix, w_in, q_norm, w_uq, kv_norm, w_ukv, w_pool, pool_scale,
              ssd_conv_w, ssd_conv_b, ssd_dt_bias, ssd_a_log, ssd_d, ssd_norm,
              lru_conv_w, lru_conv_b, lru_w_a, lru_b_a, lru_w_i, lru_b_i, lru_lambda,
              w_branch, w_out, g_mlp, w_ff1, w_ff2, g_ple, w_ple_gate, w_ple, g_final):
    b, s, _ = x.shape
    cos, sin = rope_tables(positions)
    pts = _split_points()
    for l in range(DEPTH):
        h = rmsnorm(x, g_mix[l])
        u = h @ w_in[l]
        c_q, c_kv, k_r, u_pool, z, xbc, dt, lru_g, lru_x, gates = jnp.split(u, pts, axis=-1)
        y_a = mla_mixer(c_q, c_kv, k_r, cos, sin, q_norm[l], w_uq[l], kv_norm[l], w_ukv[l])
        y_b = pool_mixer(u_pool, w_pool[l], pool_scale[l])
        y_c = ssd_mixer(z, xbc, dt, ssd_conv_w[l], ssd_conv_b[l], ssd_dt_bias[l], ssd_a_log[l],
                        ssd_d[l], ssd_norm[l])
        y_d = rglru_mixer(lru_g, lru_x, lru_conv_w[l], lru_conv_b[l], lru_w_a[l], lru_b_a[l],
                          lru_w_i[l], lru_b_i[l], lru_lambda[l])
        gates = jax.nn.sigmoid(gates.reshape(b, s, N_BRANCH, D_MODEL))
        merged = (gates[:, :, 0] * (y_a @ w_branch[l, 0])
                  + gates[:, :, 1] * (y_b @ w_branch[l, 1])
                  + gates[:, :, 2] * (y_c @ w_branch[l, 2])
                  + gates[:, :, 3] * (y_d @ w_branch[l, 3]))
        x = x + merged @ w_out[l]
        h2 = rmsnorm(x, g_mlp[l])
        x = x + jnp.square(jax.nn.relu(h2 @ w_ff1[l])) @ w_ff2[l]
        ple_gate = jax.nn.sigmoid(rmsnorm(x, g_ple[l]) @ w_ple_gate[l])
        x = x + (p[l] @ w_ple[l]) * ple_gate
    return rmsnorm(x, g_final)


GRID_W = 64
CTX_LEN = 256
CHUNK = 64
GLA_HEADS = 4
GLA_DK = 64
GLA_DV = 128
GLA_GATE_RANK = 16
GLA_GATE_TAU = 16.0
RET_HEADS = 4
RET_DK = 128
RET_DV = 128
RET_GAMMA_EXP0 = 5
ROPE_BASE = 10000.0
N_EXPERTS = 16
EC_CAPACITY_FACTOR = 2
EXPERT_FF = 1408
N_ADA = 6

GLA_QK = GLA_HEADS * GLA_DK
GLA_V = GLA_HEADS * GLA_DV
RET_QK = RET_HEADS * RET_DK
RET_V = RET_HEADS * RET_DV
MIX_WIDTH_2 = GLA_V + RET_V
IN_WIDTHS = (GLA_QK, GLA_QK, GLA_V, 2 * GLA_GATE_RANK, GLA_V, RET_QK, RET_QK, RET_V, RET_V)
IN_WIDTH = sum(IN_WIDTHS)
IN_SPLIT_POINTS = tuple(int(p) for p in np.cumsum(IN_WIDTHS)[:-1])


F32 = jnp.float32

def _rmsnorm(x, w):
    xf = x.astype(F32)
    y = xf * lax.rsqrt(jnp.mean(xf * xf, axis=-1, keepdims=True) + EPS)
    return (y * w).astype(x.dtype)

def _head_rmsnorm(o, w):
    B, T, H, d = o.shape
    of = o.astype(F32)
    y = of * lax.rsqrt(jnp.mean(of * of, axis=-1, keepdims=True) + EPS)
    return y.reshape(B, T, H * d) * w

def _head_layernorm(o, w):
    B, T, H, d = o.shape
    of = o.astype(F32)
    mu = jnp.mean(of, axis=-1, keepdims=True)
    var = jnp.mean(jnp.square(of - mu), axis=-1, keepdims=True)
    return ((of - mu) * lax.rsqrt(var + EPS)).reshape(B, T, H * d) * w

def _flip(a):
    return jnp.flip(a, axis=1)

def _to_chunks(a):
    B, T, H, d = a.shape
    return a.reshape(B, T // CHUNK, CHUNK, H, d).transpose(1, 0, 3, 2, 4)

def _from_chunks(a):
    N, B, H, C, d = a.shape
    return a.transpose(1, 0, 3, 2, 4).reshape(B, N * C, H, d)

def _grid_rope_angles(n_tok):
    rows = n_tok // GRID_W
    row = jnp.broadcast_to(jnp.arange(rows)[:, None], (rows, GRID_W)).reshape(-1).astype(F32)
    col = jnp.broadcast_to(jnp.arange(GRID_W)[None, :], (rows, GRID_W)).reshape(-1).astype(F32)
    n_freq = RET_DK // 4
    inv = ROPE_BASE ** (-jnp.arange(n_freq, dtype=F32) / n_freq)
    return jnp.concatenate([row[:, None] * inv, col[:, None] * inv], axis=-1)

def _apply_rope(a, ang):
    half = a.shape[-1] // 2
    cos = jnp.cos(ang)[None, :, None, :]
    sin = jnp.sin(ang)[None, :, None, :]
    a1, a2 = a[..., :half], a[..., half:]
    return jnp.concatenate([a1 * cos - a2 * sin, a1 * sin + a2 * cos], axis=-1)

def _gla_chunked(q, k, v, log_a, s0):
    mask = jnp.tril(jnp.ones((CHUNK, CHUNK), dtype=bool))[:, :, None]

    def step(s, xs):
        qc, kc, vc, gc = xs
        b = jnp.cumsum(gc, axis=2)
        b_end = b[:, :, -1:, :]
        decay = jnp.exp(jnp.where(mask, b[:, :, :, None, :] - b[:, :, None, :, :], -jnp.inf))
        scores = jnp.einsum('bhik,bhjk,bhijk->bhij', qc, kc, decay)
        o = jnp.einsum('bhij,bhjv->bhiv', scores, vc) + jnp.einsum('bhik,bhkv->bhiv', qc * jnp.exp(b), s)
        s = jnp.exp(b_end)[:, :, 0, :, None] * s + jnp.einsum('bhjk,bhjv->bhkv', kc * jnp.exp(b_end - b), vc)
        return s, o

    s_end, o = lax.scan(step, s0, (_to_chunks(q), _to_chunks(k), _to_chunks(v), _to_chunks(log_a)))
    return _from_chunks(o), s_end

def _retention_chunked(q, k, v, log_gamma, s0):
    pos = jnp.arange(CHUNK, dtype=F32)
    lg = log_gamma.astype(F32)[:, None, None]
    rel = pos[:, None] - pos[None, :]
    d_intra = jnp.where(rel >= 0, jnp.exp(lg * jnp.maximum(rel, 0.0)), 0.0)
    q_decay = jnp.exp(lg * (pos + 1.0)[:, None])
    k_decay = jnp.exp(lg * (CHUNK - 1.0 - pos)[:, None])
    c_decay = jnp.exp(lg * CHUNK)

    def step(s, xs):
        qc, kc, vc = xs
        scores = jnp.einsum('bhik,bhjk->bhij', qc, kc) * d_intra
        o = jnp.einsum('bhij,bhjv->bhiv', scores, vc) + jnp.einsum('bhik,bhkv->bhiv', qc * q_decay, s)
        s = c_decay * s + jnp.einsum('bhjk,bhjv->bhkv', kc * k_decay, vc)
        return s, o

    s_end, o = lax.scan(step, s0, (_to_chunks(q), _to_chunks(k), _to_chunks(v)))
    return _from_chunks(o), s_end

def _gla_final_state(k, v, log_a):
    b = jnp.cumsum(log_a, axis=1)
    w = jnp.exp(b[:, -1:] - b)
    return jnp.einsum('bthk,bthv->bhkv', k * w, v)

def _ret_final_state(k, v, log_gamma):
    T = k.shape[1]
    w = jnp.exp(log_gamma.astype(F32)[None, :] * jnp.arange(T - 1, -1, -1, dtype=F32)[:, None])
    return jnp.einsum('bthk,bthv->bhkv', k * w[None, :, :, None], v)

def _project(h, w_in, gla_gate_w, gla_gate_b, rope):
    B, T, _ = h.shape
    gq, gk, gv, gz, gg, rq, rk, rv, rg = jnp.split(h @ w_in, IN_SPLIT_POINTS, axis=-1)
    gq = gq.reshape(B, T, GLA_HEADS, GLA_DK) * (GLA_DK ** -0.5)
    gk = gk.reshape(B, T, GLA_HEADS, GLA_DK)
    gv = gv.reshape(B, T, GLA_HEADS, GLA_DV)
    pre = jnp.einsum('btdr,drk->btdk', gz.reshape(B, T, 2, GLA_GATE_RANK), gla_gate_w) + gla_gate_b
    log_a = (jax.nn.log_sigmoid(pre.astype(F32)) / GLA_GATE_TAU).reshape(B, T, 2, GLA_HEADS, GLA_DK)
    rq = rq.reshape(B, T, RET_HEADS, RET_DK)
    rk = rk.reshape(B, T, RET_HEADS, RET_DK) * (RET_DK ** -0.5)
    if rope is not None:
        rq = _apply_rope(rq, rope)
        rk = _apply_rope(rk, rope)
    rv = rv.reshape(B, T, RET_HEADS, RET_DV)
    return gq, gk, gv, log_a, gg, rq, rk, rv, rg

def _zero_states(B):
    g = jnp.zeros((B, GLA_HEADS, GLA_DK, GLA_DV), F32)
    r = jnp.zeros((B, RET_HEADS, RET_DK, RET_DV), F32)
    return (g, g, r, r)

def _token_mixer(h, w_in, gla_gate_w, gla_gate_b, ret_decay_logit, gla_norm_w, ret_norm_w, w_out, init_states, rope):
    gq, gk, gv, log_a, gg, rq, rk, rv, rg = _project(h, w_in, gla_gate_w, gla_gate_b, rope)
    log_gamma = jax.nn.log_sigmoid(ret_decay_logit.astype(F32))
    s_gf, s_gb, s_rf, s_rb = init_states
    o_gf, s_gf = _gla_chunked(gq, gk, gv, log_a[:, :, 0], s_gf)
    o_gb, s_gb = _gla_chunked(_flip(gq), _flip(gk), _flip(gv), _flip(log_a[:, :, 1]), s_gb)
    o_rf, s_rf = _retention_chunked(rq, rk, rv, log_gamma[0], s_rf)
    o_rb, s_rb = _retention_chunked(_flip(rq), _flip(rk), _flip(rv), log_gamma[1], s_rb)
    o_g = _head_rmsnorm(o_gf + _flip(o_gb), gla_norm_w) * jax.nn.silu(gg)
    o_r = _head_layernorm(o_rf + _flip(o_rb), ret_norm_w) * jax.nn.silu(rg)
    out = jnp.concatenate([o_g, o_r], axis=-1) @ w_out
    return out, (s_gf, s_gb, s_rf, s_rb)

def _context_states(hc, w_in, gla_gate_w, gla_gate_b, ret_decay_logit):
    _, gk, gv, log_a, _, _, rk, rv, _ = _project(hc, w_in, gla_gate_w, gla_gate_b, None)
    log_gamma = jax.nn.log_sigmoid(ret_decay_logit.astype(F32))
    s_gf = _gla_final_state(gk, gv, log_a[:, :, 0])
    s_gb = _gla_final_state(_flip(gk), _flip(gv), _flip(log_a[:, :, 1]))
    s_rf = _ret_final_state(rk, rv, log_gamma[0])
    s_rb = _ret_final_state(_flip(rk), _flip(rv), log_gamma[1])
    return (s_gf, s_gb, s_rf, s_rb)

def _expert_choice_ffn(h, w_router, w_gate, w_up, w_down):
    B, T, _ = h.shape
    cap = EC_CAPACITY_FACTOR * T // N_EXPERTS
    aff = jax.nn.softmax((h @ w_router).astype(F32), axis=-1)
    gate, idx = lax.top_k(jnp.swapaxes(aff, 1, 2), cap)
    bidx = jnp.arange(B)[:, None, None]
    xe = h[bidx, idx]
    a = jnp.einsum('becd,edf->becf', xe, w_gate)
    u = jnp.einsum('becd,edf->becf', xe, w_up)
    ye = jnp.einsum('becf,efd->becd', jax.nn.silu(a) * u, w_down) * gate[..., None]
    return jnp.zeros_like(h).at[bidx, idx].add(ye.astype(h.dtype))

def second_inputs(seed: int = 0) -> dict:
    key = jax.random.key(seed)
    ks = jax.random.split(key, 24)
    n = lambda k, shape, s: jax.random.normal(k, shape, F32) * s
    logit0 = jnp.asarray(np.log(2.0 ** (RET_GAMMA_EXP0 + np.arange(RET_HEADS)) - 1.0), F32)
    return {
        'x': n(ks[0], (BATCH, SEQ, D_MODEL), 1.0),
        'c': n(ks[1], (BATCH, D_MODEL), 1.0),
        'ctx': n(ks[2], (BATCH, CTX_LEN, D_MODEL), 1.0),
        'c_ctx': n(ks[3], (D_MODEL,), 1.0),
        'w_ada': n(ks[4], (DEPTH, D_MODEL, N_ADA * D_MODEL), 0.02),
        'b_ada': n(ks[5], (DEPTH, N_ADA * D_MODEL), 0.02),
        'norm1_w': 1.0 + n(ks[6], (DEPTH, D_MODEL), 0.02),
        'w_in': n(ks[7], (DEPTH, D_MODEL, IN_WIDTH), D_MODEL ** -0.5),
        'gla_gate_w': n(ks[8], (DEPTH, 2, GLA_GATE_RANK, GLA_QK), GLA_GATE_RANK ** -0.5),
        'gla_gate_b': n(ks[9], (DEPTH, 2, GLA_QK), 0.1),
        'ret_decay_logit': logit0[None, None, :] + n(ks[10], (DEPTH, 2, RET_HEADS), 0.05),
        'gla_norm_w': 1.0 + n(ks[11], (DEPTH, GLA_V), 0.02),
        'ret_norm_w': 1.0 + n(ks[12], (DEPTH, RET_V), 0.02),
        'w_out': n(ks[13], (DEPTH, MIX_WIDTH_2, D_MODEL), MIX_WIDTH_2 ** -0.5),
        'norm2_w': 1.0 + n(ks[14], (DEPTH, D_MODEL), 0.02),
        'w_router': n(ks[15], (DEPTH, D_MODEL, N_EXPERTS), D_MODEL ** -0.5),
        'w_exp_gate': n(ks[16], (DEPTH, N_EXPERTS, D_MODEL, EXPERT_FF), D_MODEL ** -0.5),
        'w_exp_up': n(ks[17], (DEPTH, N_EXPERTS, D_MODEL, EXPERT_FF), D_MODEL ** -0.5),
        'w_exp_down': n(ks[18], (DEPTH, N_EXPERTS, EXPERT_FF, D_MODEL), EXPERT_FF ** -0.5),
        'final_norm_w': 1.0 + n(ks[19], (D_MODEL,), 0.02),
    }

def second_block(x, c, ctx, c_ctx, w_ada, b_ada, norm1_w, w_in, gla_gate_w, gla_gate_b, ret_decay_logit,
              gla_norm_w, ret_norm_w, w_out, norm2_w, w_router, w_exp_gate, w_exp_up, w_exp_down, final_norm_w):
    B, n_lat, D = x.shape
    rope = _grid_rope_angles(n_lat)
    for i in range(DEPTH):
        last = i == DEPTH - 1
        mod = (jax.nn.silu(c) @ w_ada[i] + b_ada[i]).reshape(B, N_ADA, D)[:, :, None, :]
        mod_c = (jax.nn.silu(c_ctx) @ w_ada[i] + b_ada[i]).reshape(N_ADA, D)
        hc = _rmsnorm(ctx, norm1_w[i]) * (1.0 + mod_c[1]) + mod_c[0]
        if last:
            ctx_states = _context_states(hc, w_in[i], gla_gate_w[i], gla_gate_b[i], ret_decay_logit[i])
        else:
            ctx_out, ctx_states = _token_mixer(hc, w_in[i], gla_gate_w[i], gla_gate_b[i], ret_decay_logit[i],
                                               gla_norm_w[i], ret_norm_w[i], w_out[i], _zero_states(B), None)
        h = _rmsnorm(x, norm1_w[i]) * (1.0 + mod[:, 1]) + mod[:, 0]
        x_out, _ = _token_mixer(h, w_in[i], gla_gate_w[i], gla_gate_b[i], ret_decay_logit[i],
                                gla_norm_w[i], ret_norm_w[i], w_out[i], ctx_states, rope)
        x = x + mod[:, 2] * x_out
        h2 = _rmsnorm(x, norm2_w[i]) * (1.0 + mod[:, 4]) + mod[:, 3]
        x = x + mod[:, 5] * _expert_choice_ffn(h2, w_router[i], w_exp_gate[i], w_exp_up[i], w_exp_down[i])
        if not last:
            ctx = ctx + mod_c[2] * ctx_out
            hc2 = _rmsnorm(ctx, norm2_w[i]) * (1.0 + mod_c[4]) + mod_c[3]
            ctx = ctx + mod_c[5] * _expert_choice_ffn(hc2, w_router[i], w_exp_gate[i], w_exp_up[i], w_exp_down[i])
    return _rmsnorm(x, final_norm_w)


def setup_inputs(seed=0):
    out = dict(first_inputs(seed))
    for name, value in second_inputs(seed + 1).items():
        if name != "x":
            out[name + "_2"] = value
    return out


def reference(
    x, p, positions, g_mix, w_in, q_norm, w_uq, kv_norm, w_ukv, w_pool, pool_scale, ssd_conv_w,
    ssd_conv_b, ssd_dt_bias, ssd_a_log, ssd_d, ssd_norm, lru_conv_w, lru_conv_b, lru_w_a,
    lru_b_a, lru_w_i, lru_b_i, lru_lambda, w_branch, w_out, g_mlp, w_ff1, w_ff2, g_ple,
    w_ple_gate, w_ple, g_final, c_2, ctx_2, c_ctx_2, w_ada_2, b_ada_2, norm1_w_2, w_in_2,
    gla_gate_w_2, gla_gate_b_2, ret_decay_logit_2, gla_norm_w_2, ret_norm_w_2, w_out_2,
    norm2_w_2, w_router_2, w_exp_gate_2, w_exp_up_2, w_exp_down_2, final_norm_w_2,
):
    x = first_block(
        x, p, positions, g_mix, w_in, q_norm, w_uq, kv_norm, w_ukv, w_pool, pool_scale,
        ssd_conv_w, ssd_conv_b, ssd_dt_bias, ssd_a_log, ssd_d, ssd_norm, lru_conv_w, lru_conv_b,
        lru_w_a, lru_b_a, lru_w_i, lru_b_i, lru_lambda, w_branch, w_out, g_mlp, w_ff1, w_ff2,
        g_ple, w_ple_gate, w_ple, g_final,
    )
    return second_block(
        x, c_2, ctx_2, c_ctx_2, w_ada_2, b_ada_2, norm1_w_2, w_in_2, gla_gate_w_2, gla_gate_b_2,
        ret_decay_logit_2, gla_norm_w_2, ret_norm_w_2, w_out_2, norm2_w_2, w_router_2,
        w_exp_gate_2, w_exp_up_2, w_exp_down_2, final_norm_w_2,
    )


_drawn_inputs = setup_inputs


def setup_inputs(seed=0):
    import zlib

    import numpy as np

    out = dict(_drawn_inputs(seed))
    spreads = {}
    factors = {'q_norm': 8.0,
     'kv_norm': 8.0,
     'ssd_conv_b': 7.222,
     'lru_conv_b': 3.253,
     'lru_b_a': 64.0,
     'lru_b_i': 64.0,
     'g_ple': 7.845,
     'norm1_w_2': 4.745,
     'gla_gate_b_2': 5.283,
     'gla_norm_w_2': 8.0,
     'ret_norm_w_2': 8.0,
     'norm2_w_2': 6.914}
    for name, (base, spread) in spreads.items():
        noise = np.random.default_rng([zlib.crc32(name.encode()), seed]).standard_normal(out[name].shape)
        drawn = base * np.exp(spread * noise) if base else spread * noise
        out[name] = jnp.asarray(drawn.astype(out[name].dtype))
    for name, factor in factors.items():
        out[name] = (out[name] * factor).astype(out[name].dtype)
    return out
```

```python
from contextlib import ExitStack

import numpy as np
import concourse.bass as bass
from concourse import mybir

F32 = mybir.dt.float32
F32R = mybir.dt.float32r
I32 = mybir.dt.int32
U32 = mybir.dt.uint32
ALU = mybir.AluOpType
AF = mybir.ActivationFunctionType
AX = mybir.AxisListType
EPS = 1e-6
T = 1024
H2 = 512

PAR = [("g_mix", 8), ("q_norm", 3), ("kv_norm", 2), ("pool_scale", 4), ("conv_w", 24), ("conv_b", 6),
       ("ssd_norm", 4), ("ssd_d", 4), ("lconv_w", 16), ("lconv_b", 4), ("b_a", 4), ("b_i", 4), ("lam", 4),
       ("g_mlp", 8), ("g_ple", 8), ("g_final", 8), ("norm1", 8), ("norm2", 8), ("b_ada", 48), ("gate_b", 4),
       ("gla_norm", 4), ("ret_norm", 4), ("cc", 16), ("dt_bias", 1), ("a_log", 1), ("ret_logit", 8)]
CON = [("ident", 128), ("ones", 128), ("mle", 128), ("mge", 128), ("mneg", 128), ("inv", 1), ("sgn", 1),
       ("icnt", 64), ("relf", 128), ("relb", 128), ("posf", 128), ("posb", 128), ("colf", 1), ("colb", 1)]


def offsets(table):
    out, at = {}, 0
    for name, n in table:
        out[name] = (at, n)
        at += n
    return out, at


PO, NPAR = offsets(PAR)
CO, NCON = offsets(CON)


class Tok:
    def __init__(self, sem, val):
        self.sem, self.val = sem, val


class Eng:

    def __init__(self, name, sem):
        self.name, self.sem, self.n, self.list, self.seen = name, sem, 0, [], {}

    def wait(self, toks):
        for t in toks:
            if t is None:
                continue
            if self.seen.get(t.sem.name, 0) < t.val:
                self.seen[t.sem.name] = t.val
                self.list.append(("wait", t.sem, t.val))

    def put(self, method, args, kw, w=(), inc=True):
        self.wait(w)
        if inc:
            self.n += 1
        self.list.append(("op", method, args, kw, (self.sem, 1) if inc else None))
        return self.t

    @property
    def t(self):
        return Tok(self.sem, self.n) if self.n else None

    def play(self, eng):
        table = {"tensor_tensor": eng.tensor_tensor if self.name in ("dve", "pool") else None,
                 "wait_ge": eng.wait_ge, "dma_start": eng.dma_start}
        if self.name == "dve":
            table.update(tensor_scalar=eng.tensor_scalar, scalar_tensor_tensor=eng.scalar_tensor_tensor,
                         tensor_tensor_scan=eng.tensor_tensor_scan, tensor_copy=eng.tensor_copy,
                         memset=eng.memset, reciprocal=eng.reciprocal, tensor_reduce=eng.tensor_reduce,
                         max=eng.max, max_index=eng.max_index, match_replace=eng.match_replace)
        if self.name == "pool":
            table.update(tensor_scalar=eng.tensor_scalar, tensor_copy=eng.tensor_copy, memset=eng.memset,
                         indirect_dma_start=eng.indirect_dma_start)
        if self.name == "act":
            table.update(activation=eng.activation)
        if self.name == "pe":
            table.update(matmul=eng.matmul, transpose=eng.transpose)
        for item in self.list:
            if item[0] == "wait":
                eng.wait_ge(item[1], item[2])
            else:
                _, method, args, kw, inc = item
                ins = table[method](*args, **kw)
                if inc:
                    ins.then_inc(*inc)


class Slot:

    def __init__(self, sem):
        self.sem, self.val = sem, 0

    def next(self):
        self.val += 16
        return Tok(self.sem, self.val)

    @property
    def t(self):
        return Tok(self.sem, self.val) if self.val else None


class Prog:
    def __init__(self, nc, ctx):
        self.nc, self.ctx = nc, ctx
        self.pe, self.act, self.dve, self.pool, self.sp = (
            Eng(n, ctx.enter_context(nc.semaphore("c_" + n))) for n in ("pe", "act", "dve", "pool", "sp"))
        self.slots = []

    def slot(self, name):
        s = Slot(self.ctx.enter_context(self.nc.semaphore("d_" + name)))
        self.slots.append(s)
        return s

    def A(self, out, in_, f=AF.Copy, w=(), **kw):
        return self.act.put("activation", (out, in_, f), kw, [self.act.t, *w])

    def V(self, method, *args, w=(), **kw):
        return self.dve.put(method, args, kw, [self.dve.t, *w])

    def G(self, method, *args, w=(), **kw):
        return self.pool.put(method, args, kw, [self.pool.t, *w])

    def mm(self, out, l, r, start, stop, w=(), inc=False):
        return self.pe.put("matmul", (out, l, r), dict(start=start, stop=stop), w, inc)

    def tr(self, out, in_, ident, w=(), inc=False):
        return self.pe.put("transpose", (out, in_, ident), {}, w, inc)

    def dma(self, eng, out, in_, slot, w=()):
        eng.wait(w)
        t = slot.next()
        eng.list.append(("op", "dma_start", (out, in_), {}, (slot.sem, 16)))
        return t

    def idma(self, slot, w=(), **kw):
        self.pool.wait(w)
        t = slot.next()
        self.pool.list.append(("op", "indirect_dma_start", (), kw, (slot.sem, 16)))
        return t

    def barrier(self):
        toks = [e.t for e in (self.pe, self.act, self.dve, self.pool)] + [s.t for s in self.slots]
        for e in (self.pe, self.act, self.dve, self.pool, self.sp):
            e.wait(toks)


def program(nc, I, out, stop=99):
    ctx = ExitStack()
    P = Prog(nc, ctx)
    pe, act, dve, pool, sp = P.pe, P.act, P.dve, P.pool, P.sp
    A, V, G, mm, tr = P.A, P.V, P.G, P.mm, P.tr

    def sb(name, n, dt=F32, c=ctx, p=128):
        return c.enter_context(nc.sbuf_tensor(name, [p, n], dt))[:, :]

    def scratch(name, shape):
        return nc.dram_tensor(name, shape, F32, kind="Internal").ap()

    D_u = scratch("D_u", [22, 128, T])
    D_g = scratch("D_g", [32, 128, T])
    D_y = scratch("D_y", [16, 128, T])
    D_dt = scratch("D_dt", [8, T])
    D_xb = scratch("D_xb", [8, 128, T])
    D_v = scratch("D_v", [29, 128, 1280])
    D_o = scratch("D_o", [8, 128, T])
    D_h = scratch("D_h", [T, 1024])
    D_acc = scratch("D_acc", [T, 1024])

    par = sb("par", NPAR)
    con = sb("con", NCON)
    bank = [ctx.enter_context(nc.psum_tensor(f"bank{i}", [128, 512], F32))[:, :] for i in range(8)]

    def pr(name, i=0, n=1):
        return par[:, PO[name][0] + i:PO[name][0] + i + n]

    def cn(name, a=0, b=None):
        o, n = CO[name]
        return con[:, o + a:o + (n if b is None else b)]

    ident, ones = cn("ident"), cn("ones")

    c1 = ExitStack()
    WH, WL = sb("WH", 2048, F32R), sb("WL", 2048, F32R)
    WR = sb("WR", 3 * 1024)
    stg = sb("stg", 2048)
    XH, XL = sb("XH", 8 * T, F32R, c1), sb("XL", 8 * T, F32R, c1)
    s_par = P.slot("par")
    s_wr = [P.slot(f"wr{i}") for i in range(3)]
    s_ld = [P.slot(f"ld{i}") for i in range(4)]
    s_st = [P.slot(f"st{i}") for i in range(2)]
    s_x = P.slot("x")
    s_m = [P.slot(f"m{i}") for i in range(6)]

    P.dma(sp, par, I["par"], s_par)
    t_par = P.dma(sp, con, I["con"], s_par)

    W = dict(n=0, loaded=[], raw_free=[None] * 3, spl_free=[None] * 2, halves=[None] * 2)

    def w_load(src, K):
        n = W["n"]
        W["n"] += 1
        i = n % 3
        t = P.dma(sp, WR[:, i * 1024:i * 1024 + K * 128], src, s_wr[i], [*(W["raw_free"][i] or [])])
        W["loaded"].append((n, K, t))

    def w_split(eng="pool"):
        n, K, t = W["loaded"].pop(0)
        i, j = n % 3, n % 2
        raw = WR[:, i * 1024:i * 1024 + K * 128]
        hi, lo = WH[:, j * 1024:j * 1024 + K * 128], WL[:, j * 1024:j * 1024 + K * 128]
        a = A(hi, raw, w=[t, W["spl_free"][j]])
        put = G if eng == "pool" else V
        b = put("tensor_tensor", lo, raw, hi.bitcast(F32), ALU.subtract, w=[t, a, W["spl_free"][j]])
        W["raw_free"][i] = [a, b]
        return j, [a, b]

    def stream(tiles, eng="pool"):
        tiles = list(tiles)
        for s, K in tiles[:2]:
            w_load(s, K)
        nxt = w_split(eng)
        for n, (s, K) in enumerate(tiles):
            if n + 2 < len(tiles):
                w_load(*tiles[n + 2])
            cur = nxt
            nxt = w_split(eng) if n + 1 < len(tiles) else None
            yield cur

    bank_free = [None] * 8

    def gemm(w, K, x, cols, b, xw=()):
        j, wt = w
        n = cols[1] - cols[0]
        first = True
        for k in range(K):
            whi = WH[:, j * 1024 + k * 128:j * 1024 + k * 128 + 128]
            wlo = WL[:, j * 1024 + k * 128:j * 1024 + k * 128 + 128]
            xhi, xlo = x(k, cols)
            for l, r in ((whi, xhi), (whi, xlo), (wlo, xhi)):
                last = k == K - 1 and l is wlo
                t = mm(bank[b][:, 0:n], l, r, first, last,
                       w=[*wt, *xw, bank_free[b]] if first else (), inc=last)
                first = False
        W["spl_free"][j] = t
        return t

    def xs(S):
        return lambda k, c: (XH[:, k * S + c[0]:k * S + c[1]], XL[:, k * S + c[0]:k * S + c[1]])

    def split_x(dst, src, w=()):
        hi, lo = XH[:, dst[0]:dst[1]], XL[:, dst[0]:dst[1]]
        a = A(hi, src, w=w)
        return V("tensor_tensor", lo, src, hi.bitcast(F32), ALU.subtract, w=[a, *w])

    dve_t = [None, None]

    c0 = ExitStack()
    xT = sb("xT", 8 * T, c=c0)
    sq = sb("sq", 2 * T, c=c0)
    acc = sb("acc", T, c=c0)
    r = sb("r", T, c=c0)
    for j in range(4):
        P.dma(sp, xT[:, 2 * j * T:(2 * j + 2) * T].rearrange("p (a t) -> p a t", a=2),
              I["xT"][2 * j:2 * j + 2].rearrange("a p t -> p a t"), s_ld[j])

    def xc(j):
        return xT[:, j * T:(j + 1) * T]

    for j in range(8):
        if j == 0:
            t = A(acc, xc(0), AF.Square, w=[s_ld[0].t])
        else:
            q = sq[:, (j % 2) * T:(j % 2) * T + T]
            a = A(q, xc(j), AF.Square, w=[s_ld[j // 2].t, dve_t[j % 2]])
            t = dve_t[j % 2] = V("tensor_tensor", acc, acc, q, ALU.add, w=[a])

    def rstd_tail(acc, r, D, n, banks, t):
        for h in range(0, n, 512):
            b = banks[h // 512]
            m = min(512, n - h)
            t2 = mm(bank[b][:, 0:m], ones, acc[:, h:h + m], True, True, w=[t, bank_free[b], t_par], inc=True)
            v = V("tensor_scalar", r[:, h:h + m], bank[b][:, 0:m], 1.0 / D, EPS, ALU.mult, ALU.add,
                  w=[t2, act.t])
            bank_free[b] = v
            V("reciprocal", r[:, h:h + m], r[:, h:h + m])
        return A(r[:, 0:n], r[:, 0:n], AF.Sqrt, w=[dve.t])

    t = rstd_tail(acc, r, 1024, T, (0, 1), t)
    hx = None
    for j in range(8):
        v = V("scalar_tensor_tensor", xc(j), xc(j), pr("g_mix", j), r, ALU.mult, ALU.mult, w=[t, t_par])
        hx = split_x((j * T, (j + 1) * T), xc(j), w=[v])
    P.barrier()
    c0.close()

    u_tok = {}
    cM = ExitStack()
    cqv = sb("cqv", 6 * T, c=cM)
    G_done = {}

    def stream_g():
        tiles = [(I["w_in"][m], 8) for m in range(60)]
        ev = 0
        for m, w in enumerate(stream(tiles)):
            if m < 6:
                dst = cqv[:, m * T:(m + 1) * T]
            else:
                i = m % 2
                dst = stg[:, i * T:(i + 1) * T]
            for h in range(2):
                g = gemm(w, 8, xs(T), (h * 512, h * 512 + 512), h, xw=[hx])
                d = dst[:, h * 512:h * 512 + 512]
                ww = [g] if m < 6 else [g, s_st[m % 2].t]
                if m < 28:
                    e = V("tensor_copy", d, bank[h][:, :], w=ww) if h else A(d, bank[h][:, :], w=ww)
                else:
                    e = A(d, bank[h][:, :], AF.Tanh, scale=0.5, w=ww)
                bank_free[h] = e
                if h == 0:
                    e0 = e
                yield
            if m < 6:
                u_tok[m] = [e0, e]
            elif m < 28:
                u_tok[m] = [P.dma(sp, D_u[m - 6], dst, s_st[m % 2], [e0, e])]
            else:
                u_tok[m] = [P.dma(sp, D_g[m - 28], dst, s_st[m % 2], [e0, e])]

    def need(*ms):
        return [t for m in ms for t in u_tok[m]]

    B_S = ((2, 3), (4, 5))
    B_T, B_O = 6, 7
    gbank = {}

    def bw(b, t):
        bank_free[b] = t
        return t

    def small_mm2(banks, parts, w=()):
        out = []
        for h in range(2):
            ps = parts(h)
            for n, (l, rr) in enumerate(ps):
                t = mm(bank[banks[h]][:, :] if l.shape[-1] == 128 else bank[banks[h]][0:l.shape[-1], :],
                       l, rr, n == 0, n == len(ps) - 1,
                       w=[*w, bank_free[banks[h]]] if n == 0 else (), inc=n == len(ps) - 1)
            out.append(t)
        return out

    def mixer_mla(c):
        uq = sb("uq", 4 * 384, c=c)
        ukv = sb("ukv", 4 * 256, c=c)
        PT = sb("PT", 8 * 512, c=c)
        uqr, vw = PT[:, 0:1536], PT[:, 1536:2560]
        cs = sb("cs", 2 * T, c=c)
        cosT, sinT = cs[:, 0:T], cs[:, T:2 * T]
        rp = sb("rp", 2 * T, c=c)
        yt = sb("yt", T, c=c)
        tA, tB = PT[:, 2560:3584], yt
        vN = sb("vN", 8 * 512, c=c)
        posr = vN[:, 0:T].bitcast(I32)
        P.dma(pool, uq, I["w_uq"][:, 0:1536], s_m[0])
        P.dma(pool, ukv, I["w_ukv"][:, 0:1024], s_m[1])
        P.dma(pool, uqr, I["w_uq"][:, 1536:3072], s_m[4])
        P.dma(pool, vw, I["w_ukv"][:, 1024:2048], s_m[5])
        P.dma(pool, posr[0:1, :], I["positions"], s_m[2])
        P.dma(pool, D_dt, cqv[32:40, 5 * T:6 * T], s_m[3], need(5))
        V("tensor_copy", tA[0:1, :], posr[0:1, :], w=[s_m[2].t])
        for h in range(2):
            t = mm(bank[2 + h][:, :], ones[0:1, :], tA[0:1, h * 512:h * 512 + 512], True, True,
                   w=[dve.t, bank_free[2 + h]], inc=True)
            v = V("tensor_scalar", tB[:, h * 512:h * 512 + 512], bank[2 + h][:, :], cn("inv"), None, ALU.mult, w=[t])
            bw(2 + h, v)
        V("tensor_scalar", cosT, tB, 1.0 / (2 * np.pi), 12582912.0, ALU.mult, ALU.add)
        V("tensor_scalar", cosT, cosT, -12582912.0, None, ALU.add)
        for cc in (6.28125, 0.0019350051879882812, 3.019916050561733e-07):
            V("scalar_tensor_tensor", tB, cosT, -cc, tB, ALU.mult, ALU.add)
        V("tensor_scalar", tB, tB, 3.1415925, -3.1415925, ALU.min, ALU.max)
        A(sinT, tB, AF.Sin, w=[dve.t])
        A(cosT, tB, AF.Sin, scale=0.5, w=[dve.t])
        V("tensor_scalar", sinT, sinT, cn("sgn"), None, ALU.mult, w=[act.t])
        V("tensor_tensor", cosT, cosT, cosT, ALU.mult)
        V("tensor_scalar", cosT, cosT, -2.0, 1.0, ALU.mult, ALU.add)
        yield
        cq = [cqv[:, j * T:(j + 1) * T] for j in range(3)]
        ckv = [cqv[:, j * T:(j + 1) * T] for j in range(3, 5)]
        krdt = cqv[:, 5 * T:6 * T]
        for seg, D, g in ((cq, 384, "q_norm"), (ckv, 256, "kv_norm")):
            for j, s in enumerate(seg):
                if j == 0:
                    t = A(tA, s, AF.Square, w=[dve.t, *need(0, 1, 2, 3, 4, 5)])
                else:
                    a = A(tB, s, AF.Square, w=[dve.t])
                    t = V("tensor_tensor", tA, tA, tB, ALU.add, w=[a])
            t = rstd_tail(tA, tB, D, T, (2, 3), t)
            for j, s in enumerate(seg):
                nt = V("scalar_tensor_tensor", s, s, pr(g, j), tB, ALU.mult, ALU.mult, w=[t])
            yield
        for g in range(2):
            for n, c0_ in enumerate((g, 2 + g)):
                ts = small_mm2(B_S[n], lambda h: [(uqr[:, c0_ * 384 + k * 128:c0_ * 384 + k * 128 + 128],
                                                   cq[k][:, h * 512:h * 512 + 512]) for k in range(3)],
                               w=[nt, s_m[4].t])
                for h in range(2):
                    hs = slice(h * 512, h * 512 + 512)
                    tab = (cosT, sinT)[n]
                    dst = (rp[:, g * T:(g + 1) * T], tA)[n]
                    bw(B_S[n][h], V("tensor_tensor", dst[:, hs], bank[B_S[n][h]][:, :], tab[:, hs], ALU.mult,
                                    w=[ts[h]]))
            V("tensor_tensor", rp[:, g * T:(g + 1) * T], rp[:, g * T:(g + 1) * T], tA, ALU.add)
            yield
        kr = krdt
        V("tensor_tensor", tA[64:96, :], krdt[0:32, :], cosT[0:32, :], ALU.mult)
        V("tensor_tensor", kr[64:96, :], krdt[64:96, :], sinT[64:96, :], ALU.mult)
        V("tensor_tensor", kr[64:96, :], kr[64:96, :], tA[64:96, :], ALU.add)
        for tc in range(8):
            b = B_S[tc % 2][0]
            for k in range(2):
                t = mm(bank[b][:, :], ckv[k][:, tc * 128:tc * 128 + 128], vw[:, k * 512:512 + k * 512],
                       k == 0, k == 1, w=[nt, s_m[5].t, bank_free[b]] if k == 0 else (), inc=k == 1)
            bw(b, A(vN[:, tc * 512:tc * 512 + 512], bank[b][:, :], w=[t]))
            if tc % 4 == 3:
                yield
        tv = act.t
        qk = sb("qk", 4 * T, c=c)
        Pm = cs
        st = sb("st", 32, c=c)
        SC = 96.0 ** -0.5
        ts_ = [None, None]
        pv_t = None
        for i in range(4):
            q_, k_ = [qk[:, a * T:(a + 1) * T] for a in range(2)], [qk[:, (2 + a) * T:(3 + a) * T] for a in range(2)]
            for n, (dst, chunk, K, wt, src) in enumerate(((q_, uq[:, i * 384:(i + 1) * 384], 3, s_m[0], cq),
                                                          (k_, ukv[:, i * 256:(i + 1) * 256], 2, s_m[1], ckv))):
                ts = small_mm2(B_S[n], lambda h: [(chunk[:, k * 128:k * 128 + 128],
                                                   src[k][:, h * 512:h * 512 + 512]) for k in range(K)],
                               w=[nt, wt.t])
                for h in range(2):
                    hs = slice(h * 512, h * 512 + 512)
                    b = B_S[n][h]
                    A(dst[0][0:64, hs], bank[b][0:64, :], w=[ts[h], pv_t])
                    bw(b, A(dst[1][0:64, hs], bank[b][64:128, :]))
            for a in range(2):
                hh = 2 * i + a
                A(q_[a][64:96, :], rp[32 * (hh % 4):32 * (hh % 4) + 32, (hh // 4) * T:(hh // 4 + 1) * T], w=[dve.t, pv_t])
                A(k_[a][64:96, :], kr[64:96, :], w=[pv_t])
            qk_t = act.t
            yield
            units = [(a, qb) for a in range(2) for qb in range(8)]
            state = {}

            def s1(u):
                a, qb = units[u]
                n = (qb + 1) * 128
                bs = B_S[u % 2]
                for h in range(0, n, 512):
                    b = bs[h // 512]
                    m = min(512, n - h)
                    t = mm(bank[b][:, 0:m], q_[a][0:96, qb * 128:qb * 128 + 128], k_[a][0:96, h:h + m], True, True,
                           w=[qk_t, bank_free[b]], inc=True)
                db = bs[(n - 1) // 512]
                o = (n - 128) % 512
                V("tensor_tensor", bank[db][:, o:o + 128], bank[db][:, o:o + 128], cn("mneg"), ALU.add, w=[t])
                c4 = (u % 4) * 8
                for h in range(0, n, 512):
                    b = bs[h // 512]
                    m = min(512, n - h)
                    V("tensor_reduce", st[:, c4 + h // 512:c4 + h // 512 + 1], bank[b][:, 0:m], AX.X, ALU.max)
                if n > 512:
                    V("tensor_tensor", st[:, c4:c4 + 1], st[:, c4:c4 + 1], st[:, c4 + 1:c4 + 2], ALU.max)
                v = V("tensor_scalar", st[:, c4 + 2:c4 + 3], st[:, c4:c4 + 1], -SC, None, ALU.mult)
                p = Pm[:, (u % 2) * T:(u % 2) * T + n]
                for h in range(0, n, 512):
                    b = bs[h // 512]
                    m = min(512, n - h)
                    e = A(p[:, h:h + m], bank[b][:, 0:m], AF.Exp, bias=st[:, c4 + 2:c4 + 3], scale=SC,
                          accum_out=st[:, c4 + 3 + h // 512:c4 + 4 + h // 512], w=[v, state.get(("tr", u - 2)), pool.t])
                    bw(b, e)
                state[u] = e

            def s2(u):
                a, qb = units[u]
                n = (qb + 1) * 128
                c4 = (u % 4) * 8
                p = Pm[:, (u % 2) * T:(u % 2) * T + n]
                w = [state[u]]
                if n > 512:
                    V("tensor_tensor", st[:, c4 + 3:c4 + 4], st[:, c4 + 3:c4 + 4], st[:, c4 + 4:c4 + 5], ALU.add, w=w)
                v = V("reciprocal", st[:, c4 + 5:c4 + 6], st[:, c4 + 3:c4 + 4], w=w)
                g = V("tensor_scalar", p, p, st[:, c4 + 5:c4 + 6], None, ALU.mult, w=[v, *w])
                qh, ql = qb // 4, qb % 4
                for k0 in range(0, qb + 1, 4):
                    kn = min(4, qb + 1 - k0)
                    for k in range(k0, k0 + kn):
                        t = tr(bank[B_T][:, (k - k0) * 128:(k - k0) * 128 + 128], p[:, k * 128:k * 128 + 128], ident,
                               w=[g, bank_free[B_T]] if k == k0 else (), inc=k == k0 + kn - 1)
                    bw(B_T, A(PT[:, :].rearrange("p (k q) -> p k q", k=8)[:, k0:k0 + kn, ql * 128:ql * 128 + 128],
                              bank[B_T][:, 0:kn * 128].rearrange("p (k q) -> p k q", q=128),
                              w=[t, state.get("pv")]))
                state[("tr", u)] = t
                if ql == 3:
                    hh = 2 * i + a
                    kc = qb + 1
                    for k in range(kc):
                        o = max(0, (k - 4 * qh) * 128)
                        t = mm(bank[B_O][a * 64:a * 64 + 64, o:512], vN[:, k * 512 + hh * 64:k * 512 + hh * 64 + 64],
                               PT[:, k * 512 + o:k * 512 + 512], k == 0, k == kc - 1,
                               w=[act.t, tv, bank_free[B_O]] if k == 0 else (), inc=k == kc - 1)
                    state["pv"] = t
                    bw(B_O, V("tensor_copy", yt[a * 64:a * 64 + 64, qh * 512:qh * 512 + 512],
                              bank[B_O][a * 64:a * 64 + 64, :], w=[t, s_m[3].t]))

            s1(0)
            for u in range(16):
                if u + 1 < 16:
                    s1(u + 1)
                s2(u)
                if u % 2:
                    yield
            pv_t = state["pv"]
            P.dma(pool, D_y[i], yt, s_m[3], [dve.t])

    def log1p_exp(v, t1, t2, t3, out):
        A(t1, v, AF.Abs, w=[dve.t])
        A(t1, t1, AF.Exp, scale=-1.0)
        V("tensor_scalar", t2, t1, 2.0, None, ALU.add, w=[act.t])
        V("reciprocal", t2, t2)
        V("tensor_tensor", t1, t1, t2, ALU.mult)
        V("tensor_tensor", t2, t1, t1, ALU.mult)
        V("tensor_scalar", t3, t2, 1.0 / 17, None, ALU.mult)
        for k in (15, 13, 11, 9, 7, 5, 3):
            V("scalar_tensor_tensor", t3, t3, 1.0 / k, t2, ALU.add, ALU.mult)
        V("scalar_tensor_tensor", t3, t3, 1.0, t1, ALU.add, ALU.mult)
        V("tensor_scalar", t2, v, 0.0, None, ALU.max)
        return V("scalar_tensor_tensor", out, t3, 2.0, t2, ALU.mult, ALU.add)

    def conv(dst, raw, wt, bias):
        V("tensor_scalar", dst, raw[:, 3:3 + T], wt[:, 3:4], bias, ALU.mult, ALU.add)
        for k in range(3):
            t = V("scalar_tensor_tensor", dst, raw[:, k:k + T], wt[:, k:k + 1], dst, ALU.mult, ALU.add)
        return t

    def b3(a, n):
        return a.unsqueeze(2).broadcast_to([a.shape[0], a.shape[1], n])

    def mixer_ssd(c):
        xb = sb("xb", 6 * T, c=c)
        xdt = sb("xdt", 8 * 512, c=c)
        CB = sb("CB", 2 * T, c=c)
        Hs = sb("Hs", 8 * 256, c=c)
        Lb = sb("Lb", 2 * T, c=c)
        Mb = sb("Mb", 2 * T, c=c)
        Eb = sb("Eb", T, c=c)
        raws = sb("raws", 2 * 1028, c=c)
        bmN = sb("bmN", 8 * 128, c=c)
        xd = sb("xd", 512, c=c)
        hw = sb("hw", 32, c=c)
        smal = sb("smal", 64 * 4 + 32, c=c)
        dtN, acN, deN, la = (smal[:, i * 64:(i + 1) * 64] for i in range(4))
        eD = smal[:, 256:288]
        dt8, ac8, r8, sel8 = (Lb[0:8, 0:T], Lb[0:8, T:2 * T], Mb[0:8, 0:T], Mb[0:8, T:2 * T])
        acs_t = sb("acs_t", T, c=c)
        sel_t = sb("sel_t", T, c=c)
        P.dma(pool, r8, I["scon"][0], s_m[0])
        P.dma(pool, sel_t[0:8, :], I["scon"][1], s_m[0])
        P.dma(pool, dt8, D_dt, s_m[1])
        for i in range(2):
            V("memset", raws[:, i * 1028:i * 1028 + 3], 0.0)
        mset = dve.t
        V("tensor_scalar", hw, par[:, PO["conv_w"][0]:PO["conv_w"][0] + 32], 0.5, None, ALU.mult)
        raw_t = [None, None]

        def load_raw(n, src, w=()):
            i = n % 2
            P.dma(pool, raws[:, i * 1028 + 3:i * 1028 + 3 + T], src, s_m[2 + i], [mset, raw_t[i], *w])

        load_raw(0, D_u[4], need(10))
        load_raw(1, D_u[5], need(11))
        V("tensor_scalar", dt8, dt8, par[0:8, PO["dt_bias"][0]:PO["dt_bias"][0] + 1], None, ALU.add, w=[s_m[1].t])
        log1p_exp(dt8, Eb[0:8, :], xdt[0:8, 0:T], xdt[0:8, T:2 * T], dt8)
        A(smal[0:8, 256:257], par[0:8, PO["a_log"][0]:PO["a_log"][0] + 1], AF.Exp)
        V("tensor_scalar", Eb[0:8, :], dt8, smal[0:8, 256:257], -1.0, ALU.mult, ALU.mult, w=[act.t])
        ta = V("tensor_tensor_scan", acs_t[0:8, :], r8, Eb[0:8, :], 0.0, ALU.mult, ALU.add, w=[s_m[0].t])
        yield
        for cc in range(8):
            tr(bank[6][:, cc * 8:cc * 8 + 8], dt8[:, cc * 128:cc * 128 + 128], ident[0:8, 0:8],
               w=[ta, bank_free[6]] if cc == 0 else ())
            t = tr(bank[6][:, 64 + cc * 8:72 + cc * 8], acs_t[0:8, cc * 128:cc * 128 + 128], ident[0:8, 0:8], inc=cc == 7)
        V("tensor_copy", dtN, bank[6][:, 0:64], w=[t])
        bw(6, V("tensor_copy", acN, bank[6][:, 64:128]))
        for h in range(8):
            t = mm(bank[7][:, h * 8:h * 8 + 8], sel_t[0:8, h * 128:h * 128 + 128], acs_t[0:8, 127::128], True, True,
                   w=[bank_free[7], s_m[0].t] if h == 0 else (), inc=h == 7)
        v = V("tensor_tensor", deN.rearrange("p (c h) -> p c h", c=8), bank[7][:, 0:64].rearrange("p (h c) -> p c h", h=8),
              acN.rearrange("p (c h) -> p c h", c=8), ALU.subtract, w=[t])
        A(deN, deN, AF.Exp, w=[v])
        for g in range(2):
            A(eD[g * 64:g * 64 + 64, :].rearrange("p (c r) -> p c r", c=8),
              bank[7][g * 64:g * 64 + 64, g * 32:g * 32 + 32].rearrange("p (r c) -> p c r", c=8), AF.Exp)
        bw(7, act.t)
        order = (4, 5, 0, 1, 2, 3)
        for n, j in enumerate(order):
            i = n % 2
            dst = xb[:, j * T:(j + 1) * T]
            dve.wait([s_m[2 + i].t])
            raw_t[i] = conv(dst, raws[:, i * 1028:(i + 1) * 1028], hw[:, 4 * j:4 * j + 4], hw[:, 24 + j:25 + j])
            if n + 2 < 6:
                jj = order[n + 2]
                load_raw(n + 2, D_u[jj], need(6 + jj))
            a = A(Eb, dst, AF.Tanh, w=[dve.t])
            V("scalar_tensor_tensor", dst, Eb, 1.0, dst, ALU.add, ALU.mult, w=[a])
            yield
        bm, cm = xb[:, 4 * T:5 * T], xb[:, 5 * T:6 * T]
        txb = dve.t
        for cc in range(8):
            b = 6 + cc % 2
            t = tr(bank[b][:, 0:128], bm[:, cc * 128:cc * 128 + 128], ident, w=[txb, bank_free[b]], inc=True)
            bw(b, A(bmN[:, cc * 128:cc * 128 + 128], bank[b][:, 0:128], w=[t]))
            b = B_S[0][cc % 2]
            for j in range(4):
                t = tr(bank[b][:, j * 128:j * 128 + 128], xb[:, j * T + cc * 128:j * T + cc * 128 + 128], ident,
                       w=[bank_free[b]] if j == 0 else (), inc=j == 3)
            bw(b, V("tensor_tensor", xdt[:, cc * 512:cc * 512 + 512].rearrange("p (h e) -> p h e", h=8),
                    bank[b][:, :].rearrange("p (h e) -> p h e", h=8), b3(dtN[:, cc * 8:cc * 8 + 8], 64), ALU.mult, w=[t]))
        yield
        for g in range(2):
            for cc in range(8):
                b = B_S[1][cc // 4]
                t = mm(bank[b][:, (cc % 4) * 128:(cc % 4) * 128 + 128], bm[g * 64:g * 64 + 64, cc * 128:cc * 128 + 128],
                       cm[g * 64:g * 64 + 64, cc * 128:cc * 128 + 128], True, True, w=[bank_free[b]] if cc % 4 == 0 else (),
                       inc=cc % 4 == 3)
                if cc % 4 == 3:
                    o = g * T + (cc // 4) * 512
                    bw(b, V("tensor_tensor", CB[:, o:o + 512].rearrange("p (c l) -> p c l", c=4),
                            bank[b][:, :].rearrange("p (c l) -> p c l", c=4),
                            cn("mle").unsqueeze(1).broadcast_to([128, 4, 128]), ALU.mult, w=[t]))
        th = V("memset", Hs[:, 0:256], 0.0)
        xt = None
        for cc in range(7):
            b = 6 + cc % 2
            v = V("tensor_tensor", xd.rearrange("p (h e) -> p h e", h=8),
                  xdt[:, cc * 512:cc * 512 + 512].rearrange("p (h e) -> p h e", h=8), b3(deN[:, cc * 8:cc * 8 + 8], 64),
                  ALU.mult, w=[act.t, xt])
            for g in range(2):
                xt = mm(bank[b][g * 64:g * 64 + 64, 0:256], bmN[:, cc * 128 + g * 64:cc * 128 + g * 64 + 64],
                        xd[:, g * 256:g * 256 + 256], True, True, w=[v, bank_free[b]] if g == 0 else (), inc=g == 1)
            V("tensor_tensor", Hs[:, (cc + 1) * 256:(cc + 2) * 256].rearrange("p (r e) -> p r e", r=4),
              Hs[:, cc * 256:(cc + 1) * 256].rearrange("p (r e) -> p r e", r=4), b3(eD[:, cc * 4:cc * 4 + 4], 64), ALU.mult)
            th = bw(b, V("tensor_tensor", Hs[:, (cc + 1) * 256:(cc + 2) * 256], Hs[:, (cc + 1) * 256:(cc + 2) * 256],
                         bank[b][:, 0:256], ALU.add, w=[xt]))
            if cc % 3 == 2:
                yield
        Mt = [None, None]

        def pre(h):
            g, i = h // 4, h % 2
            Lh, Mh = Lb[:, i * T:(i + 1) * T], Mb[:, i * T:(i + 1) * T]
            for k in range(2):
                b = B_S[0][k]
                t = mm(bank[b][:, :], sel_t[0:8, h * 128:h * 128 + 128], acs_t[0:8, k * 512:k * 512 + 512], True, True,
                       w=[bank_free[b]], inc=True)
                for cc in range(4 * k, 4 * k + 4):
                    V("tensor_scalar", Lh[:, cc * 128:cc * 128 + 128], bank[b][:, (cc % 4) * 128:(cc % 4) * 128 + 128],
                      acN[:, cc * 8 + h:cc * 8 + h + 1], 0.0, ALU.subtract, ALU.min, w=[t, Mt[i]])
                e = A(Mh[g * 64:g * 64 + 64, k * 512:k * 512 + 512], bank[b][g * 64:g * 64 + 64, :], AF.Exp, w=[dve.t, Mt[i]])
                bw(b, V("tensor_tensor", Mh[g * 64:g * 64 + 64, k * 512:k * 512 + 512],
                        Mh[g * 64:g * 64 + 64, k * 512:k * 512 + 512],
                        cm[g * 64:g * 64 + 64, k * 512:k * 512 + 512], ALU.mult, w=[e]))
            a = A(Lh, Lh, AF.Exp, w=[dve.t])
            return V("tensor_tensor", Lh, Lh, CB[:, g * T:(g + 1) * T], ALU.mult, w=[a])

        nxt = pre(0)
        for h in range(8):
            g, i, r_, j = h // 4, h % 2, h % 4, h // 2
            cur = nxt
            if h + 1 < 8:
                nxt = pre(h + 1)
            Lh, Mh = Lb[:, i * T:(i + 1) * T], Mb[:, i * T:(i + 1) * T]
            o = (h % 2) * 64
            for cc in range(8):
                b = B_S[1][cc // 4]
                reg = bank[b][o:o + 64, (cc % 4) * 128:(cc % 4) * 128 + 128]
                mm(reg, xdt[:, cc * 512 + h * 64:cc * 512 + h * 64 + 64], Lh[:, cc * 128:cc * 128 + 128], True, False,
                   w=[cur, bank_free[b], th])
                Mt[i] = mm(reg, Hs[g * 64:g * 64 + 64, cc * 256 + r_ * 64:cc * 256 + r_ * 64 + 64],
                           Mh[g * 64:g * 64 + 64, cc * 128:cc * 128 + 128], False, True, inc=cc == 7)
            if i:
                for k in range(2):
                    xj = xb[:, j * T + k * 512:j * T + k * 512 + 512]
                    bw(B_S[1][k], V("scalar_tensor_tensor", xj, xj, pr("ssd_d", j), bank[B_S[1][k]][:, :], ALU.mult,
                                    ALU.add, w=[Mt[i]]))
            yield
        zt = None
        for j in range(4):
            z_, xj = CB[:, (j % 2) * T:(j % 2) * T + T], xb[:, j * T:(j + 1) * T]
            t = P.dma(pool, z_, D_u[14 + j], s_m[4 + j % 2], [dve.t, *need(20 + j)])
            a = A(Lb[:, 0:T], z_, AF.Tanh, scale=0.5, w=[t, dve.t])
            V("scalar_tensor_tensor", z_, Lb[:, 0:T], 1.0, z_, ALU.add, ALU.mult, w=[a])
            V("scalar_tensor_tensor", xj, xj, 0.5, z_, ALU.mult, ALU.mult)
            if j == 0:
                t = A(Mb[:, 0:T], xj, AF.Square, w=[dve.t])
            else:
                a = A(Lb[:, T:2 * T], xj, AF.Square, w=[dve.t])
                t = V("tensor_tensor", Mb[:, 0:T], Mb[:, 0:T], Lb[:, T:2 * T], ALU.add, w=[a])
        t = rstd_tail(Mb[:, 0:T], Eb, 512, T, (2, 3), t)
        for j in range(4):
            xj = xb[:, j * T:(j + 1) * T]
            v = V("scalar_tensor_tensor", xj, xj, pr("ssd_norm", j), Eb, ALU.mult, ALU.mult, w=[t])
            P.dma(pool, D_y[8 + j], xj, s_m[j], [v])
        yield

    def mixer_lru(c):
        av, mv, uv = sb("av", 4 * T, c=c), sb("mv", 4 * T, c=c), sb("uv", 4 * T, c=c)
        raws = sb("raws2", 2 * 1028, c=c)
        t1, t2 = sb("lt1", T, c=c), sb("lt2", T, c=c)
        wai = sb("wai", 8 * 128, c=c)
        hb = sb("hb", 24, c=c)
        P.dma(pool, wai, I["w_lru"], s_m[5])
        for i in range(2):
            V("memset", raws[:, i * 1028:i * 1028 + 3], 0.0)
        mset = dve.t
        raw_t = [None, None]

        def load_raw(n, j):
            P.dma(pool, raws[:, (n % 2) * 1028 + 3:(n % 2) * 1028 + 3 + T], D_u[6 + j], s_m[n % 2],
                  [mset, raw_t[n % 2], *need(12 + j)])

        load_raw(0, 0)
        load_raw(1, 1)
        V("tensor_scalar", hb[:, 0:8], par[:, PO["b_a"][0]:PO["b_a"][0] + 8], 0.5, None, ALU.mult)
        V("tensor_scalar", hb[:, 8:12], pr("lam", 0, 4), -1.0, None, ALU.mult)
        log1p_exp(hb[:, 8:12], hb[:, 12:16], hb[:, 16:20], hb[:, 20:24], hb[:, 8:12])
        V("tensor_scalar", hb[:, 8:12], hb[:, 8:12], -4.0, None, ALU.mult)
        for j in range(4):
            a_, m_, u_ = av[:, j * T:(j + 1) * T], mv[:, j * T:(j + 1) * T], uv[:, j * T:(j + 1) * T]
            dve.wait([s_m[j % 2].t])
            xct = raw_t[j % 2] = conv(u_, raws[:, (j % 2) * 1028:(j % 2 + 1) * 1028], pr("lconv_w", 4 * j, 4), pr("lconv_b", j))
            if j + 2 < 4:
                load_raw(j + 2, j + 2)
            for s, dst in enumerate((t1, t2)):
                for k in range(2):
                    b = B_S[s][k]
                    t = mm(bank[b][:, :], wai[:, (s * 4 + j) * 128:(s * 4 + j + 1) * 128], u_[:, k * 512:k * 512 + 512],
                           True, True, w=[xct, bank_free[b], s_m[5].t], inc=True)
                    bw(b, A(dst[:, k * 512:k * 512 + 512], bank[b][:, :], AF.Tanh, scale=0.5, bias=hb[:, 4 * s + j:4 * s + j + 1],
                            w=[t, xct]))
            ta = act.t
            V("tensor_scalar", t1, t1, 1.0, hb[:, 8 + j:9 + j], ALU.add, ALU.mult, w=[ta])
            v = V("tensor_scalar", t2, t2, 0.5, 0.5, ALU.mult, ALU.add)
            A(a_, t1, AF.Exp, w=[v])
            a = A(m_, t1, AF.Tanh, scale=-1.0)
            V("tensor_tensor", u_, u_, t2, ALU.mult, w=[pe.t])
            V("tensor_tensor", t2, a_, a_, ALU.mult, w=[a])
            V("scalar_tensor_tensor", m_, t2, 1.0, m_, ALU.add, ALU.mult)
            yield
        for j in range(4):
            a = A(mv[:, j * T:(j + 1) * T], mv[:, j * T:(j + 1) * T], AF.Sqrt, w=[dve.t])
        for j in range(4):
            m_ = mv[:, j * T:(j + 1) * T]
            V("tensor_tensor", uv[:, j * T:(j + 1) * T], uv[:, j * T:(j + 1) * T], m_, ALU.mult, w=[a])
            V("tensor_tensor_scan", m_, av[:, j * T:(j + 1) * T], uv[:, j * T:(j + 1) * T], 0.0, ALU.mult, ALU.add)
            yield
        for j in range(4):
            g_, m_ = av[:, j * T:(j + 1) * T], mv[:, j * T:(j + 1) * T]
            t = P.dma(pool, g_, D_u[18 + j], s_m[2 + j % 2], [dve.t, *need(24 + j)])
            a = A(t1, g_, AF.Square, w=[t, dve.t])
            V("tensor_scalar", t1, t1, 0.044715, 1.0, ALU.mult, ALU.add, w=[a])
            v = V("tensor_tensor", t1, t1, g_, ALU.mult)
            a = A(t1, t1, AF.Tanh, scale=0.7978845608028654, w=[v])
            V("scalar_tensor_tensor", t1, t1, 1.0, g_, ALU.add, ALU.mult, w=[a])
            v = V("scalar_tensor_tensor", m_, m_, 0.5, t1, ALU.mult, ALU.mult)
            P.dma(pool, D_y[12 + j], m_, s_m[4], [v, s_m[4].t])
            yield

    def mixer_pool(c):
        raw = sb("praw", 2 * 1040, c=c)
        tmp = sb("ptmp", 2 * 1040, c=c)
        wp = sb("wp", 512, c=c)
        yo = sb("yo", 2 * T, c=c)
        P.dma(pool, wp, I["w_pool"], s_m[5])
        for a in (raw, tmp):
            for i in range(2):
                V("memset", a[:, i * 1040:i * 1040 + 16], 0.0)
        mset = dve.t
        used = [None, None]
        for g in range(4):
            i = g % 2
            rw = raw[:, i * 1040:(i + 1) * 1040]
            t = P.dma(pool, rw[:, 16:], D_u[10 + g], s_m[i], [mset, used[i], *need(16 + g)])
            cur, n = rw, 0
            for st_ in (1, 2, 4, 8)[:g + 1]:
                nx = tmp[:, n * 1040:(n + 1) * 1040]
                V("tensor_tensor", nx[:, 16:], cur[:, 16:], cur[:, 16 - st_:1040 - st_], ALU.add, w=[t, pe.t])
                cur, n = nx, 1 - n
            wd = 2 << g
            d = tmp[:, n * 1040:(n + 1) * 1040]
            V("tensor_tensor", d[:, 16:32], cur[:, 16:32], cn("icnt", 16 * g, 16 * g + 16), ALU.mult)
            V("tensor_tensor", d[:, 16:32], d[:, 16:32], rw[:, 16:32], ALU.subtract)
            v = used[i] = V("scalar_tensor_tensor", d[:, 32:], cur[:, 32:], 1.0 / wd, rw[:, 32:], ALU.mult, ALU.subtract)
            for k in range(2):
                b = B_S[g % 2][k]
                t = mm(bank[b][:, :], wp[:, g * 128:g * 128 + 128], d[:, 16 + k * 512:16 + k * 512 + 512], True, True,
                       w=[v, bank_free[b], s_m[5].t], inc=True)
                a = bw(b, A(yo[:, i * T + k * 512:i * T + k * 512 + 512], bank[b][:, :], scale=pr("pool_scale", g),
                            w=[t, s_m[2 + i].t]))
            P.dma(pool, D_y[4 + g], yo[:, i * T:(i + 1) * T], s_m[2 + i], [a])
            yield

    def run_m():
        for f in (mixer_mla, mixer_ssd, mixer_lru, mixer_pool):
            c = ExitStack()
            yield from f(c)
            P.barrier()
            c.close()
            if f is mixer_mla:
                cM.close()

    gs = stream_g()
    while 5 not in u_tok:
        next(gs)
    ms = run_m()
    lead = 0.0
    while True:
        a = next(ms, "end")
        lead += 1.4 if a != "end" else 1000
        while lead >= 1:
            lead -= 1
            if next(gs, "end") == "end":
                break
        if a == "end":
            break
    P.barrier()
    nb = [0]

    def take_bank():
        b = nb[0] % 8
        nb[0] += 1
        return b

    res = sb("res", 8 * T, c=c1)
    c2 = ExitStack()
    mrg = sb("mrg", 8 * T, c=c2)
    yr = sb("yr", 2 * T, c=c2)
    gr = sb("gr", 3 * T, c=c2)
    y_pe = [None] * 4

    def load_y(b):
        for j in range(4):
            i = j % 2
            t = P.dma(pool, yr[:, i * T:(i + 1) * T], D_y[4 * b + j], s_m[i], [dve.t, act.t])
            o = ((b % 2) * 4 + j) * T
            v = split_x((o, o + T), yr[:, i * T:(i + 1) * T], w=[t, y_pe[b - 2] if b > 1 else None])
        return v

    tiles = [(I["w_branch"][b * 8 + m], 4) for b in range(4) for m in range(8)]
    gt, gfree = [None] * 3, [None] * 3

    def load_g(n):
        b, m = divmod(n, 8)
        gt[n % 3] = P.dma(sp, gr[:, (n % 3) * T:(n % 3 + 1) * T], D_g[n], s_ld[n % 3], [gfree[n % 3]])

    load_g(0)
    load_g(1)
    yv = load_y(0)
    for n, w in enumerate(stream(tiles)):
        b, m = divmod(n, 8)
        if n + 2 < 32:
            load_g(n + 2)
        if m == 2 and b < 3:
            yn = load_y(b + 1)
        g_ = gr[:, (n % 3) * T:(n % 3 + 1) * T]
        for h in range(2):
            bk = take_bank()
            hs = slice(h * 512, h * 512 + 512)
            off = (b % 2) * 4 * T
            t = gemm(w, 4, lambda k, c_: (XH[:, off + k * T + c_[0]:off + k * T + c_[1]],
                                          XL[:, off + k * T + c_[0]:off + k * T + c_[1]]),
                     (h * 512, h * 512 + 512), bk, xw=[yv])
            dst = mrg[:, m * T + h * 512:m * T + h * 512 + 512]
            if b == 0:
                gfree[n % 3] = bw(bk, V("scalar_tensor_tensor", dst, g_[:, hs], 1.0, bank[bk][:, :], ALU.add, ALU.mult,
                                        w=[t, gt[n % 3]]))
            else:
                gfree[n % 3] = bw(bk, V("scalar_tensor_tensor", g_[:, hs], g_[:, hs], 1.0, bank[bk][:, :], ALU.add,
                                        ALU.mult, w=[t, gt[n % 3]]))
                gfree[n % 3] = V("tensor_tensor", dst, dst, g_[:, hs], ALU.add)
        if m == 7:
            y_pe[b] = t
            if b < 3:
                yv = yn
    for j in range(8):
        xv = split_x((j * T, (j + 1) * T), mrg[:, j * T:(j + 1) * T], w=[dve.t, pe.t])
    xt_ = [None] * 2
    for m in range(2):
        xt_[m] = P.dma(sp, yr[:, m * T:(m + 1) * T], I["xT"][m], s_x if m else s_ld[3], [dve.t])
    for m, w in enumerate(stream([(I["w_out"][m], 8) for m in range(8)])):
        for h in range(2):
            bk = take_bank()
            t = gemm(w, 8, xs(T), (h * 512, h * 512 + 512), bk, xw=[xv])
            v = bw(bk, V("scalar_tensor_tensor", res[:, m * T + h * 512:m * T + h * 512 + 512], bank[bk][:, :], 0.5,
                         yr[:, (m % 2) * T + h * 512:(m % 2) * T + h * 512 + 512], ALU.mult, ALU.add,
                         w=[t, xt_[m % 2]]))
        if m + 2 < 8:
            xt_[m % 2] = P.dma(sp, yr[:, (m % 2) * T:(m % 2 + 1) * T], I["xT"][m + 2], s_x if m % 2 else s_ld[3], [v])
    P.barrier()
    c2.close()

    def norm_x(gain, write):
        sq_, ac = stg[:, 0:T], stg[:, T:2 * T]
        for j in range(8):
            rj = res[:, j * T:(j + 1) * T]
            if j == 0:
                t = A(ac, rj, AF.Square, w=[dve.t, pe.t, pool.t])
            else:
                a = A(sq_, rj, AF.Square, w=[t, dve.t])
                t = V("tensor_tensor", ac, ac, sq_, ALU.add, w=[a])
        t = rstd_tail(ac, ac, 1024, T, (6, 7), t)
        free = [None, None]
        for j in range(8):
            for h in range(2):
                q = sq_[:, h * 512:h * 512 + 512]
                v = V("scalar_tensor_tensor", q, res[:, j * T + h * 512:j * T + h * 512 + 512], pr(gain, j),
                      ac[:, h * 512:h * 512 + 512], ALU.mult, ALU.mult, w=[t, free[h]])
                free[h] = write(j, h, q, v)
        return dve.t

    def to_x(j, h, q, v):
        return split_x((j * T + h * 512, j * T + h * 512 + 512), q, w=[v])

    xv = norm_x("g_mlp", to_x)
    c2 = ExitStack()
    FH, FL = sb("FH", 8 * T, F32R, c2), sb("FL", 8 * T, F32R, c2)

    def fx(o):
        return lambda k, c_: (FH[:, o + k * T + c_[0]:o + k * T + c_[1]], FL[:, o + k * T + c_[0]:o + k * T + c_[1]])

    tiles = []
    for f in range(9):
        if f < 8:
            tiles += [(I["w_ff1"][4 * f + j], 8) for j in range(4)]
        if f:
            tiles += [(I["w_ff2"][8 * (f - 1) + m], 4) for m in range(8)]
    ws = stream(tiles)
    f_pe, f_v = [None] * 2, [None] * 2
    qf = [None] * 4
    nq = 0
    for f in range(9):
        if f < 8:
            o = (f % 2) * 4 * T
            for j in range(4):
                w = next(ws)
                for h in range(2):
                    bk = take_bank()
                    t = gemm(w, 8, xs(T), (h * 512, h * 512 + 512), bk, xw=[xv])
                    q = stg[:, nq * 512:nq * 512 + 512]
                    bw(bk, A(q, bank[bk][:, :], AF.Relu, w=[t, qf[nq], f_pe[f % 2]]))
                    v = V("tensor_tensor", q, q, q, ALU.mult, w=[act.t])
                    s_ = slice(o + j * T + h * 512, o + j * T + h * 512 + 512)
                    a = A(FH[:, s_], q, w=[v])
                    qf[nq] = f_v[f % 2] = V("tensor_tensor", FL[:, s_], q, FH[:, s_].bitcast(F32), ALU.subtract, w=[a])
                    nq = (nq + 1) % 4
        if f:
            o = ((f - 1) % 2) * 4 * T
            for m in range(8):
                w = next(ws)
                for h in range(2):
                    bk = take_bank()
                    t = gemm(w, 4, fx(o), (h * 512, h * 512 + 512), bk, xw=[f_v[(f - 1) % 2]])
                    rs = res[:, m * T + h * 512:m * T + h * 512 + 512]
                    bw(bk, V("tensor_tensor", rs, rs, bank[bk][:, :], ALU.add, w=[t]))
            f_pe[(f - 1) % 2] = t
    next(ws, None)
    xv = norm_x("g_ple", to_x)
    tp = P.dma(sp, stg[:, :], I["pT"], s_x, [dve.t, act.t])
    for h in range(4):
        a = A(FH[:, h * 512:h * 512 + 512], stg[:, h * 512:h * 512 + 512], w=[tp, pe.t])
        pv = V("tensor_tensor", FL[:, h * 512:h * 512 + 512], stg[:, h * 512:h * 512 + 512],
               FH[:, h * 512:h * 512 + 512].bitcast(F32), ALU.subtract, w=[a])
    ws = stream([x_ for m in range(8) for x_ in ((I["w_ple_gate"][m], 8), (I["w_ple"][m], 2))])
    for m in range(8):
        w = next(ws)
        bs = [take_bank(), take_bank()]
        ts = [gemm(w, 8, xs(T), (h * 512, h * 512 + 512), bs[h], xw=[xv]) for h in range(2)]
        w = next(ws)
        for h in range(2):
            q = stg[:, nq * 512:nq * 512 + 512]
            a = bw(bs[h], A(q, bank[bs[h]][:, :], AF.Tanh, scale=0.5, w=[ts[h], dve.t]))
            bk = take_bank()
            t = gemm(w, 2, fx(0), (h * 512, h * 512 + 512), bk, xw=[pv])
            bw(bk, V("scalar_tensor_tensor", q, q, 1.0, bank[bk][:, :], ALU.add, ALU.mult, w=[a, t]))
            rs = res[:, m * T + h * 512:m * T + h * 512 + 512]
            V("scalar_tensor_tensor", rs, q, 0.5, rs, ALU.mult, ALU.add)
            nq = (nq + 1) % 4
    next(ws, None)

    def to_res(j, h, q, v):
        return V("tensor_copy", res[:, j * T + h * 512:j * T + h * 512 + 512], q)

    norm_x("g_final", to_res)
    for j in range(8):
        P.dma(sp, D_xb[j], res[:, j * T:(j + 1) * T], s_ld[j % 4], [dve.t])
        sp.wait([s_ld[j % 4].t]) if j >= 4 else None
    P.barrier()
    c2.close()
    c1.close()

    S = 1280
    c1 = ExitStack()
    md = sb("md", 48 * 2, c=c1)
    mod = md.rearrange("p (m s) -> p m s", s=2)
    cs_ = sb("cs_", 40, c=c1)
    XH, XL = sb("XH2", 8 * S, F32R, c1), sb("XL2", 8 * S, F32R, c1)
    stg2 = sb("stg2", 2 * S, c=c1)
    c2 = ExitStack()
    xb_ = sb("xb_", 8 * T, c=c2)
    cx = sb("cx", 8 * 256, c=c2)
    r2 = sb("r2", S, c=c2)
    cf = sb("cf", 16, c=c2)
    for j in range(4):
        P.dma(sp, xb_[:, 2 * j * T:(2 * j + 2) * T].rearrange("p (a t) -> p a t", a=2),
              D_xb[2 * j:2 * j + 2].rearrange("a p t -> a p t").rearrange("a p t -> p a t"), s_ld[j])
    P.dma(sp, cx, I["ctxT"], s_x)
    A(cf, pr("cc", 0, 16), AF.Tanh, scale=0.5)
    V("scalar_tensor_tensor", cf, cf, 1.0, pr("cc", 0, 16), ALU.add, ALU.mult, w=[act.t])
    cv = V("tensor_scalar", cf, cf, 0.5, None, ALU.mult)
    for m in range(48):
        n = W["n"]
        W["n"] += 1
        i = n % 3
        t = P.dma(sp, WR[:, i * 1024:(i + 1) * 1024], I["w_ada"][m], s_wr[i], [*(W["raw_free"][i] or [])])
        b = 2 + m % 2
        for k in range(8):
            p_ = mm(bank[b][:, 0:2], WR[:, i * 1024 + k * 128:i * 1024 + k * 128 + 128], cf[:, 2 * k:2 * k + 2],
                    k == 0, k == 7, w=[t, cv, bank_free[b]] if k == 0 else (), inc=k == 7)
        W["raw_free"][i] = [p_]
        bw(b, V("tensor_scalar", mod[:, m, :], bank[b][:, 0:2], pr("b_ada", m), None, ALU.add, w=[p_]))
    for q in range(2):
        V("scalar_tensor_tensor", cs_[:, q * 8:q * 8 + 8], mod[:, 8:16, q], 1.0, pr("norm1", 0, 8), ALU.add, ALU.mult)
    V("scalar_tensor_tensor", cs_[:, 16:24], mod[:, 32:40, 0], 1.0, pr("norm2", 0, 8), ALU.add, ALU.mult)

    def rms_chunks(chunks, n, sqt, acc_, r_, w):
        for j, cj in enumerate(chunks):
            if j == 0:
                t = A(acc_, cj, AF.Square, w=[dve.t, pe.t, *w(j)])
            else:
                a = A(sqt, cj, AF.Square, w=[dve.t, *w(j)])
                t = V("tensor_tensor", acc_, acc_, sqt, ALU.add, w=[a])
        return rstd_tail(acc_, r_, 1024, n, (4, 5), t)

    t = rms_chunks([cx[:, j * 256:(j + 1) * 256] for j in range(8)], 256, stg[:, 0:256], stg[:, 256:512],
                   r2[:, T:S], lambda j: [s_x.t])
    for j in range(8):
        cj = cx[:, j * 256:(j + 1) * 256]
        V("scalar_tensor_tensor", cj, cj, cs_[:, 8 + j:9 + j], r2[:, T:S], ALU.mult, ALU.mult, w=[t])
        v = V("tensor_scalar", cj, cj, mod[:, j, 1:2], None, ALU.add)
        hx = split_x((j * S + T, j * S + S), cj, w=[v])
    t = rms_chunks([xb_[:, j * T:(j + 1) * T] for j in range(8)], T, stg[:, 0:T], stg[:, T:2 * T], r2[:, 0:T],
                   lambda j: [s_ld[j // 2].t])
    for j in range(8):
        xj = xb_[:, j * T:(j + 1) * T]
        V("scalar_tensor_tensor", xj, xj, cs_[:, j:j + 1], r2[:, 0:T], ALU.mult, ALU.mult, w=[t])
        v = V("tensor_scalar", xj, xj, mod[:, j, 0:1], None, ALU.add)
        hx = split_x((j * S, j * S + T), xj, w=[v])
    P.barrier()
    c2.close()

    v_tok = {}

    def stream_g2():
        for m, w in enumerate(stream([(I["w_in2"][m], 8) for m in range(29)])):
            i = m % 2
            dst = stg2[:, i * S:(i + 1) * S]
            es = []
            segs = [(0, 512), (512, 1024)] + ([(1024, 1280)] if m < 7 or 13 <= m < 21 else [])
            for h, (a, b_) in enumerate(segs):
                bk = h % 2
                g = gemm(w, 8, xs(S), (a, b_), bk, xw=[hx])
                e = V("tensor_copy", dst[:, a:b_], bank[bk][:, 0:b_ - a], w=[g, s_st[i].t]) if h == 1 else \
                    A(dst[:, a:b_], bank[bk][:, 0:b_ - a], w=[g, s_st[i].t])
                bank_free[bk] = e
                es.append(e)
                yield
            n = segs[-1][1]
            v_tok[m] = P.dma(sp, D_v[m][:, 0:n], dst[:, 0:n], s_st[i], es)

    def needv(*ms):
        return [v_tok[m] for m in ms]

    def head_out(h, o_, rr, sq_, gt_, gain, mean, gidx, slot, dslot):
        if mean:
            for k in range(2):
                b = B_S[1][k]
                hs = slice(k * 512, k * 512 + 512)
                t = mm(bank[b][:, :], ones, o_[:, hs], True, True, w=[dve.t, bank_free[b]], inc=True)
                bw(b, V("scalar_tensor_tensor", o_[:, hs], bank[b][:, :], -1.0 / 128, o_[:, hs], ALU.mult, ALU.add, w=[t]))
        t = A(sq_, o_, AF.Square, w=[dve.t, pe.t])
        t = rstd_tail(sq_, rr, 128, T, B_S[1], t)
        V("scalar_tensor_tensor", o_, o_, gain, rr, ALU.mult, ALU.mult, w=[t])
        t = P.dma(pool, gt_, D_v[gidx][:, 0:T], slot, [dve.t, *needv(gidx)])
        a = A(sq_, gt_, AF.Tanh, scale=0.5, w=[t, dve.t])
        V("scalar_tensor_tensor", sq_, sq_, 1.0, gt_, ALU.add, ALU.mult, w=[a])
        v = V("scalar_tensor_tensor", o_, o_, 0.5, sq_, ALU.mult, ALU.mult)
        P.dma(pool, D_o[h], o_, dslot, [v])

    def v3(a, n=128):
        return a.rearrange("p (c i) -> p c i", i=n)

    def mixer_gla(c):
        q_, k_ = sb("gq", T, c=c), sb("gk", S, c=c)
        vN = sb("gvN", 10 * 256, c=c)
        b_ = sb("gb", S, c=c)
        qJ = sb("gqJ", 4 * T, c=c)
        kp, ke, keN = sb("gkp", T, c=c), sb("gke", S, c=c), sb("gkeN", S, c=c)
        qe = sb("gqe", T, c=c)
        Ss = sb("gSs", 8 * 128, c=c)
        ST = sb("gST", 2 * 512, c=c)
        o2 = sb("go", 2 * T, c=c)
        gw = stg[:, 0:512]
        sm = stg[:, 512:560]
        P.dma(pool, gw[0:32, :], I["gla_gw"], s_m[0])
        for rc in range(2):
            P.dma(pool, q_, D_v[7 + rc][:, 0:T], s_m[1], [dve.t, pe.t, act.t, *needv(7, 8)])
            P.dma(pool, k_, D_v[1 + rc], s_m[2], [dve.t, *needv(1, 2)])
            for a in range(2):
                t = P.dma(pool, ke, D_v[3 + 2 * rc + a], s_m[3], [dve.t, pe.t, *needv(3, 4, 5, 6)])
                for c0_ in range(0, 10, 4):
                    b = 6 + (c0_ // 4) % 2
                    n = min(4, 10 - c0_)
                    for cc in range(c0_, c0_ + n):
                        p_ = tr(bank[b][:, (cc - c0_) * 128:(cc - c0_) * 128 + 128], ke[:, cc * 128:cc * 128 + 128], ident,
                                w=[t, bank_free[b]] if cc == c0_ else (), inc=cc == c0_ + n - 1)
                    bw(b, A(vN.rearrange("p (c x) -> p c x", c=10)[:, c0_:c0_ + n, a * 128:a * 128 + 128],
                            v3(bank[b][:, 0:n * 128]), w=[p_]))
            yield
            V("tensor_scalar", q_, q_, 0.125, None, ALU.mult, w=[s_m[1].t])
            for d in range(2):
                gz = qJ[0:32, 0:S]
                tz = P.dma(pool, gz, D_v[0][0:32, :], s_m[4], [dve.t, pe.t, act.t, *needv(0)])
                for h, (a0, a1) in enumerate(((0, 512), (512, 1024), (1024, 1280))):
                    b = (2, 3, 4)[h]
                    p_ = mm(bank[b][:, 0:a1 - a0], gw[0:32, (2 * d + rc) * 128:(2 * d + rc) * 128 + 128],
                            gz[:, a0:a1], True, True, w=[tz, s_m[0].t, bank_free[b]], inc=True)
                    bw(b, A(b_[:, a0:a1], bank[b][:, 0:a1 - a0], AF.Identity, bias=pr("gate_b", 2 * d + rc), w=[p_, dve.t]))
                A(ke, b_, AF.Abs)
                A(ke, ke, AF.Exp, scale=-1.0)
                a = A(ke, ke, AF.Ln, bias=1.0)
                V("tensor_scalar", b_, b_, 0.0, None, ALU.min, w=[a])
                V("tensor_tensor", b_, b_, ke, ALU.subtract)
                V("tensor_scalar", keN, b_, 1.0 / 16, None, ALU.mult, w=[pe.t])
                for cc in range(10):
                    lo, hi = cc * 128, cc * 128 + 128
                    sl = slice(lo, hi) if d == 0 else slice(hi - 1, lo - 1 if lo else None, -1)
                    V("tensor_tensor_scan", b_[:, sl], keN[:, sl], keN[:, sl], 0.0, ALU.add, ALU.bypass)
                yield
                eo = 127 if d == 0 else 0
                ro = 15 if d == 0 else 16
                b3_ = v3(b_)
                bend = b3_[:, :, eo:eo + 1]
                V("tensor_tensor", v3(ke), b3_, bend.broadcast_to([128, 10, 128]), ALU.subtract)
                a = A(ke, ke, AF.Exp, scale=-1.0, w=[dve.t])
                aend = sm[:, d * 16:d * 16 + 10]
                A(aend.unsqueeze(2), bend, AF.Exp)
                v = V("tensor_tensor", ke, ke, k_, ALU.mult, w=[a, s_m[2].t])
                for c0_ in range(0, 10, 4):
                    b = 6 + (c0_ // 4) % 2
                    n = min(4, 10 - c0_)
                    for cc in range(c0_, c0_ + n):
                        p_ = tr(bank[b][:, (cc - c0_) * 128:(cc - c0_) * 128 + 128], ke[:, cc * 128:cc * 128 + 128], ident,
                                w=[v, bank_free[b]] if cc == c0_ else (), inc=cc == c0_ + n - 1)
                    bw(b, A(keN[:, c0_ * 128:(c0_ + n) * 128], bank[b][:, 0:n * 128], w=[p_, dve.t]))
                for J in range(4):
                    V("tensor_tensor", v3(qJ[:, J * T:(J + 1) * T]), b3_[:, 0:8, :],
                      b3_[:, 0:8, 32 * J + ro:32 * J + ro + 1].broadcast_to([128, 8, 128]), ALU.subtract, w=[pe.t])
                    V("tensor_scalar", qJ[:, J * T:(J + 1) * T], qJ[:, J * T:(J + 1) * T], 40.0, None, ALU.min)
                a = A(qJ, qJ, AF.Exp, w=[dve.t])
                kb = b_[:, 0:T].rearrange("p (m i) -> p m i", i=32)
                V("tensor_tensor", kp.rearrange("p (m i) -> p m i", i=32), kb,
                  kb[:, :, ro:ro + 1].broadcast_to([128, 32, 32]), ALU.subtract, w=[pe.t])
                v = V("tensor_scalar", kp, kp, -40.0, None, ALU.max)
                A(kp, kp, AF.Exp, scale=-1.0, w=[v])
                a2 = A(qe, b_[:, 0:T], AF.Exp, w=[v, pe.t])
                V("tensor_tensor", qJ.rearrange("p (j t) -> p j t", j=4), qJ.rearrange("p (j t) -> p j t", j=4),
                  q_.unsqueeze(1).broadcast_to([128, 4, T]), ALU.mult, w=[a])
                V("tensor_tensor", kp, kp, k_[:, 0:T], ALU.mult, w=[a2])
                vq = V("tensor_tensor", qe, qe, q_, ALU.mult)
                yield
                order = ([8, 9] + list(range(7))) if d == 0 else ([9, 8] + list(range(7, 0, -1)))
                nxt_of = {8: 9, 9: 0} if d == 0 else {9: 8, 8: 7}
                tmpS = ST[:, 0:128]
                tmpS2 = ST[:, 128:256]
                prev = None
                for n, cc in enumerate(order):
                    b = 6 + n % 2
                    for a in range(2):
                        p_ = mm(bank[b][a * 64:a * 64 + 64, 0:128], keN[:, cc * 128 + a * 64:cc * 128 + a * 64 + 64],
                                vN[:, cc * 256 + a * 128:cc * 256 + a * 128 + 128], True, True,
                                w=[act.t, bank_free[b]] if a == 0 else (), inc=a == 1)
                    if n == 0:
                        dstS = tmpS
                    elif n == 1:
                        i0 = 0 if d == 0 else 7
                        dstS = Ss[:, i0 * 128:i0 * 128 + 128]
                    else:
                        i0 = cc + 1 if d == 0 else cc - 1
                        dstS = Ss[:, i0 * 128:i0 * 128 + 128]
                    if n == 0:
                        bw(b, V("tensor_copy", dstS, bank[b][:, 0:128], w=[p_]))
                    else:
                        bw(b, V("scalar_tensor_tensor", dstS, prev, aend[:, cc:cc + 1], bank[b][:, 0:128], ALU.mult,
                                ALU.add, w=[p_]))
                    prev = dstS
                tS = dve.t
                yield
                mask = cn("mle") if d == 0 else cn("mge")
                stt_ = [None, None]
                for a in range(2):
                    rs = slice(a * 64, a * 64 + 64)
                    for k in range(2):
                        b = B_S[0][k]
                        for cc in range(4 * k, 4 * k + 4):
                            for J in range(4):
                                p_ = mm(bank[b][32 * J:32 * J + 32, (cc % 4) * 128:(cc % 4) * 128 + 128],
                                        kp[rs, cc * 128 + 32 * J:cc * 128 + 32 * J + 32],
                                        qJ[rs, J * T + cc * 128:J * T + cc * 128 + 128], True, True,
                                        w=[vq, bank_free[b]] if cc % 4 == 0 and J == 0 else (), inc=cc % 4 == 3 and J == 3)
                        sv = bw(b, V("tensor_tensor", v3(ST[:, k * 512:k * 512 + 512]), v3(bank[b][:, :]),
                                     mask.unsqueeze(1).broadcast_to([128, 4, 128]), ALU.mult, w=[p_, stt_[k]]))
                        b = B_S[1][k]
                        for cc in range(4 * k, 4 * k + 4):
                            reg = bank[b][:, (cc % 4) * 128:(cc % 4) * 128 + 128]
                            mm(reg, vN[:, cc * 256 + a * 128:cc * 256 + a * 128 + 128],
                               ST[:, cc * 128:cc * 128 + 128], True, False, w=[sv, bank_free[b], tS])
                            p_ = mm(reg, Ss[rs, cc * 128:cc * 128 + 128], qe[rs, cc * 128:cc * 128 + 128], False, True,
                                    inc=cc % 4 == 3)
                        stt_[k] = p_
                        dst = o2[:, a * T + k * 512:a * T + k * 512 + 512]
                        if d == 0:
                            bw(b, V("tensor_copy", dst, bank[b][:, :], w=[p_, s_m[5].t]))
                        else:
                            bw(b, V("tensor_tensor", dst, dst, bank[b][:, :], ALU.add, w=[p_]))
                    yield
            for a in range(2):
                h = 2 * rc + a
                head_out(h, o2[:, a * T:(a + 1) * T], kp, qe, ke[:, 0:T], pr("gla_norm", h), False, 9 + h, s_m[3], s_m[5])
                pool.wait([s_m[5].t])
                yield

    def mixer_ret(c):
        q_, k_ = sb("rq", T, c=c), sb("rk", S, c=c)
        vN, kN = sb("rvN", S, c=c), sb("rkN", S, c=c)
        keN = [sb(f"rke{d}", S, c=c) for d in range(2)]
        qe = [sb(f"rqe{d}", T, c=c) for d in range(2)]
        Ss = [sb(f"rSs{d}", T, c=c) for d in range(2)]
        rC, rS = sb("rC", T, c=c), sb("rS", T, c=c)
        ST = sb("rST", 2 * 512, c=c)
        tm = sb("rtm", S, c=c)
        o_ = sb("ro", T, c=c)
        Dm = sb("rDm", 128 * 4, c=c)
        lg = sb("rlg", 48, c=c)
        P.dma(pool, rC, I["rope2"][0], s_m[0])
        P.dma(pool, rS, I["rope2"][1], s_m[0])
        V("tensor_scalar", lg[:, 0:8], pr("ret_logit", 0, 8), -1.0, None, ALU.mult)
        log1p_exp(lg[:, 0:8], lg[:, 8:16], lg[:, 16:24], lg[:, 24:32], lg[:, 0:8])
        V("tensor_scalar", lg[:, 0:8], lg[:, 0:8], -1.0, None, ALU.mult)
        A(lg[:, 8:16], lg[:, 0:8], AF.Exp, scale=128.0, w=[dve.t])
        for d, nm in enumerate(("colf", "colb")):
            V("tensor_scalar", lg[:, 16 + 4 * d:20 + 4 * d], lg[:, 4 * d:4 * d + 4], cn(nm), None, ALU.mult)
        A(lg[:, 16:24], lg[:, 16:24], AF.Exp, w=[dve.t])
        for h in range(4):
            tq = P.dma(pool, q_, D_v[21 + h][:, 0:T], s_m[1], [dve.t, pe.t, act.t, *needv(21 + h)])
            tk = P.dma(pool, k_, D_v[13 + h], s_m[2], [dve.t, pe.t, *needv(13 + h)])
            tv = P.dma(pool, tm, D_v[17 + h], s_m[3], [dve.t, pe.t, *needv(17 + h)])
            pool.wait([tq, tk, tv])

            def turn(src, dst, w):
                for c0_ in range(0, 10, 4):
                    b = 6 + (c0_ // 4) % 2
                    n = min(4, 10 - c0_)
                    for cc in range(c0_, c0_ + n):
                        p_ = tr(bank[b][:, (cc - c0_) * 128:(cc - c0_) * 128 + 128], src[:, cc * 128:cc * 128 + 128], ident,
                                w=[w, bank_free[b]] if cc == c0_ else (), inc=cc == c0_ + n - 1)
                    bw(b, A(dst[:, c0_ * 128:(c0_ + n) * 128], bank[b][:, 0:n * 128], w=[p_, dve.t]))

            turn(tm, vN, tv)
            for d, (rel, mk) in enumerate((("relf", "mle"), ("relb", "mge"))):
                a = A(Dm[:, d * 128:d * 128 + 128], cn(rel), AF.Exp, scale=lg[:, 4 * d + h:4 * d + h + 1], w=[dve.t])
                V("tensor_tensor", Dm[:, d * 128:d * 128 + 128], Dm[:, d * 128:d * 128 + 128], cn(mk), ALU.mult, w=[a])
                A(Dm[:, 256 + d * 128:384 + d * 128], cn("posf" if d == 0 else "posb"), AF.Exp,
                  scale=lg[:, 4 * d + h:4 * d + h + 1])
            V("tensor_tensor", Dm[:, 0:128], Dm[:, 0:128], Dm[:, 128:256], ALU.add)
            sw = tm[:, 0:T]
            dve.wait([s_m[0].t, tq, tk, pe.t])
            for x_, sc in ((q_, 1.0), (k_, 128.0 ** -0.5)):
                xx = x_[:, 0:T]
                V("tensor_tensor", sw[0:64, :], xx[64:128, :], rS[64:128, :], ALU.mult)
                V("tensor_tensor", sw[64:128, :], xx[0:64, :], rS[0:64, :], ALU.mult)
                V("tensor_tensor", xx, xx, rC, ALU.mult)
                V("tensor_tensor", xx, xx, sw, ALU.add)
            v = V("tensor_scalar", k_, k_, 128.0 ** -0.5, None, ALU.mult)
            turn(k_, kN, v)
            yield
            for d in range(2):
                V("tensor_scalar", keN[d], kN, lg[:, 16 + 4 * d + h:17 + 4 * d + h], None, ALU.mult, w=[act.t, pe.t])
                V("tensor_tensor", v3(qe[d]), v3(q_), Dm[:, 256 + d * 128:384 + d * 128].unsqueeze(1).broadcast_to([128, 8, 128]),
                  ALU.mult)
            vk = dve.t
            orders = ([8, 9] + list(range(7)), [9, 8] + list(range(7, 0, -1)))
            prev = [None, None]
            for n in range(9):
                for d in range(2):
                    cc = orders[d][n]
                    b = 6 + d
                    p_ = mm(bank[b][:, 0:128], keN[d][:, cc * 128:cc * 128 + 128], vN[:, cc * 128:cc * 128 + 128],
                            True, True, w=[vk, bank_free[b]], inc=True)
                    if n == 0:
                        dstS = ST[:, d * 128:d * 128 + 128]
                        bw(b, V("tensor_copy", dstS, bank[b][:, 0:128], w=[p_]))
                    else:
                        i0 = (0 if d == 0 else 7) if n == 1 else (cc + 1 if d == 0 else cc - 1)
                        dstS = Ss[d][:, i0 * 128:i0 * 128 + 128]
                        bw(b, V("scalar_tensor_tensor", dstS, prev[d], lg[:, 8 + 4 * d + h:9 + 4 * d + h],
                                bank[b][:, 0:128], ALU.mult, ALU.add, w=[p_]))
                    prev[d] = dstS
                if n % 3 == 2:
                    yield
            for k in range(2):
                b = B_S[0][k]
                for cc in range(4 * k, 4 * k + 4):
                    p_ = mm(bank[b][:, (cc % 4) * 128:(cc % 4) * 128 + 128], k_[:, cc * 128:cc * 128 + 128],
                            q_[:, cc * 128:cc * 128 + 128], True, True, w=[bank_free[b]] if cc % 4 == 0 else (),
                            inc=cc % 4 == 3)
                sv = bw(b, V("tensor_tensor", v3(ST[:, k * 512:k * 512 + 512]), v3(bank[b][:, :]),
                             Dm[:, 0:128].unsqueeze(1).broadcast_to([128, 4, 128]), ALU.mult, w=[p_]))
                b = B_S[1][k]
                for cc in range(4 * k, 4 * k + 4):
                    reg = bank[b][:, (cc % 4) * 128:(cc % 4) * 128 + 128]
                    cs3 = slice(cc * 128, cc * 128 + 128)
                    mm(reg, vN[:, cs3], ST[:, cs3], True, False, w=[sv, bank_free[b]])
                    mm(reg, Ss[0][:, cs3], qe[0][:, cs3], False, False)
                    p_ = mm(reg, Ss[1][:, cs3], qe[1][:, cs3], False, True, inc=cc % 4 == 3)
                bw(b, V("tensor_copy", o_[:, k * 512:k * 512 + 512], bank[b][:, :], w=[p_, s_m[5].t]))
            yield
            head_out(4 + h, o_, qe[0], qe[1], tm[:, 0:T], pr("ret_norm", h), True, 25 + h, s_m[4], s_m[5])
            yield

    gs = stream_g2()
    while 8 not in v_tok:
        next(gs)

    def run_m2():
        for f in (mixer_gla, mixer_ret):
            c = ExitStack()
            yield from f(c)
            P.barrier()
            c.close()

    lead = 0.0
    for _ in run_m2():
        lead += 1.6
        while lead >= 1:
            lead -= 1
            next(gs, None)
    for _ in gs:
        pass
    P.barrier()

    c2 = ExitStack()
    res = sb("res2", 8 * T, c=c2)
    orw = sb("orw", 2 * T, c=c2)
    mfull = sb("mfull", T, c=c2)
    wr_ = sb("wrt", 128, c=c2)
    for j in range(8):
        P.dma(sp, res[:, j * T:(j + 1) * T], D_xb[j], s_ld[0])
    P.dma(sp, wr_, I["w_router"], s_ld[1])
    for j in range(8):
        i = j % 2
        t = P.dma(pool, orw[:, i * T:(i + 1) * T], D_o[j], s_m[i], [dve.t, act.t])
        xv = split_x((j * T, (j + 1) * T), orw[:, i * T:(i + 1) * T], w=[t])
    for m, w in enumerate(stream([(I["w_out2"][m], 8) for m in range(8)])):
        for h in range(2):
            bk = take_bank()
            t = gemm(w, 8, xs(T), (h * 512, h * 512 + 512), bk, xw=[xv])
            rs = res[:, m * T + h * 512:m * T + h * 512 + 512]
            bw(bk, V("scalar_tensor_tensor", rs, bank[bk][:, :], mod[:, 16 + m, 0:1], rs, ALU.mult, ALU.add,
                     w=[t, s_ld[0].t]))
    xt2 = dve.t
    P.barrier()

    def turn_out(src, dram, w, slots):
        for tc in range(8):
            i = tc % 2
            for q in range(2):
                bk = take_bank()
                for j in range(4):
                    p_ = tr(bank[bk][:, j * 128:j * 128 + 128],
                            src[:, (4 * q + j) * T + tc * 128:(4 * q + j) * T + tc * 128 + 128], ident,
                            w=[w, bank_free[bk]] if j == 0 else (), inc=j == 3)
                e = bw(bk, A(orw[:, i * T + q * 512:i * T + q * 512 + 512], bank[bk][:, :], w=[p_, slots[i].t]))
            P.dma(sp, dram[tc * 128:tc * 128 + 128, :], orw[:, i * T:(i + 1) * T], slots[i], [e])

    turn_out(res, D_acc, xt2, s_ld[2:4])
    cbt = XH[:, 0:8 * 128].bitcast(F32) if False else mfull
    t = rms_chunks([res[:, j * T:(j + 1) * T] for j in range(8)], T, stg[:, 0:T], stg[:, T:2 * T], stg[:, T:2 * T],
                   lambda j: [])
    pe_acc = pe.t
    for j in range(8):
        xj = res[:, j * T:(j + 1) * T]
        V("scalar_tensor_tensor", xj, xj, cs_[:, 16 + j:17 + j], stg[:, T:2 * T], ALU.mult, ALU.mult, w=[t, pe_acc])
        v = V("tensor_scalar", xj, xj, mod[:, 24 + j, 0:1], None, ALU.add)
    hv = v
    b = take_bank()
    for tc in range(8):
        for k in range(8):
            p_ = mm(bank[b][:, tc * 16:tc * 16 + 16], res[:, k * T + tc * 128:k * T + tc * 128 + 128],
                    wr_[:, k * 16:k * 16 + 16], k == 0, k == 7, w=[hv, bank_free[b], s_ld[1].t] if k == 0 else (),
                    inc=k == 7 and tc == 7)
    af = sb("af", 128, c=c1) if False else stg[:, 0:128]
    l3 = bank[b][:, 0:128].rearrange("p (c e) -> p c e", e=16)
    a3 = af.rearrange("p (c e) -> p c e", e=16)
    mx = stg[:, 128:136]
    V("tensor_reduce", mx, l3, AX.X, ALU.max, w=[p_, act.t])
    bw(b, V("tensor_tensor", a3, l3, b3(mx, 16), ALU.subtract))
    a = A(af, af, AF.Exp, w=[dve.t])
    V("tensor_reduce", mx, a3, AX.X, ALU.add, w=[a])
    V("reciprocal", mx, mx)
    v = V("tensor_tensor", a3, a3, b3(mx, 16), ALU.mult)
    affT = stg[0:16, T:2 * T]
    for k in range(2):
        b = take_bank()
        for j in range(4):
            p_ = tr(bank[b][0:16, j * 128:j * 128 + 128], af[:, (4 * k + j) * 16:(4 * k + j) * 16 + 16], ident,
                    w=[v, bank_free[b]] if j == 0 else (), inc=j == 3)
        bw(b, V("tensor_copy", affT[:, k * 512:k * 512 + 512], bank[b][0:16, :], w=[p_]))
    turn_out(res, D_h, hv, s_ld[2:4])
    gv_, ix, ixf = stg[0:16, 256:384], stg[0:16, 384:512].bitcast(U32), stg[0:16, 512:640]
    for rd in range(16):
        g8 = gv_[:, rd * 8:rd * 8 + 8]
        V("max", g8, affT)
        V("max_index", ix[:, rd * 8:rd * 8 + 8], g8, affT)
        V("match_replace", affT, g8, affT, -1.0)
    V("tensor_copy", ixf, ix)
    P.barrier()
    c2.close()
    c1.close()

    c1 = ExitStack()
    gT = sb("gT", 16, c=c1)
    iT = sb("iT", 16, U32, c=c1)
    m5 = sb("m5", T, c=c1)
    fnw = sb("fnw", T, c=c1)
    cb = sb("cb", 8 * 128, c=c1)
    wa = sb("wa", 8 * 128, c=c1)
    XEH, XEL = WH, WL
    HH, HL = sb("HH", 2 * 1408, F32R, c1), sb("HL", 2 * 1408, F32R, c1)
    NR = 6
    er = sb("ER", (NR - 1) * 3072, c=c1)
    ER = [er[:, i * 3072:(i + 1) * 3072] for i in range(NR - 1)] + [WR]
    EH, EL = sb("EH", 2 * 3072, F32R, c1), sb("EL", 2 * 3072, F32R, c1)
    xe = sb("xe", 2 * 1024, c=c1)
    ye = sb("ye", 1024, c=c1)
    hN = sb("hN", 2 * 384, c=c1)
    s_e = [P.slot(f"e{i}") for i in range(NR)]
    s_g = [P.slot(f"g{i}") for i in range(2)]
    s_acc, s_mf = P.slot("acc"), P.slot("mf")
    b = take_bank()
    tr(bank[b][:, 0:16], gv_, ident[0:16, 0:16], w=[bank_free[b]])
    p_ = tr(bank[b][:, 16:32], ixf, ident[0:16, 0:16], inc=True)
    V("tensor_copy", gT, bank[b][:, 0:16], w=[p_])
    tix = bw(b, V("tensor_copy", iT, bank[b][:, 16:32]))

    pieces = []
    for e in range(16):
        for q in range(4):
            n = 384 if q < 3 else 256
            pieces += [(e, 0, q, 8 * n), (e, 1, q, 8 * n)]
        pieces += [(e, 2, q, 11 * 256) for q in range(4)]
    p_raw, p_spl = [None] * NR, [None] * 2
    p_tok = {}

    def e_load(n):
        e, kind, q, size = pieces[n]
        i = n % NR
        src = I[("wg", "wu", "wd")[kind]][e]
        off = q * 8 * 384 if kind < 2 else q * 11 * 256
        p_tok[n] = P.dma(sp, ER[i][:, 0:size], src[:, off:off + size], s_e[i], [*(p_raw[i] or [])])

    def e_split(n):
        size = pieces[n][3]
        i, j = n % NR, n % 2
        raw = ER[i][:, 0:size]
        hi, lo = (t_[:, j * 3072:j * 3072 + size] for t_ in (EH, EL))
        a = A(hi, raw, w=[p_tok[n], p_spl[j]])
        cut = size // 2
        v = V("tensor_tensor", lo, raw, hi.bitcast(F32), ALU.subtract, w=[a])
        p_raw[i] = [a, v]
        return v

    for n in range(NR - 1):
        e_load(n)
    t = P.dma(act, fnw[:, :], I["fnorm"].broadcast_to([128, 1024]), s_mf)
    cf2 = fnw
    cfc = hN[:, 0:16]
    A(cfc, pr("cc", 0, 16), AF.Tanh, scale=0.5)
    V("scalar_tensor_tensor", cfc, cfc, 1.0, pr("cc", 0, 16), ALU.add, ALU.mult, w=[act.t])
    v = V("tensor_scalar", cb.rearrange("p (k n) -> p k n", k=8),
          cfc.rearrange("p (k s) -> p k s", s=2)[:, :, 0:1].broadcast_to([128, 8, 128]), 0.5, None, ALU.mult)
    tw = None
    for m in range(8):
        tw = P.dma(act, wa, I["w_ada"][40 + m], s_mf, [tw and pe.t, s_mf.t])
        b = 6 + m // 4
        for k in range(8):
            p_ = mm(bank[b][:, (m % 4) * 128:(m % 4) * 128 + 128], cb[:, k * 128:k * 128 + 128],
                    wa[:, k * 128:k * 128 + 128], k == 0, k == 7, w=[v, tw, bank_free[b]] if k == 0 else (), inc=k == 7)
    tb = P.dma(act, wa, I["b_ada5"].broadcast_to([128, 1024]), s_mf, [p_])
    for k in range(2):
        bw(6 + k, V("tensor_tensor", m5[:, k * 512:k * 512 + 512], bank[6 + k][:, :], wa[:, k * 512:k * 512 + 512], ALU.add,
                    w=[p_, tb]))

    g_tok, xe_free, x_tok = {}, [None] * 2, {}

    def gather(e):
        g_tok[e] = P.idma(s_g[e % 2], [tix, xe_free[e % 2]], out=xe[:, (e % 2) * 1024:(e % 2 + 1) * 1024],
                          out_offset=None, in_=D_h[:, :],
                          in_offset=bass.IndirectOffsetOnAxis(ap=iT[:, e:e + 1], axis=0))

    xh_pe = [None] * 2

    def turn_x(e):
        i = e % 2
        for q in range(2):
            b = 6 + q
            for j in range(4):
                p_ = tr(bank[b][:, j * 128:j * 128 + 128],
                        xe[:, i * 1024 + (4 * q + j) * 128:i * 1024 + (4 * q + j) * 128 + 128], ident,
                        w=[g_tok[e], bank_free[b]] if j == 0 else (), inc=j == 3)
            s_ = slice(i * 1024 + q * 512, i * 1024 + q * 512 + 512)
            a = A(XEH[:, s_], bank[b][:, :], w=[p_, xh_pe[i]])
            v = bw(b, V("tensor_tensor", XEL[:, s_], bank[b][:, :], XEH[:, s_].bitcast(F32), ALU.subtract, w=[a]))
        xe_free[i] = p_
        x_tok[e] = v

    def egemm(n, b, col, width, K, L, ltok):
        j = n % 2
        for k in range(K):
            lh, ll = L(k)
            rh = EH[:, j * 3072 + k * width:j * 3072 + (k + 1) * width]
            rl = EL[:, j * 3072 + k * width:j * 3072 + (k + 1) * width]
            mm(bank[b][:, col:col + width], lh, rh, k == 0, False, w=[*ltok, bank_free[b]] if k == 0 else ())
            mm(bank[b][:, col:col + width], lh, rl, False, False)
            p_ = mm(bank[b][:, col:col + width], ll, rh, False, k == K - 1, inc=k == K - 1)
        p_spl[j] = p_
        return p_

    gather(0)
    gather(1)
    turn_x(0)
    sp_tok = {0: e_split(0)}
    hh_pe = [None] * 2
    hn_free = [None] * 2
    y_free = None
    NP_ = len(pieces)
    done = None
    for n in range(NP_):
        e, kind, q, size = pieces[n]
        if n + NR - 1 < NP_:
            e_load(n + NR - 1)
        if n + 1 < NP_:
            sp_tok[n + 1] = e_split(n + 1)
        i = e % 2
        if kind < 2:
            w_ = 384 if q < 3 else 256
            b = 2 * (q % 2) + kind
            t = egemm(n, b, 0, w_, 8, lambda k: (XEH[:, i * 1024 + k * 128:i * 1024 + k * 128 + 128],
                                                 XEL[:, i * 1024 + k * 128:i * 1024 + k * 128 + 128]),
                      [sp_tok[n], x_tok[e]])
            if kind == 0:
                ta = t
            else:
                if q == 3:
                    xh_pe[i] = t
                hn = hN[:, (q % 2) * 384:(q % 2) * 384 + w_]
                a = A(hn, bank[b - 1][:, 0:w_], AF.Tanh, scale=0.5, w=[ta, hn_free[q % 2], dve.t])
                v = V("scalar_tensor_tensor", hn, hn, 1.0, bank[b - 1][:, 0:w_], ALU.add, ALU.mult, w=[a])
                bw(b - 1, v)
                v = bw(b, V("scalar_tensor_tensor", hn, hn, 0.5, bank[b][:, 0:w_], ALU.mult, ALU.mult, w=[t]))
                bt = 4 + q % 2
                for j in range(w_ // 128):
                    p_ = tr(bank[bt][:, j * 128:j * 128 + 128], hn[:, j * 128:j * 128 + 128], ident,
                            w=[v, bank_free[bt]] if j == 0 else (), inc=j == w_ // 128 - 1)
                hn_free[q % 2] = p_
                s_ = slice(i * 1408 + q * 384, i * 1408 + q * 384 + w_)
                a = A(HH[:, s_], bank[bt][:, 0:w_], w=[p_, hh_pe[i]])
                h_tok = bw(bt, V("tensor_tensor", HL[:, s_], bank[bt][:, 0:w_], HH[:, s_].bitcast(F32), ALU.subtract,
                                 w=[a]))
        else:
            if q == 0 and e + 1 < 16:
                turn_x(e + 1)
                if e + 2 < 16:
                    gather(e + 2)
            b = 4 + q % 2
            t = egemm(n, b, 0, 256, 11, lambda k: (HH[:, i * 1408 + k * 128:i * 1408 + k * 128 + 128],
                                                   HL[:, i * 1408 + k * 128:i * 1408 + k * 128 + 128]),
                      [sp_tok[n], h_tok])
            if q == 3:
                hh_pe[i] = t
            v = bw(b, V("scalar_tensor_tensor", ye[:, q * 256:q * 256 + 256], bank[b][:, 0:256], gT[:, e:e + 1],
                        m5[:, q * 256:q * 256 + 256], ALU.mult, ALU.mult, w=[t, y_free]))
            if q == 3:
                y_free = P.idma(s_acc, [v, s_acc.t], out=D_acc[:, :],
                                out_offset=bass.IndirectOffsetOnAxis(ap=iT[:, e:e + 1], axis=0),
                                in_=ye[:, :], in_offset=None, compute_op=ALU.add)
    fin = P.slot("fin")
    f_l = [P.slot(f"fl{i}") for i in range(2)]
    f_s = [P.slot(f"fs{i}") for i in range(2)]
    for tc in range(8):
        i = tc % 2
        xr = ER[i][:, 0:1024]
        yo = ER[i][:, 1024:2048]
        ss = hN[:, i * 4:i * 4 + 1]
        t = P.dma(sp, xr, D_acc[tc * 128:tc * 128 + 128, :], f_l[i], [s_acc.t, dve.t, act.t, pe.t])
        a = A(yo, xr, AF.Square, accum_out=ss, w=[t, dve.t, f_s[i].t])
        V("tensor_scalar", ss, ss, 1.0 / 1024, EPS, ALU.mult, ALU.add, w=[a])
        v = V("reciprocal", ss, ss)
        a = A(ss, ss, AF.Sqrt, w=[v])
        v = V("scalar_tensor_tensor", yo, xr, ss, fnw, ALU.mult, ALU.mult, w=[a, s_mf.t])
        P.dma(sp, out[tc * 128:tc * 128 + 128, :], yo, f_s[i], [v])
    sp.wait([s.t for s in P.slots])
    P.barrier()
    c1.close()

    block = ctx.enter_context(nc.Block())

    @block.tensor
    def _(e):
        pe.play(e)

    @block.scalar
    def _(e):
        act.play(e)

    @block.vector
    def _(e):
        dve.play(e)

    @block.gpsimd
    def _(e):
        pool.play(e)

    @block.sync
    def _(e):
        sp.play(e)

    ctx.close()


def chunks(w, cols):
    K = w.shape[0] // 128
    return w[:, cols].reshape(K, 128, -1).transpose(1, 0, 2)


def layout(x, **A):
    L = {}
    f = np.float32
    ar = np.arange
    L["xT"] = np.ascontiguousarray(x[0].T.reshape(8, 128, 1024))
    w = A["w_in"][0]
    pad = lambda *parts: np.concatenate(parts, 1)
    sw = np.r_[16:32, 0:16]
    kr = w[:, 640:672]
    z = lambda n: np.zeros((1024, n), f)
    krdt = np.concatenate([kr, w[:, 2464:2472], z(24), kr[:, sw], z(32)], 1)
    cols = [w[:, 0:640], krdt, w[:, 1696:2464], w[:, 2984:3496], w[:, 672:1184], w[:, 1184:1696],
            w[:, 2472:2984], w[:, 3496:7592]]
    w = np.concatenate(cols, 1)
    tile = lambda w: np.ascontiguousarray(
        w.reshape(w.shape[0] // 128, 128, w.shape[1] // 128, 128).transpose(2, 1, 0, 3)).reshape(
            w.shape[1] // 128, 128, -1)
    L["w_in"] = tile(w)
    uq = A["w_uq"][0].reshape(384, 8, 96)
    uq = np.concatenate([uq[:, :, :64].reshape(384, 512), uq[:, :, 64:].reshape(384, 256),
                         uq[:, :, 64:][:, :, sw].reshape(384, 256)], 1)
    L["w_uq"] = np.ascontiguousarray(tile(uq).transpose(1, 0, 2)).reshape(128, 8 * 384)
    ukv = A["w_ukv"][0].reshape(256, 8, 128)
    kn = tile(np.ascontiguousarray(ukv[:, :, :64]).reshape(256, 512)).transpose(1, 0, 2).reshape(128, 1024)
    vv = np.ascontiguousarray(ukv[:, :, 64:]).reshape(2, 128, 512).transpose(1, 0, 2).reshape(128, 1024)
    L["w_ukv"] = np.concatenate([kn, vv], 1)
    wl = np.zeros((2, 4, 128, 128), f)
    for s, n in enumerate(("lru_w_a", "lru_w_i")):
        for b in range(8):
            o = (b % 2) * 64
            wl[s, b // 2, o:o + 64, o:o + 64] = A[n][0, b]
    L["w_lru"] = np.ascontiguousarray(wl.reshape(8, 128, 128).transpose(1, 0, 2)).reshape(128, 1024)
    L["w_branch"] = np.concatenate([tile(A["w_branch"][0, b]) for b in range(4)])
    L["w_out"] = tile(A["w_out"][0])
    L["w_ff1"] = tile(A["w_ff1"][0])
    L["w_ff2"] = np.concatenate([tile(A["w_ff2"][0, q * 512:(q + 1) * 512]) for q in range(8)])
    L["w_ple_gate"] = tile(A["w_ple_gate"][0])
    L["w_ple"] = tile(A["w_ple"][0])
    L["pT"] = np.ascontiguousarray(A["p"][0, 0].T.reshape(2, 128, 1024).transpose(1, 0, 2)).reshape(128, 2048)
    L["w_ada"] = tile(A["w_ada_2"][0])
    L["b_ada5"] = np.ascontiguousarray(A["b_ada_2"][:, 5120:])
    L["fnorm"] = np.ascontiguousarray(A["final_norm_w_2"][None])
    L["ctxT"] = np.ascontiguousarray(A["ctx_2"][0].T.reshape(8, 128, 256).transpose(1, 0, 2)).reshape(128, 2048)
    w2 = A["w_in_2"][0]
    L["w_in2"] = tile(np.concatenate([w2[:, 1024:1056], np.zeros((1024, 96), f), w2[:, 256:512], w2[:, 512:1024],
                                      w2[:, 0:256], w2[:, 1056:1568], w2[:, 2080:2592], w2[:, 2592:3104],
                                      w2[:, 1568:2080], w2[:, 3104:3616]], 1))
    gw = np.zeros((32, 2, 256), f)
    for d in range(2):
        gw[16 * d:16 * d + 16, d] = A["gla_gate_w_2"][0, d]
    L["gla_gw"] = gw.reshape(32, 512)
    L["w_out2"] = tile(A["w_out_2"][0])
    L["w_router"] = np.ascontiguousarray(A["w_router_2"][0].reshape(8, 128, 16).transpose(1, 0, 2)).reshape(128, 128)
    row = np.broadcast_to(ar(16)[:, None], (16, 64)).reshape(-1).astype(f)
    cl = np.broadcast_to(ar(64)[None], (16, 64)).reshape(-1).astype(f)
    iv = (f(10000.0) ** (-ar(32, dtype=f) / f(32))).astype(f)
    ang = np.concatenate([iv[:, None] * row[None], iv[:, None] * cl[None]], 0).astype(f)
    L["rope2"] = np.stack([np.concatenate([np.cos(ang)] * 2), np.concatenate([np.sin(ang), -np.sin(ang)])]).astype(f)

    def cut(w, widths, K):
        w = w.reshape(16, K, 128, -1)
        out, at = [], 0
        for n in widths:
            out.append(w[:, :, :, at:at + n].transpose(0, 2, 1, 3).reshape(16, 128, K * n))
            at += n
        return np.concatenate(out, 2)

    L["wg"] = cut(A["w_exp_gate_2"][0], (384, 384, 384, 256), 8)
    L["wu"] = cut(A["w_exp_up_2"][0], (384, 384, 384, 256), 8)
    L["wd"] = cut(A["w_exp_down_2"][0], (256,) * 4, 11)
    L["w_pool"] = np.ascontiguousarray(A["w_pool"][0].transpose(1, 0, 2)).reshape(128, 512)
    L["positions"] = A["positions"]

    par = np.zeros((128, NPAR), f)

    def put(name, a):
        o, n = PO[name]
        par[:a.shape[0], o:o + n] = a

    col = lambda v: v.reshape(-1, 128).T
    put("g_mix", col(A["g_mix"][0]))
    put("q_norm", col(A["q_norm"][0]))
    put("kv_norm", col(A["kv_norm"][0]))
    put("pool_scale", col(A["pool_scale"][0]))
    put("conv_w", A["ssd_conv_w"][0].reshape(4, 6, 128).transpose(2, 1, 0).reshape(128, 24))
    put("conv_b", col(A["ssd_conv_b"][0]))
    put("ssd_norm", col(A["ssd_norm"][0]))
    put("ssd_d", col(np.repeat(A["ssd_d"][0], 64)))
    put("lconv_w", A["lru_conv_w"][0].reshape(4, 4, 128).transpose(2, 1, 0).reshape(128, 16))
    put("lconv_b", col(A["lru_conv_b"][0]))
    put("b_a", col(A["lru_b_a"][0]))
    put("b_i", col(A["lru_b_i"][0]))
    put("lam", col(A["lru_lambda"][0]))
    put("g_mlp", col(A["g_mlp"][0]))
    put("g_ple", col(A["g_ple"][0]))
    put("g_final", col(A["g_final"]))
    put("norm1", col(A["norm1_w_2"][0]))
    put("norm2", col(A["norm2_w_2"][0]))
    put("b_ada", col(A["b_ada_2"][0]))
    put("gate_b", col(A["gla_gate_b_2"][0].reshape(-1)))
    put("gla_norm", col(A["gla_norm_w_2"][0]))
    put("ret_norm", col(A["ret_norm_w_2"][0]))
    put("cc", np.stack([col(A["c_2"][0]), col(A["c_ctx_2"])], 2).reshape(128, 16))
    put("dt_bias", A["ssd_dt_bias"][0][:, None])
    put("a_log", A["ssd_a_log"][0][:, None])
    put("ret_logit", np.broadcast_to(A["ret_decay_logit_2"][0].reshape(1, 8), (128, 8)))
    L["par"] = par

    con = np.zeros((128, NCON), f)

    def putc(name, a):
        o, n = CO[name]
        con[:a.shape[0], o:o + n] = a

    p, q = ar(128)[:, None], ar(128)[None, :]
    putc("ident", np.eye(128, dtype=f))
    putc("ones", np.ones((128, 128), f))
    putc("mle", (p <= q).astype(f))
    putc("mge", (p >= q).astype(f))
    putc("mneg", np.where(q > p, f(-1e30), f(0)))
    inv = (f(1.0) / (f(10000.0) ** (ar(0, 32, 2, dtype=f) / f(32)))).astype(f)
    putc("inv", inv[ar(128) % 16][:, None])
    putc("sgn", np.where(ar(128) % 32 < 16, f(-1), f(1))[:, None])
    ic = np.concatenate([1.0 / np.minimum(ar(16) + 1, ww) for ww in (2, 4, 8, 16)])
    putc("icnt", np.broadcast_to(ic[None].astype(f), (128, 64)))
    putc("relf", np.maximum(q - p, 0).astype(f))
    putc("relb", np.maximum(p - q, 0).astype(f))
    putc("posf", np.broadcast_to((q + 1).astype(f), (128, 128)))
    putc("posb", np.broadcast_to((128 - q).astype(f), (128, 128)))
    putc("colf", (127 - p).astype(f))
    putc("colb", p.astype(f))
    s8 = np.zeros((8, 8, 128), f)
    s8[ar(8), ar(8)] = 1
    L["scon"] = np.stack([np.broadcast_to((ar(1024) % 128 != 0).astype(f)[None], (8, 1024)), s8.reshape(8, 1024)])
    L["con"] = con
    return L


def kernel(**inputs):
    import numpy as _np
    import concourse.bacc as _bacc
    from concourse import mybir as _mybir
    from concourse.bass_utils import run_bass_kernel_spmd as _run

    L = layout(**{k: _np.asarray(v) for k, v in inputs.items()})
    nc = _bacc.Bacc("TRN2", target_bir_lowering=False, num_devices=1)
    arrays, I = {}, {}
    for name, a in L.items():
        a = _np.ascontiguousarray(a)
        arrays[f"in_{name}_dram"] = a
        I[name] = nc.dram_tensor(f"in_{name}_dram", a.shape, _mybir.dt.from_np(a.dtype), kind="ExternalInput").ap()
    out = nc.dram_tensor("out_0_dram", (1024, 1024), F32, kind="ExternalOutput").ap()
    program(nc, I, out)
    r = _run(nc, [arrays], core_ids=[0])
    return r.results[0]["out_0_dram"].reshape(1, 1024, 1024)
```

```python
from contextlib import ExitStack

import numpy as np
import concourse.bass as bass
from concourse import mybir

F32 = mybir.dt.float32
F32R = mybir.dt.float32r
I32 = mybir.dt.int32
U32 = mybir.dt.uint32
ALU = mybir.AluOpType
AF = mybir.ActivationFunctionType
AX = mybir.AxisListType
EPS = 1e-6
T = 1024
H2 = 512

PAR = [("g_mix", 8), ("q_norm", 3), ("kv_norm", 2), ("pool_scale", 4), ("conv_w", 24), ("conv_b", 6),
       ("ssd_norm", 4), ("ssd_d", 4), ("lconv_w", 16), ("lconv_b", 4), ("b_a", 4), ("b_i", 4), ("lam", 4),
       ("g_mlp", 8), ("g_ple", 8), ("g_final", 8), ("norm1", 8), ("norm2", 8), ("b_ada", 48), ("gate_b", 4),
       ("gla_norm", 4), ("ret_norm", 4), ("cc", 16), ("dt_bias", 1), ("a_log", 1), ("ret_logit", 8)]
CON = [("ident", 128), ("ones", 128), ("mle", 128), ("mneg", 128), ("inv", 1), ("sgn", 1),
       ("icnt", 64), ("mge", 128), ("relf", 128), ("relb", 128), ("posf", 128), ("posb", 128), ("colf", 1), ("colb", 1)]


def offsets(table):
    out, at = {}, 0
    for name, n in table:
        out[name] = (at, n)
        at += n
    return out, at


PO, NPAR = offsets(PAR)
CO, NCON = offsets(CON)
NCON1 = CO["mge"][0]


class Tok:
    def __init__(self, sem, val, at=0.0):
        self.sem, self.val, self.at = sem, val, at


def width(ap):
    n = 1
    for x in ap.shape[1:]:
        n *= x
    return n


class Eng:

    def __init__(self, name, sem, prog):
        self.name, self.sem, self.n, self.list, self.seen = name, sem, 0, [], {}
        self.time, self.prog = 0.0, prog

    def wait(self, toks):
        for t in toks:
            if t is None:
                continue
            self.time = max(self.time, t.at + (0.1 if t.sem is not self.sem else 0.06))
            if self.seen.get(t.sem.name, 0) < t.val:
                self.seen[t.sem.name] = t.val
                self.list.append(("wait", t.sem, t.val))

    def put(self, method, args, kw, w=(), inc=True, dur=0.1):
        self.prog.fill_to(max([self.time] + [t.at for t in w if t is not None]))
        self.wait(w)
        self.time += dur
        if inc:
            self.n += 1
            self.last = self.time
        self.list.append(("op", method, args, kw, (self.sem, 1) if inc else None))
        return self.t

    @property
    def t(self):
        return Tok(self.sem, self.n, self.last) if self.n else None

    def play(self, eng):
        table = {"tensor_tensor": eng.tensor_tensor if self.name in ("dve", "pool") else None,
                 "wait_ge": eng.wait_ge, "dma_start": eng.dma_start}
        if self.name == "dve":
            table.update(tensor_scalar=eng.tensor_scalar, scalar_tensor_tensor=eng.scalar_tensor_tensor,
                         tensor_tensor_scan=eng.tensor_tensor_scan, tensor_copy=eng.tensor_copy,
                         memset=eng.memset, reciprocal=eng.reciprocal, tensor_reduce=eng.tensor_reduce,
                         max=eng.max, max_index=eng.max_index, match_replace=eng.match_replace)
        if self.name == "pool":
            table.update(tensor_scalar=eng.tensor_scalar, tensor_copy=eng.tensor_copy, memset=eng.memset,
                         indirect_dma_start=eng.indirect_dma_start)
        if self.name == "act":
            table.update(activation=eng.activation)
        if self.name == "pe":
            table.update(matmul=eng.matmul, transpose=eng.transpose)
        for item in self.list:
            if item[0] == "wait":
                eng.wait_ge(item[1], item[2])
            else:
                _, method, args, kw, inc = item
                ins = table[method](*args, **kw)
                if inc:
                    ins.then_inc(*inc)


class Slot:

    def __init__(self, sem):
        self.sem, self.val, self.at = sem, 0, 0.0

    def next(self, at):
        self.val += 16
        self.at = at
        return Tok(self.sem, self.val, at)

    @property
    def t(self):
        return Tok(self.sem, self.val, self.at) if self.val else None


class Prog:
    def __init__(self, nc, ctx):
        self.nc, self.ctx = nc, ctx
        self.pe, self.act, self.dve, self.pool, self.sp = (
            Eng(n, ctx.enter_context(nc.semaphore("c_" + n)), self) for n in ("pe", "act", "dve", "pool", "sp"))
        self.slots, self.filler, self.filling = [], None, False

    def fill_to(self, at):
        if self.filler is None or self.filling:
            return
        self.filling = True
        while self.pe.time + 0.6 < at:
            if next(self.filler, "end") == "end":
                self.filler = None
                break
        self.filling = False

    def slot(self, name):
        s = Slot(self.ctx.enter_context(self.nc.semaphore("d_" + name)))
        self.slots.append(s)
        return s

    def A(self, out, in_, f=AF.Copy, w=(), **kw):
        return self.act.put("activation", (out, in_, f), kw, [self.act.t, *w], dur=0.2 + width(out) / 1200)

    def V(self, method, *args, w=(), **kw):
        n = width(args[1] if method in ("tensor_reduce", "max", "max_index") else args[0])
        if method in ("reciprocal", "tensor_tensor_scan"):
            n *= 2
        if method in ("tensor_scalar", "memset"):
            n *= 0.6
        return self.dve.put(method, args, kw, [self.dve.t, *w], dur=0.07 + n / 960)

    def G(self, method, *args, w=(), **kw):
        return self.pool.put(method, args, kw, [self.pool.t, *w], dur=0.1 + width(args[0]) * 0.0024)

    def mm(self, out, l, r, start, stop, w=(), inc=False):
        n = width(out)
        d = n / 2350 if l.dtype == F32R else max(n, 64) / 580
        return self.pe.put("matmul", (out, l, r), dict(start=start, stop=stop), w, inc, dur=d)

    def tr(self, out, in_, ident, w=(), inc=False):
        return self.pe.put("transpose", (out, in_, ident), {}, w, inc, dur=0.06)

    def dma(self, eng, out, in_, slot, w=()):
        eng.wait(w)
        eng.time += 1.1 if eng is self.pool else 0.06
        t = slot.next(eng.time + 2.3 + out.shape[0] * width(out) * 4 / 300e3)
        eng.list.append(("op", "dma_start", (out, in_), {}, (slot.sem, 16)))
        return t

    def idma(self, slot, w=(), **kw):
        self.pool.wait(w)
        self.pool.time += 1.1
        t = slot.next(self.pool.time + 5.0)
        self.pool.list.append(("op", "indirect_dma_start", (), kw, (slot.sem, 16)))
        return t

    def barrier(self):
        toks = [e.t for e in (self.pe, self.act, self.dve, self.pool)] + [s.t for s in self.slots]
        for e in (self.pe, self.act, self.dve, self.pool, self.sp):
            e.wait(toks)
        m = max(e.time for e in (self.pe, self.act, self.dve, self.pool))
        for e in (self.pe, self.act, self.dve, self.pool, self.sp):
            e.time = m


def program(nc, I, out, stop=99):
    ctx = ExitStack()
    P = Prog(nc, ctx)
    pe, act, dve, pool, sp = P.pe, P.act, P.dve, P.pool, P.sp
    A, V, G, mm, tr = P.A, P.V, P.G, P.mm, P.tr

    def sb(name, n, dt=F32, c=ctx, p=128):
        return c.enter_context(nc.sbuf_tensor(name, [p, n], dt))[:, :]

    def scratch(name, shape):
        return nc.dram_tensor(name, shape, F32, kind="Internal").ap()

    D_u = scratch("D_u", [22, 128, T])
    D_g = scratch("D_g", [32, 128, T])
    D_y = scratch("D_y", [16, 128, T])
    D_dt = scratch("D_dt", [8, T])
    D_xb = scratch("D_xb", [8, 128, T])
    D_v = scratch("D_v", [29, 128, 1280])
    D_o = scratch("D_o", [8, 128, T])
    D_h = scratch("D_h", [T, 1024])
    D_m5 = scratch("D_m5", [1, 1024])
    D_acc = scratch("D_acc", [T, 1024])

    par = sb("par", NPAR)
    con = sb("con", NCON1)
    con2 = [None]
    bank = [ctx.enter_context(nc.psum_tensor(f"bank{i}", [128, 512], F32))[:, :] for i in range(8)]

    def pr(name, i=0, n=1):
        return par[:, PO[name][0] + i:PO[name][0] + i + n]

    def cn(name, a=0, b=None):
        o, n = CO[name]
        src, o = (con, o) if o < NCON1 else (con2[0], o - NCON1)
        return src[:, o + a:o + (n if b is None else b)]

    ident, ones = cn("ident"), cn("ones")

    c1 = ExitStack()
    WH, WL = sb("WH", 2048, F32R), sb("WL", 2048, F32R)
    WR = sb("WR", 3 * 1024)
    stg = sb("stg", 2048)
    res = sb("res", 8 * T)
    aq2 = sb("aq2", 2 * T)
    acq, ac2 = aq2[:, 0:T], aq2[:, T:2 * T]
    md = sb("md", 96)
    mod = md.rearrange("p (m s) -> p m s", s=2)
    cs_ = sb("cs_", 24)
    cf = sb("cf", 16)
    XH, XL = sb("XH", 8 * T, F32R, c1), sb("XL", 8 * T, F32R, c1)
    s_par = P.slot("par")
    s_wr = [P.slot(f"wr{i}") for i in range(3)]
    s_ld = [P.slot(f"ld{i}") for i in range(4)]
    s_st = [P.slot(f"st{i}") for i in range(2)]
    s_x = P.slot("x")
    s_m = [P.slot(f"m{i}") for i in range(6)]

    P.dma(sp, par, I["par"], s_par)
    t_par = P.dma(sp, con, I["con"][:, 0:NCON1], s_par)

    W = dict(n=0, spl=0, gemm=None, loaded=[], raw_free=[None] * 3, spl_free=[None] * 2, halves=[None] * 2)

    def w_load(src, K):
        n = W["n"]
        W["n"] += 1
        i = n % 3
        t = P.dma(sp, WR[:, i * 1024:i * 1024 + abs(K) * 128], src, s_wr[i], [*(W["raw_free"][i] or [])])
        W["loaded"].append((n, K, t))

    def w_split(eng="pool"):
        n, K, t = W["loaded"].pop(0)
        if K < 0:
            return None, (n % 3, t)
        i, j = n % 3, W["spl"] % 2
        W["spl"] += 1
        raw = WR[:, i * 1024:i * 1024 + K * 128]
        hi, lo = WH[:, j * 1024:j * 1024 + K * 128], WL[:, j * 1024:j * 1024 + K * 128]
        a = A(hi, raw, w=[t, W["spl_free"][j]])
        put = G if eng == "pool" else V
        b = put("tensor_tensor", lo, raw, hi.bitcast(F32), ALU.subtract, w=[t, a, W["spl_free"][j]])
        W["raw_free"][i] = [a, b]
        return j, [a, b]

    def stream(tiles, eng="pool"):
        tiles = list(tiles)
        for s, K in tiles[:2]:
            w_load(s, K)
        nxt = w_split(eng)
        for n, (s, K) in enumerate(tiles):
            if n + 2 < len(tiles):
                w_load(*tiles[n + 2])
            cur = nxt
            nxt = w_split(eng) if n + 1 < len(tiles) else None
            yield cur

    bank_free = [None] * 8

    def gemm_steps(w, K, x, cols, b, xw=(), xk=None):
        j, wt = w
        n = cols[1] - cols[0]
        first = True
        for k in range(K):
            whi = WH[:, j * 1024 + k * 128:j * 1024 + k * 128 + 128]
            wlo = WL[:, j * 1024 + k * 128:j * 1024 + k * 128 + 128]
            xhi, xlo = x(k, cols)
            for i, (l, r) in enumerate(((whi, xhi), (whi, xlo), (wlo, xhi))):
                last = k == K - 1 and l is wlo
                t = mm(bank[b][:, 0:n], l, r, first, last,
                       w=[*(wt + list(xw) + [bank_free[b]] if first else ()),
                          *([xk[k]] if xk and i == 0 else ())], inc=last)
                first = False
            if not last:
                yield
        W["spl_free"][j] = t
        W["gemm"] = t

    def gemm(*args, **kw):
        for _ in gemm_steps(*args, **kw):
            pass
        return W["gemm"]

    def evac(out, in_, w):
        if act.time <= dve.time:
            return A(out, in_, w=w)
        return V("tensor_copy", out, in_, w=w)

    def xs(S):
        return lambda k, c: (XH[:, k * S + c[0]:k * S + c[1]], XL[:, k * S + c[0]:k * S + c[1]])

    def split_x(dst, src, w=()):
        hi, lo = XH[:, dst[0]:dst[1]], XL[:, dst[0]:dst[1]]
        a = A(hi, src, w=w)
        return V("tensor_tensor", lo, src, hi.bitcast(F32), ALU.subtract, w=[a, *w])

    dve_t = [None, None]

    def xc(j):
        return res[:, j * T:(j + 1) * T]

    c0 = ExitStack()
    sq = sb("sq", 2 * T, c=c0)
    r = sb("r", T, c=c0)
    for j in range(4):
        P.dma(sp, res[:, 2 * j * T:(2 * j + 2) * T].rearrange("p (a t) -> p a t", a=2),
              I["xT"][2 * j:2 * j + 2].rearrange("a p t -> p a t"), s_ld[j])

    def rstd_tail(acc, r, D, n, banks, t):
        for h in range(0, n, 512):
            b = banks[h // 512]
            m = min(512, n - h)
            t2 = mm(bank[b][:, 0:m], ones, acc[:, h:h + m], True, True, w=[t, bank_free[b], t_par], inc=True)
            v = V("tensor_scalar", r[:, h:h + m], bank[b][:, 0:m], 1.0 / D, EPS, ALU.mult, ALU.add,
                  w=[t2, act.t])
            bank_free[b] = v
            V("reciprocal", r[:, h:h + m], r[:, h:h + m])
        return A(r[:, 0:n], r[:, 0:n], AF.Sqrt, w=[dve.t])

    for j in range(8):
        if j == 0:
            t = A(acq, xc(0), AF.Square, w=[s_ld[0].t])
        else:
            q = sq[:, (j % 2) * T:(j % 2) * T + T]
            a = A(q, xc(j), AF.Square, w=[s_ld[j // 2].t, dve_t[j % 2]])
            t = dve_t[j % 2] = V("tensor_tensor", acq, acq, q, ALU.add, w=[a])
    t = rstd_tail(acq, r, 1024, T, (0, 1), t)
    hx = []
    for j in range(8):
        v = V("scalar_tensor_tensor", xc(j), xc(j), pr("g_mix", j), r, ALU.mult, ALU.mult, w=[t, t_par])
        hx.append(split_x((j * T, (j + 1) * T), xc(j), w=[v]))
    c0.close()

    u_tok = {}
    cM = ExitStack()
    cqv = sb("cqv", 6 * T, c=cM)

    class Region:

        def __init__(self, c):
            self.c, self.at = c, 0

        def __call__(self, name, n, c=None):
            if self.at + n <= 8 * T:
                self.at += n
                return res[:, self.at - n:self.at]
            return sb(name, n, c=self.c)

    A(cf, pr("cc", 0, 16), AF.Tanh, scale=0.5, w=[t_par])
    V("scalar_tensor_tensor", cf, cf, 1.0, pr("cc", 0, 16), ALU.add, ALU.mult, w=[act.t])
    cv = V("tensor_scalar", cf, cf, 0.5, None, ALU.mult)

    def ada_tile(m, i, t):
        b = m % 2
        for k in range(8):
            o = i * 1024 + k * 128
            p_ = mm(bank[b][:, 0:2], WR[:, o:o + 128], cf[:, 2 * k:2 * k + 2],
                    k == 0, k == 7, w=[t, cv, bank_free[b]] if k == 0 else (), inc=k == 7)
        W["raw_free"][i] = [p_]
        bank_free[b] = V("tensor_scalar", mod[:, m, :], bank[b][:, 0:2], pr("b_ada", m), None, ALU.add, w=[p_])

    t_h = [dve.t, act.t]

    def stream_g():
        tiles = [(I["w_in"][m], 8) for m in range(60)] + [(I["w_ada"][m], -8) for m in range(16)]
        for m, w in enumerate(stream(tiles)):
            if m >= 60:
                ada_tile(m - 60, *w[1])
                yield
                continue
            i = m % 2
            dst = cqv[:, m * T:(m + 1) * T] if m < 6 else stg[:, i * T:(i + 1) * T]
            es = []
            for h in range(2):
                yield from gemm_steps(w, 8, xs(T), (h * 512, h * 512 + 512), h, xk=hx if m == 0 else None)
                d = dst[:, h * 512:h * 512 + 512]
                ww = [W["gemm"]] + (t_h if m < 6 else [s_st[i].t])
                if m < 28:
                    e = evac(d, bank[h][:, :], ww)
                else:
                    e = A(d, bank[h][:, :], AF.Tanh, scale=0.5, w=ww)
                bank_free[h] = e
                es.append(e)
                yield
            if m < 6:
                u_tok[m] = es
            elif m < 28:
                u_tok[m] = [P.dma(sp, D_u[m - 6], dst, s_st[i], es)]
            else:
                u_tok[m] = [P.dma(sp, D_g[m - 28], dst, s_st[i], es)]

    def pull(table, ms):
        was, P.filling = P.filling, True
        while any(m not in table for m in ms):
            next(P.filler)
        P.filling = was

    def need(*ms):
        pull(u_tok, ms)
        return [t for m in ms for t in u_tok[m]]

    B_S = ((2, 3), (4, 5))
    B_T, B_O = 6, 7
    gbank = {}

    def bw(b, t):
        bank_free[b] = t
        return t

    def small_mm2(banks, parts, w=()):
        out = []
        for h in range(2):
            ps = parts(h)
            for n, (l, rr) in enumerate(ps):
                t = mm(bank[banks[h]][:, :] if l.shape[-1] == 128 else bank[banks[h]][0:l.shape[-1], :],
                       l, rr, n == 0, n == len(ps) - 1,
                       w=[*w, bank_free[banks[h]]] if n == 0 else (), inc=n == len(ps) - 1)
            out.append(t)
        return out

    def mixer_mla(c):
        vN = c("vN", 8 * 512)
        cs = c("cs", 2 * T)
        rp = c("rp", 2 * T)
        uq = c("uq", 4 * 384)
        ukv = ac2
        PT = c("PT", 8 * 512)
        uqr, vw = PT[:, 0:1536], PT[:, 1536:2560]
        cosT, sinT = cs[:, 0:T], cs[:, T:2 * T]
        yt = acq
        tA, tB = PT[:, 2560:3584], yt
        posr = vN[:, 0:T].bitcast(I32)
        P.dma(pool, uq, I["w_uq"][:, 0:1536], s_m[0])
        P.dma(pool, ukv, I["w_ukv"][:, 0:1024], s_m[1])
        P.dma(pool, uqr, I["w_uq"][:, 1536:3072], s_m[4])
        P.dma(pool, vw, I["w_ukv"][:, 1024:2048], s_m[5])
        P.dma(pool, posr[0:1, :], I["positions"], s_m[2])
        P.dma(pool, D_dt, cqv[32:40, 5 * T:6 * T], s_m[3], need(5))
        V("tensor_copy", tA[0:1, :], posr[0:1, :], w=[s_m[2].t])
        for h in range(2):
            t = mm(bank[2 + h][:, :], ones[0:1, :], tA[0:1, h * 512:h * 512 + 512], True, True,
                   w=[dve.t, bank_free[2 + h]], inc=True)
            v = V("tensor_scalar", tB[:, h * 512:h * 512 + 512], bank[2 + h][:, :], cn("inv"), None, ALU.mult, w=[t])
            bw(2 + h, v)
        V("tensor_scalar", cosT, tB, 1.0 / (2 * np.pi), 12582912.0, ALU.mult, ALU.add)
        V("tensor_scalar", cosT, cosT, -12582912.0, None, ALU.add)
        for cc in (6.28125, 0.0019350051879882812, 3.019916050561733e-07):
            V("scalar_tensor_tensor", tB, cosT, -cc, tB, ALU.mult, ALU.add)
        V("tensor_scalar", tB, tB, 3.1415925, -3.1415925, ALU.min, ALU.max)
        A(sinT, tB, AF.Sin, w=[dve.t])
        A(cosT, tB, AF.Sin, scale=0.5, w=[dve.t])
        V("tensor_scalar", sinT, sinT, cn("sgn"), None, ALU.mult, w=[act.t])
        V("tensor_tensor", cosT, cosT, cosT, ALU.mult)
        V("tensor_scalar", cosT, cosT, -2.0, 1.0, ALU.mult, ALU.add)
        yield
        cq = [cqv[:, j * T:(j + 1) * T] for j in range(3)]
        ckv = [cqv[:, j * T:(j + 1) * T] for j in range(3, 5)]
        krdt = cqv[:, 5 * T:6 * T]
        for seg, D, g in ((cq, 384, "q_norm"), (ckv, 256, "kv_norm")):
            for j, s in enumerate(seg):
                if j == 0:
                    t = A(tA, s, AF.Square, w=[dve.t, *need(0, 1, 2, 3, 4, 5)])
                else:
                    a = A(tB, s, AF.Square, w=[dve.t])
                    t = V("tensor_tensor", tA, tA, tB, ALU.add, w=[a])
            t = rstd_tail(tA, tB, D, T, (2, 3), t)
            for j, s in enumerate(seg):
                nt = V("scalar_tensor_tensor", s, s, pr(g, j), tB, ALU.mult, ALU.mult, w=[t])
            yield
        for g in range(2):
            for n, c0_ in enumerate((g, 2 + g)):
                ts = small_mm2(B_S[n], lambda h: [(uqr[:, c0_ * 384 + k * 128:c0_ * 384 + k * 128 + 128],
                                                   cq[k][:, h * 512:h * 512 + 512]) for k in range(3)],
                               w=[nt, s_m[4].t])
                for h in range(2):
                    hs = slice(h * 512, h * 512 + 512)
                    tab = (cosT, sinT)[n]
                    dst = (rp[:, g * T:(g + 1) * T], tA)[n]
                    bw(B_S[n][h], V("tensor_tensor", dst[:, hs], bank[B_S[n][h]][:, :], tab[:, hs], ALU.mult,
                                    w=[ts[h]]))
            V("tensor_tensor", rp[:, g * T:(g + 1) * T], rp[:, g * T:(g + 1) * T], tA, ALU.add)
            yield
        kr = krdt
        V("tensor_tensor", tA[64:96, :], krdt[0:32, :], cosT[0:32, :], ALU.mult)
        V("tensor_tensor", kr[64:96, :], krdt[64:96, :], sinT[64:96, :], ALU.mult)
        V("tensor_tensor", kr[64:96, :], kr[64:96, :], tA[64:96, :], ALU.add)
        for tc in range(8):
            b = B_S[tc % 2][0]
            for k in range(2):
                t = mm(bank[b][:, :], ckv[k][:, tc * 128:tc * 128 + 128], vw[:, k * 512:512 + k * 512],
                       k == 0, k == 1, w=[nt, s_m[5].t, bank_free[b]] if k == 0 else (), inc=k == 1)
            bw(b, A(vN[:, tc * 512:tc * 512 + 512], bank[b][:, :], w=[t]))
            if tc % 4 == 3:
                yield
        tv = act.t
        qk = c("qk", 4 * T)
        Pm = cs
        st = c("st", 32)
        SC = 96.0 ** -0.5
        ts_ = [None, None]
        pv_t = None
        for i in range(4):
            q_, k_ = [qk[:, a * T:(a + 1) * T] for a in range(2)], [qk[:, (2 + a) * T:(3 + a) * T] for a in range(2)]
            for n, (dst, chunk, K, wt, src) in enumerate(((q_, uq[:, i * 384:(i + 1) * 384], 3, s_m[0], cq),
                                                          (k_, ukv[:, i * 256:(i + 1) * 256], 2, s_m[1], ckv))):
                ts = small_mm2(B_S[n], lambda h: [(chunk[:, k * 128:k * 128 + 128],
                                                   src[k][:, h * 512:h * 512 + 512]) for k in range(K)],
                               w=[nt, wt.t])
                for h in range(2):
                    hs = slice(h * 512, h * 512 + 512)
                    b = B_S[n][h]
                    A(dst[0][0:64, hs], bank[b][0:64, :], w=[ts[h], pv_t])
                    bw(b, A(dst[1][0:64, hs], bank[b][64:128, :]))
            for a in range(2):
                hh = 2 * i + a
                A(q_[a][64:96, :], rp[32 * (hh % 4):32 * (hh % 4) + 32, (hh // 4) * T:(hh // 4 + 1) * T], w=[dve.t, pv_t])
                A(k_[a][64:96, :], kr[64:96, :], w=[pv_t])
            qk_t = act.t
            yield
            units = [(a, qb) for a in range(2) for qb in range(8)]
            state = {}

            def s1(u):
                a, qb = units[u]
                n = (qb + 1) * 128
                bs = B_S[u % 2]
                for h in range(0, n, 512):
                    b = bs[h // 512]
                    m = min(512, n - h)
                    t = mm(bank[b][:, 0:m], q_[a][0:96, qb * 128:qb * 128 + 128], k_[a][0:96, h:h + m], True, True,
                           w=[qk_t, bank_free[b]], inc=True)
                db = bs[(n - 1) // 512]
                o = (n - 128) % 512
                V("tensor_tensor", bank[db][:, o:o + 128], bank[db][:, o:o + 128], cn("mneg"), ALU.add, w=[t])
                c4 = (u % 4) * 8
                for h in range(0, n, 512):
                    b = bs[h // 512]
                    m = min(512, n - h)
                    V("tensor_reduce", st[:, c4 + h // 512:c4 + h // 512 + 1], bank[b][:, 0:m], AX.X, ALU.max)
                if n > 512:
                    V("tensor_tensor", st[:, c4:c4 + 1], st[:, c4:c4 + 1], st[:, c4 + 1:c4 + 2], ALU.max)
                v = V("tensor_scalar", st[:, c4 + 2:c4 + 3], st[:, c4:c4 + 1], -SC, None, ALU.mult)
                p = Pm[:, (u % 2) * T:(u % 2) * T + n]
                for h in range(0, n, 512):
                    b = bs[h // 512]
                    m = min(512, n - h)
                    e = A(p[:, h:h + m], bank[b][:, 0:m], AF.Exp, bias=st[:, c4 + 2:c4 + 3], scale=SC,
                          accum_out=st[:, c4 + 3 + h // 512:c4 + 4 + h // 512], w=[v, state.get(("tr", u - 2)), pool.t])
                    bw(b, e)
                state[u] = e

            def s2(u):
                a, qb = units[u]
                n = (qb + 1) * 128
                c4 = (u % 4) * 8
                p = Pm[:, (u % 2) * T:(u % 2) * T + n]
                w = [state[u]]
                if n > 512:
                    V("tensor_tensor", st[:, c4 + 3:c4 + 4], st[:, c4 + 3:c4 + 4], st[:, c4 + 4:c4 + 5], ALU.add, w=w)
                v = V("reciprocal", st[:, c4 + 5:c4 + 6], st[:, c4 + 3:c4 + 4], w=w)
                g = V("tensor_scalar", p, p, st[:, c4 + 5:c4 + 6], None, ALU.mult, w=[v, *w])
                qh, ql = qb // 4, qb % 4
                for k0 in range(0, qb + 1, 4):
                    kn = min(4, qb + 1 - k0)
                    for k in range(k0, k0 + kn):
                        t = tr(bank[B_T][:, (k - k0) * 128:(k - k0) * 128 + 128], p[:, k * 128:k * 128 + 128], ident,
                               w=[g, bank_free[B_T]] if k == k0 else (), inc=k == k0 + kn - 1)
                    bw(B_T, A(PT[:, :].rearrange("p (k q) -> p k q", k=8)[:, k0:k0 + kn, ql * 128:ql * 128 + 128],
                              bank[B_T][:, 0:kn * 128].rearrange("p (k q) -> p k q", q=128),
                              w=[t, state.get("pv")]))
                state[("tr", u)] = t
                if ql == 3:
                    hh = 2 * i + a
                    kc = qb + 1
                    for k in range(kc):
                        o = max(0, (k - 4 * qh) * 128)
                        t = mm(bank[B_O][a * 64:a * 64 + 64, o:512], vN[:, k * 512 + hh * 64:k * 512 + hh * 64 + 64],
                               PT[:, k * 512 + o:k * 512 + 512], k == 0, k == kc - 1,
                               w=[act.t, tv, bank_free[B_O]] if k == 0 else (), inc=k == kc - 1)
                    state["pv"] = t
                    bw(B_O, V("tensor_copy", yt[a * 64:a * 64 + 64, qh * 512:qh * 512 + 512],
                              bank[B_O][a * 64:a * 64 + 64, :], w=[t, s_m[3].t]))

            s1(0)
            for u in range(16):
                if u + 1 < 16:
                    s1(u + 1)
                s2(u)
                if u % 2:
                    yield
            pv_t = state["pv"]
            P.dma(pool, D_y[i], yt, s_m[3], [dve.t])

    def log1p_exp(v, t1, t2, t3, out):
        A(t1, v, AF.Abs, w=[dve.t])
        A(t1, t1, AF.Exp, scale=-1.0)
        V("tensor_scalar", t2, t1, 2.0, None, ALU.add, w=[act.t])
        V("reciprocal", t2, t2)
        V("tensor_tensor", t1, t1, t2, ALU.mult)
        V("tensor_tensor", t2, t1, t1, ALU.mult)
        V("tensor_scalar", t3, t2, 1.0 / 17, None, ALU.mult)
        for k in (15, 13, 11, 9, 7, 5, 3):
            V("scalar_tensor_tensor", t3, t3, 1.0 / k, t2, ALU.add, ALU.mult)
        V("scalar_tensor_tensor", t3, t3, 1.0, t1, ALU.add, ALU.mult)
        V("tensor_scalar", t2, v, 0.0, None, ALU.max)
        return V("scalar_tensor_tensor", out, t3, 2.0, t2, ALU.mult, ALU.add)

    def conv(dst, raw, wt, bias):
        V("tensor_scalar", dst, raw[:, 3:3 + T], wt[:, 3:4], bias, ALU.mult, ALU.add)
        for k in range(3):
            t = V("scalar_tensor_tensor", dst, raw[:, k:k + T], wt[:, k:k + 1], dst, ALU.mult, ALU.add)
        return t

    def b3(a, n):
        return a.unsqueeze(2).broadcast_to([a.shape[0], a.shape[1], n])

    def mixer_ssd(c):
        xb = c("xb", 6 * T)
        xdt = c("xdt", 8 * 512)
        CB = c("CB", 2 * T)
        Hs = c("Hs", 8 * 256)
        Lb = c("Lb", 2 * T)
        Mb = c("Mb", 2 * T)
        Eb = c("Eb", T)
        raws = c("raws", 2 * 1028)
        bmN = c("bmN", 8 * 128)
        xd = c("xd", 512)
        hw = c("hw", 32)
        smal = c("smal", 64 * 4 + 32)
        dtN, acN, deN, la = (smal[:, i * 64:(i + 1) * 64] for i in range(4))
        eD = smal[:, 256:288]
        dt8, ac8, r8, sel8 = (Lb[0:8, 0:T], Lb[0:8, T:2 * T], Mb[0:8, 0:T], Mb[0:8, T:2 * T])
        acs_t = acq
        sel_t = ac2
        P.dma(pool, r8, I["scon"][0], s_m[0])
        P.dma(pool, sel_t[0:8, :], I["scon"][1], s_m[0])
        P.dma(pool, dt8, D_dt, s_m[1])
        for i in range(2):
            V("memset", raws[:, i * 1028:i * 1028 + 3], 0.0)
        mset = dve.t
        V("tensor_scalar", hw, par[:, PO["conv_w"][0]:PO["conv_w"][0] + 32], 0.5, None, ALU.mult)
        raw_t = [None, None]

        def load_raw(n, src, w=()):
            i = n % 2
            P.dma(pool, raws[:, i * 1028 + 3:i * 1028 + 3 + T], src, s_m[2 + i], [mset, raw_t[i], *w])

        load_raw(0, D_u[4], need(10))
        load_raw(1, D_u[5], need(11))
        V("tensor_scalar", dt8, dt8, par[0:8, PO["dt_bias"][0]:PO["dt_bias"][0] + 1], None, ALU.add, w=[s_m[1].t])
        log1p_exp(dt8, Eb[0:8, :], xdt[0:8, 0:T], xdt[0:8, T:2 * T], dt8)
        A(smal[0:8, 256:257], par[0:8, PO["a_log"][0]:PO["a_log"][0] + 1], AF.Exp)
        V("tensor_scalar", Eb[0:8, :], dt8, smal[0:8, 256:257], -1.0, ALU.mult, ALU.mult, w=[act.t])
        ta = V("tensor_tensor_scan", acs_t[0:8, :], r8, Eb[0:8, :], 0.0, ALU.mult, ALU.add, w=[s_m[0].t])
        yield
        for cc in range(8):
            tr(bank[6][:, cc * 8:cc * 8 + 8], dt8[:, cc * 128:cc * 128 + 128], ident[0:8, 0:8],
               w=[ta, bank_free[6]] if cc == 0 else ())
            t = tr(bank[6][:, 64 + cc * 8:72 + cc * 8], acs_t[0:8, cc * 128:cc * 128 + 128], ident[0:8, 0:8], inc=cc == 7)
        V("tensor_copy", dtN, bank[6][:, 0:64], w=[t])
        bw(6, V("tensor_copy", acN, bank[6][:, 64:128]))
        for h in range(8):
            t = mm(bank[7][:, h * 8:h * 8 + 8], sel_t[0:8, h * 128:h * 128 + 128], acs_t[0:8, 127::128], True, True,
                   w=[bank_free[7], s_m[0].t] if h == 0 else (), inc=h == 7)
        v = V("tensor_tensor", deN.rearrange("p (c h) -> p c h", c=8), bank[7][:, 0:64].rearrange("p (h c) -> p c h", h=8),
              acN.rearrange("p (c h) -> p c h", c=8), ALU.subtract, w=[t])
        A(deN, deN, AF.Exp, w=[v])
        for g in range(2):
            A(eD[g * 64:g * 64 + 64, :].rearrange("p (c r) -> p c r", c=8),
              bank[7][g * 64:g * 64 + 64, g * 32:g * 32 + 32].rearrange("p (r c) -> p c r", c=8), AF.Exp)
        bw(7, act.t)
        order = (4, 5, 0, 1, 2, 3)
        for n, j in enumerate(order):
            i = n % 2
            dst = xb[:, j * T:(j + 1) * T]
            dve.wait([s_m[2 + i].t])
            raw_t[i] = conv(dst, raws[:, i * 1028:(i + 1) * 1028], hw[:, 4 * j:4 * j + 4], hw[:, 24 + j:25 + j])
            if n + 2 < 6:
                jj = order[n + 2]
                load_raw(n + 2, D_u[jj], need(6 + jj))
            a = A(Eb, dst, AF.Tanh, w=[dve.t])
            V("scalar_tensor_tensor", dst, Eb, 1.0, dst, ALU.add, ALU.mult, w=[a])
            yield
        bm, cm = xb[:, 4 * T:5 * T], xb[:, 5 * T:6 * T]
        txb = dve.t
        for cc in range(8):
            b = 6 + cc % 2
            t = tr(bank[b][:, 0:128], bm[:, cc * 128:cc * 128 + 128], ident, w=[txb, bank_free[b]], inc=True)
            bw(b, A(bmN[:, cc * 128:cc * 128 + 128], bank[b][:, 0:128], w=[t]))
            b = B_S[0][cc % 2]
            for j in range(4):
                t = tr(bank[b][:, j * 128:j * 128 + 128], xb[:, j * T + cc * 128:j * T + cc * 128 + 128], ident,
                       w=[bank_free[b]] if j == 0 else (), inc=j == 3)
            bw(b, V("tensor_tensor", xdt[:, cc * 512:cc * 512 + 512].rearrange("p (h e) -> p h e", h=8),
                    bank[b][:, :].rearrange("p (h e) -> p h e", h=8), b3(dtN[:, cc * 8:cc * 8 + 8], 64), ALU.mult, w=[t]))
        yield
        for g in range(2):
            for cc in range(8):
                b = B_S[1][cc // 4]
                t = mm(bank[b][:, (cc % 4) * 128:(cc % 4) * 128 + 128], bm[g * 64:g * 64 + 64, cc * 128:cc * 128 + 128],
                       cm[g * 64:g * 64 + 64, cc * 128:cc * 128 + 128], True, True, w=[bank_free[b]] if cc % 4 == 0 else (),
                       inc=cc % 4 == 3)
                if cc % 4 == 3:
                    o = g * T + (cc // 4) * 512
                    bw(b, V("tensor_tensor", CB[:, o:o + 512].rearrange("p (c l) -> p c l", c=4),
                            bank[b][:, :].rearrange("p (c l) -> p c l", c=4),
                            cn("mle").unsqueeze(1).broadcast_to([128, 4, 128]), ALU.mult, w=[t]))
        th = V("memset", Hs[:, 0:256], 0.0)
        xt = None
        for cc in range(7):
            b = 6 + cc % 2
            v = V("tensor_tensor", xd.rearrange("p (h e) -> p h e", h=8),
                  xdt[:, cc * 512:cc * 512 + 512].rearrange("p (h e) -> p h e", h=8), b3(deN[:, cc * 8:cc * 8 + 8], 64),
                  ALU.mult, w=[act.t, xt])
            for g in range(2):
                xt = mm(bank[b][g * 64:g * 64 + 64, 0:256], bmN[:, cc * 128 + g * 64:cc * 128 + g * 64 + 64],
                        xd[:, g * 256:g * 256 + 256], True, True, w=[v, bank_free[b]] if g == 0 else (), inc=g == 1)
            V("tensor_tensor", Hs[:, (cc + 1) * 256:(cc + 2) * 256].rearrange("p (r e) -> p r e", r=4),
              Hs[:, cc * 256:(cc + 1) * 256].rearrange("p (r e) -> p r e", r=4), b3(eD[:, cc * 4:cc * 4 + 4], 64), ALU.mult)
            th = bw(b, V("tensor_tensor", Hs[:, (cc + 1) * 256:(cc + 2) * 256], Hs[:, (cc + 1) * 256:(cc + 2) * 256],
                         bank[b][:, 0:256], ALU.add, w=[xt]))
            if cc % 3 == 2:
                yield
        Mt = [None, None]

        def pre(h):
            g, i = h // 4, h % 2
            Lh, Mh = Lb[:, i * T:(i + 1) * T], Mb[:, i * T:(i + 1) * T]
            for k in range(2):
                b = B_S[0][k]
                t = mm(bank[b][:, :], sel_t[0:8, h * 128:h * 128 + 128], acs_t[0:8, k * 512:k * 512 + 512], True, True,
                       w=[bank_free[b]], inc=True)
                for cc in range(4 * k, 4 * k + 4):
                    V("tensor_scalar", Lh[:, cc * 128:cc * 128 + 128], bank[b][:, (cc % 4) * 128:(cc % 4) * 128 + 128],
                      acN[:, cc * 8 + h:cc * 8 + h + 1], 0.0, ALU.subtract, ALU.min, w=[t, Mt[i]])
                e = A(Mh[g * 64:g * 64 + 64, k * 512:k * 512 + 512], bank[b][g * 64:g * 64 + 64, :], AF.Exp, w=[dve.t, Mt[i]])
                bw(b, V("tensor_tensor", Mh[g * 64:g * 64 + 64, k * 512:k * 512 + 512],
                        Mh[g * 64:g * 64 + 64, k * 512:k * 512 + 512],
                        cm[g * 64:g * 64 + 64, k * 512:k * 512 + 512], ALU.mult, w=[e]))
            a = A(Lh, Lh, AF.Exp, w=[dve.t])
            return V("tensor_tensor", Lh, Lh, CB[:, g * T:(g + 1) * T], ALU.mult, w=[a])

        nxt = pre(0)
        for h in range(8):
            g, i, r_, j = h // 4, h % 2, h % 4, h // 2
            cur = nxt
            if h + 1 < 8:
                nxt = pre(h + 1)
            Lh, Mh = Lb[:, i * T:(i + 1) * T], Mb[:, i * T:(i + 1) * T]
            o = (h % 2) * 64
            for cc in range(8):
                b = B_S[1][cc // 4]
                reg = bank[b][o:o + 64, (cc % 4) * 128:(cc % 4) * 128 + 128]
                mm(reg, xdt[:, cc * 512 + h * 64:cc * 512 + h * 64 + 64], Lh[:, cc * 128:cc * 128 + 128], True, False,
                   w=[cur, bank_free[b], th])
                Mt[i] = mm(reg, Hs[g * 64:g * 64 + 64, cc * 256 + r_ * 64:cc * 256 + r_ * 64 + 64],
                           Mh[g * 64:g * 64 + 64, cc * 128:cc * 128 + 128], False, True, inc=cc == 7)
            if i:
                for k in range(2):
                    xj = xb[:, j * T + k * 512:j * T + k * 512 + 512]
                    bw(B_S[1][k], V("scalar_tensor_tensor", xj, xj, pr("ssd_d", j), bank[B_S[1][k]][:, :], ALU.mult,
                                    ALU.add, w=[Mt[i]]))
            yield
        zt = None
        for j in range(4):
            z_, xj = CB[:, (j % 2) * T:(j % 2) * T + T], xb[:, j * T:(j + 1) * T]
            t = P.dma(pool, z_, D_u[14 + j], s_m[4 + j % 2], [dve.t, *need(20 + j)])
            a = A(Lb[:, 0:T], z_, AF.Tanh, scale=0.5, w=[t, dve.t])
            V("scalar_tensor_tensor", z_, Lb[:, 0:T], 1.0, z_, ALU.add, ALU.mult, w=[a])
            V("scalar_tensor_tensor", xj, xj, 0.5, z_, ALU.mult, ALU.mult)
            if j == 0:
                t = A(Mb[:, 0:T], xj, AF.Square, w=[dve.t])
            else:
                a = A(Lb[:, T:2 * T], xj, AF.Square, w=[dve.t])
                t = V("tensor_tensor", Mb[:, 0:T], Mb[:, 0:T], Lb[:, T:2 * T], ALU.add, w=[a])
        t = rstd_tail(Mb[:, 0:T], Eb, 512, T, (2, 3), t)
        for j in range(4):
            xj = xb[:, j * T:(j + 1) * T]
            v = V("scalar_tensor_tensor", xj, xj, pr("ssd_norm", j), Eb, ALU.mult, ALU.mult, w=[t])
            P.dma(pool, D_y[8 + j], xj, s_m[j], [v])
        yield

    def mixer_lru(c):
        av, mv, uv = c("av", 4 * T), c("mv", 4 * T), c("uv", 4 * T)
        raws = c("raws2", 2 * 1028)
        t1, t2 = c("lt1", T), c("lt2", T)
        wai = c("wai", 8 * 128)
        hb = c("hb", 24)
        P.dma(pool, wai, I["w_lru"], s_m[5])
        for i in range(2):
            V("memset", raws[:, i * 1028:i * 1028 + 3], 0.0)
        mset = dve.t
        raw_t = [None, None]

        def load_raw(n, j):
            P.dma(pool, raws[:, (n % 2) * 1028 + 3:(n % 2) * 1028 + 3 + T], D_u[6 + j], s_m[n % 2],
                  [mset, raw_t[n % 2], *need(12 + j)])

        load_raw(0, 0)
        load_raw(1, 1)
        V("tensor_scalar", hb[:, 0:8], par[:, PO["b_a"][0]:PO["b_a"][0] + 8], 0.5, None, ALU.mult)
        V("tensor_scalar", hb[:, 8:12], pr("lam", 0, 4), -1.0, None, ALU.mult)
        log1p_exp(hb[:, 8:12], hb[:, 12:16], hb[:, 16:20], hb[:, 20:24], hb[:, 8:12])
        V("tensor_scalar", hb[:, 8:12], hb[:, 8:12], -4.0, None, ALU.mult)
        for j in range(4):
            a_, m_, u_ = av[:, j * T:(j + 1) * T], mv[:, j * T:(j + 1) * T], uv[:, j * T:(j + 1) * T]
            dve.wait([s_m[j % 2].t])
            xct = raw_t[j % 2] = conv(u_, raws[:, (j % 2) * 1028:(j % 2 + 1) * 1028], pr("lconv_w", 4 * j, 4), pr("lconv_b", j))
            if j + 2 < 4:
                load_raw(j + 2, j + 2)
            for s, dst in enumerate((t1, t2)):
                for k in range(2):
                    b = B_S[s][k]
                    t = mm(bank[b][:, :], wai[:, (s * 4 + j) * 128:(s * 4 + j + 1) * 128], u_[:, k * 512:k * 512 + 512],
                           True, True, w=[xct, bank_free[b], s_m[5].t], inc=True)
                    bw(b, A(dst[:, k * 512:k * 512 + 512], bank[b][:, :], AF.Tanh, scale=0.5, bias=hb[:, 4 * s + j:4 * s + j + 1],
                            w=[t, xct]))
            ta = act.t
            V("tensor_scalar", t1, t1, 1.0, hb[:, 8 + j:9 + j], ALU.add, ALU.mult, w=[ta])
            v = V("tensor_scalar", t2, t2, 0.5, 0.5, ALU.mult, ALU.add)
            A(a_, t1, AF.Exp, w=[v])
            a = A(m_, t1, AF.Tanh, scale=-1.0)
            V("tensor_tensor", u_, u_, t2, ALU.mult, w=[pe.t])
            V("tensor_tensor", t2, a_, a_, ALU.mult, w=[a])
            V("scalar_tensor_tensor", m_, t2, 1.0, m_, ALU.add, ALU.mult)
            yield
        for j in range(4):
            a = A(mv[:, j * T:(j + 1) * T], mv[:, j * T:(j + 1) * T], AF.Sqrt, w=[dve.t])
        for j in range(4):
            m_ = mv[:, j * T:(j + 1) * T]
            V("tensor_tensor", uv[:, j * T:(j + 1) * T], uv[:, j * T:(j + 1) * T], m_, ALU.mult, w=[a])
            V("tensor_tensor_scan", m_, av[:, j * T:(j + 1) * T], uv[:, j * T:(j + 1) * T], 0.0, ALU.mult, ALU.add)
            yield
        for j in range(4):
            g_, m_ = av[:, j * T:(j + 1) * T], mv[:, j * T:(j + 1) * T]
            t = P.dma(pool, g_, D_u[18 + j], s_m[2 + j % 2], [dve.t, *need(24 + j)])
            a = A(t1, g_, AF.Square, w=[t, dve.t])
            V("tensor_scalar", t1, t1, 0.044715, 1.0, ALU.mult, ALU.add, w=[a])
            v = V("tensor_tensor", t1, t1, g_, ALU.mult)
            a = A(t1, t1, AF.Tanh, scale=0.7978845608028654, w=[v])
            V("scalar_tensor_tensor", t1, t1, 1.0, g_, ALU.add, ALU.mult, w=[a])
            v = V("scalar_tensor_tensor", m_, m_, 0.5, t1, ALU.mult, ALU.mult)
            P.dma(pool, D_y[12 + j], m_, s_m[4], [v, s_m[4].t])
            yield

    def mixer_pool(c):
        raw = c("praw", 2 * 1040)
        tmp = c("ptmp", 2 * 1040)
        wp = c("wp", 512)
        yo = c("yo", 2 * T)
        P.dma(pool, wp, I["w_pool"], s_m[5])
        for a in (raw, tmp):
            for i in range(2):
                V("memset", a[:, i * 1040:i * 1040 + 16], 0.0)
        mset = dve.t
        used = [None, None]
        for g in range(4):
            i = g % 2
            rw = raw[:, i * 1040:(i + 1) * 1040]
            t = P.dma(pool, rw[:, 16:], D_u[10 + g], s_m[i], [mset, used[i], *need(16 + g)])
            cur, n = rw, 0
            for st_ in (1, 2, 4, 8)[:g + 1]:
                nx = tmp[:, n * 1040:(n + 1) * 1040]
                V("tensor_tensor", nx[:, 16:], cur[:, 16:], cur[:, 16 - st_:1040 - st_], ALU.add, w=[t, pe.t])
                cur, n = nx, 1 - n
            wd = 2 << g
            d = tmp[:, n * 1040:(n + 1) * 1040]
            V("tensor_tensor", d[:, 16:32], cur[:, 16:32], cn("icnt", 16 * g, 16 * g + 16), ALU.mult)
            V("tensor_tensor", d[:, 16:32], d[:, 16:32], rw[:, 16:32], ALU.subtract)
            v = used[i] = V("scalar_tensor_tensor", d[:, 32:], cur[:, 32:], 1.0 / wd, rw[:, 32:], ALU.mult, ALU.subtract)
            for k in range(2):
                b = B_S[g % 2][k]
                t = mm(bank[b][:, :], wp[:, g * 128:g * 128 + 128], d[:, 16 + k * 512:16 + k * 512 + 512], True, True,
                       w=[v, bank_free[b], s_m[5].t], inc=True)
                a = bw(b, A(yo[:, i * T + k * 512:i * T + k * 512 + 512], bank[b][:, :], scale=pr("pool_scale", g),
                            w=[t, s_m[2 + i].t]))
            P.dma(pool, D_y[4 + g], yo[:, i * T:(i + 1) * T], s_m[2 + i], [a])
            yield

    def run_m():
        for f in (mixer_mla, mixer_ssd, mixer_lru, mixer_pool):
            c = ExitStack()
            yield from f(Region(c))
            P.barrier()
            c.close()
            if f is mixer_mla:
                cM.close()

    P.filler = stream_g()
    pull(u_tok, range(6))
    for _ in run_m():
        pass
    if P.filler is not None:
        rest, P.filler = P.filler, None
        for _ in rest:
            pass
    P.barrier()
    nb = [0]

    qf = [None] * 4
    nq = [0]

    def q_slot():
        i = nq[0] = (nq[0] + 1) % 4
        return i, stg[:, i * 512:i * 512 + 512]

    def sum_sq(m, h, acc=None, scale=1.0):
        acc = acq if acc is None else acc
        rs, ac = res[:, m * T + h * 512:m * T + h * 512 + 512], acc[:, h * 512:h * 512 + 512]
        if m == 0:
            return A(ac, rs, AF.Square, scale=scale, w=[dve.t, pe.t])
        i, q = q_slot()
        a = A(q, rs, AF.Square, scale=scale, w=[dve.t, qf[i]])
        qf[i] = V("tensor_tensor", ac, ac, q, ALU.add, w=[a])

    def take_bank():
        b = nb[0] % 8
        nb[0] += 1
        return b

    c2 = ExitStack()
    mrg = sb("mrg", 8 * T, c=c2)
    yr = sb("yr", 2 * T, c=c2)
    gr = sb("gr", 3 * T, c=c2)
    y_pe = [None] * 4

    yt_ = [None] * 2

    def dma_y(b, j):
        i = j % 2
        yt_[i] = P.dma(pool, yr[:, i * T:(i + 1) * T], D_y[4 * b + j], s_m[i], [dve.t, act.t])

    def split_y(b, j):
        i = j % 2
        o = ((b % 2) * 4 + j) * T
        return split_x((o, o + T), yr[:, i * T:(i + 1) * T], w=[yt_[i], y_pe[b - 2] if b > 1 else None])

    tiles = [(I["w_branch"][b * 8 + m], 4) for b in range(4) for m in range(8)]
    gt, gfree = [None] * 3, [None] * 3

    def load_g(n):
        b, m = divmod(n, 8)
        gt[n % 3] = P.dma(sp, gr[:, (n % 3) * T:(n % 3 + 1) * T], D_g[n], s_ld[n % 3], [gfree[n % 3]])

    load_g(0)
    load_g(1)
    for j in range(2):
        dma_y(0, j)
    for j in range(4):
        yv = split_y(0, j)
        if j < 2:
            dma_y(0, j + 2)
    for n, w in enumerate(stream(tiles)):
        b, m = divmod(n, 8)
        if n + 2 < 32:
            load_g(n + 2)
        if b < 3 and m in (1, 3, 5):
            for j in range(2):
                if m > 1:
                    yn = split_y(b + 1, m - 3 + j)
                if m < 5:
                    dma_y(b + 1, m - 1 + j)
        g_ = gr[:, (n % 3) * T:(n % 3 + 1) * T]
        for h in range(2):
            bk = take_bank()
            hs = slice(h * 512, h * 512 + 512)
            off = (b % 2) * 4 * T
            t = gemm(w, 4, lambda k, c_: (XH[:, off + k * T + c_[0]:off + k * T + c_[1]],
                                          XL[:, off + k * T + c_[0]:off + k * T + c_[1]]),
                     (h * 512, h * 512 + 512), bk, xw=[yv])
            dst = mrg[:, m * T + h * 512:m * T + h * 512 + 512]
            if b == 0:
                gfree[n % 3] = bw(bk, V("scalar_tensor_tensor", dst, g_[:, hs], 1.0, bank[bk][:, :], ALU.add, ALU.mult,
                                        w=[t, gt[n % 3]]))
            else:
                gfree[n % 3] = bw(bk, V("scalar_tensor_tensor", g_[:, hs], g_[:, hs], 1.0, bank[bk][:, :], ALU.add,
                                        ALU.mult, w=[t, gt[n % 3]]))
                gfree[n % 3] = V("tensor_tensor", dst, dst, g_[:, hs], ALU.add)
        if m == 7:
            y_pe[b] = t
            if b < 3:
                yv = yn
    xv = []
    for j in range(8):
        xv.append(split_x((j * T, (j + 1) * T), mrg[:, j * T:(j + 1) * T], w=[dve.t, W["gemm"]]))
    xt_ = [None] * 2
    for m in range(2):
        xt_[m] = P.dma(sp, yr[:, m * T:(m + 1) * T], I["xT"][m], s_x if m else s_ld[3], [dve.t])
    for m, w in enumerate(stream([(I["w_out"][m], 8) for m in range(8)])):
        for h in range(2):
            bk = take_bank()
            t = gemm(w, 8, xs(T), (h * 512, h * 512 + 512), bk, xk=xv)
            v = bw(bk, V("scalar_tensor_tensor", res[:, m * T + h * 512:m * T + h * 512 + 512], bank[bk][:, :], 0.5,
                         yr[:, (m % 2) * T + h * 512:(m % 2) * T + h * 512 + 512], ALU.mult, ALU.add,
                         w=[t, xt_[m % 2]]))
            sum_sq(m, h)
        if m + 2 < 8:
            xt_[m % 2] = P.dma(sp, yr[:, (m % 2) * T:(m % 2 + 1) * T], I["xT"][m + 2], s_x if m % 2 else s_ld[3], [v])
    P.barrier()
    c2.close()

    def norm_x(gain):
        t = rstd_tail(acq, acq, 1024, T, (6, 7), dve.t)
        out = []
        for j in range(8):
            for h in range(2):
                i, q = q_slot()
                v = V("scalar_tensor_tensor", q, res[:, j * T + h * 512:j * T + h * 512 + 512], pr(gain, j),
                      acq[:, h * 512:h * 512 + 512], ALU.mult, ALU.mult, w=[t, qf[i]])
                v = qf[i] = split_x((j * T + h * 512, j * T + h * 512 + 512), q, w=[v, W["gemm"]])
                if h:
                    out.append(v)
        return out

    xv = norm_x("g_mlp")
    c2 = ExitStack()
    FH, FL = sb("FH", 8 * T, F32R, c2), sb("FL", 8 * T, F32R, c2)

    def fx(o):
        return lambda k, c_: (FH[:, o + k * T + c_[0]:o + k * T + c_[1]], FL[:, o + k * T + c_[0]:o + k * T + c_[1]])

    tiles = []
    for f in range(9):
        group = [(I["w_ff1"][4 * f + j], 8) for j in range(4)] if f < 8 else []
        group += [(I["w_ff2"][8 * (f - 1) + m], 4) for m in range(8)] if f else []
        for g_ in group:
            tiles.append(g_)
    ws_ = stream(tiles)

    def ff_tile():
        return next(ws_)

    f_pe, f_v = [None] * 2, [None] * 2
    for f in range(9):
        if f < 8:
            o = (f % 2) * 4 * T
            for j in range(4):
                w = ff_tile()
                for h in range(2):
                    bk = take_bank()
                    t = gemm(w, 8, xs(T), (h * 512, h * 512 + 512), bk, xk=xv)
                    i, q = q_slot()
                    bw(bk, A(q, bank[bk][:, :], AF.Relu, w=[t, qf[i], f_pe[f % 2]]))
                    v = V("tensor_tensor", q, q, q, ALU.mult, w=[act.t])
                    s_ = slice(o + j * T + h * 512, o + j * T + h * 512 + 512)
                    a = A(FH[:, s_], q, w=[v])
                    qf[i] = f_v[f % 2] = V("tensor_tensor", FL[:, s_], q, FH[:, s_].bitcast(F32), ALU.subtract, w=[a])
        if f:
            o = ((f - 1) % 2) * 4 * T
            for m in range(8):
                w = ff_tile()
                for h in range(2):
                    bk = take_bank()
                    t = gemm(w, 4, fx(o), (h * 512, h * 512 + 512), bk, xw=[f_v[(f - 1) % 2]])
                    rs = res[:, m * T + h * 512:m * T + h * 512 + 512]
                    bw(bk, V("tensor_tensor", rs, rs, bank[bk][:, :], ALU.add, w=[t]))
                    if f == 8:
                        sum_sq(m, h)
            f_pe[(f - 1) % 2] = t
    next(ws_, None)
    for q in range(2):
        V("scalar_tensor_tensor", cs_[:, q * 8:q * 8 + 8], mod[:, 8:16, q], 1.0, pr("norm1", 0, 8), ALU.add, ALU.mult)
    P.barrier()
    c2.close()
    c2 = ExitStack()
    FH, FL = sb("PH", 2 * T, F32R, c2), sb("PL", 2 * T, F32R, c2)
    pT = sb("pT", 2 * T, c=c2)
    tp = P.dma(sp, pT, I["pT"], s_x)
    xv = norm_x("g_ple")
    for h in range(4):
        hs = slice(h * 512, h * 512 + 512)
        a = A(FH[:, hs], pT[:, hs], w=[tp])
        pv = V("tensor_tensor", FL[:, hs], pT[:, hs], FH[:, hs].bitcast(F32), ALU.subtract, w=[a])
    ws = stream([x_ for m in range(8) for x_ in ((I["w_ple_gate"][m], 8), (I["w_ple"][m], 2))])
    for m in range(8):
        w = next(ws)
        bs = [take_bank(), take_bank()]
        ts = [gemm(w, 8, xs(T), (h * 512, h * 512 + 512), bs[h], xk=xv) for h in range(2)]
        w = next(ws)
        for h in range(2):
            i, q = q_slot()
            a = bw(bs[h], A(q, bank[bs[h]][:, :], AF.Tanh, scale=0.5, w=[ts[h], qf[i]]))
            bk = take_bank()
            t = gemm(w, 2, fx(0), (h * 512, h * 512 + 512), bk, xw=[pv])
            bw(bk, V("scalar_tensor_tensor", q, q, 1.0, bank[bk][:, :], ALU.add, ALU.mult, w=[a, t]))
            rs = res[:, m * T + h * 512:m * T + h * 512 + 512]
            qf[i] = V("scalar_tensor_tensor", rs, q, 0.5, rs, ALU.mult, ALU.add)
            sum_sq(m, h)
            sum_sq(m, h, ac2, pr("g_final", m))
    next(ws, None)
    P.barrier()
    c2.close()
    c1.close()

    S = 1280
    c1 = ExitStack()
    XH, XL = sb("XH2", 8 * S, F32R, c1), sb("XL2", 8 * S, F32R, c1)
    stg2 = sb("stg2", 2 * S, c=c1)
    con2[0] = sb("con2", NCON - NCON1, c=c1)
    P.dma(sp, con2[0], I["con"][:, NCON1:], s_par)
    c2 = ExitStack()
    hb_ = sb("hb_", 2 * T, c=c2)
    cx = sb("cx", 8 * 256, c=c2)
    rc_ = sb("rc_", 768, c=c2)
    P.dma(sp, cx, I["ctxT"], s_x)
    t = rstd_tail(acq, acq, 1024, T, (6, 7), dve.t)
    V("tensor_tensor", hb_[:, 0:T], acq, acq, ALU.mult, w=[t])
    for h in range(2):
        hs = slice(h * 512, h * 512 + 512)
        t2 = mm(bank[6 + h][:, :], ones, ac2[:, hs], True, True, w=[bank_free[6 + h]], inc=True)
        bw(6 + h, V("scalar_tensor_tensor", ac2[:, hs], bank[6 + h][:, :], 1.0 / 1024, hb_[:, hs], ALU.mult, ALU.mult, w=[t2]))
    V("tensor_scalar", ac2, ac2, EPS, None, ALU.add)
    V("reciprocal", ac2, ac2)
    t2 = A(ac2, ac2, AF.Sqrt, w=[dve.t])
    hxk = []
    hf = [None] * 2
    for j in range(8):
        xj = res[:, j * T:(j + 1) * T]
        v = V("scalar_tensor_tensor", xj, xj, pr("g_final", j), acq, ALU.mult, ALU.mult, w=[t])
        P.dma(sp, D_xb[j], xj, s_ld[j % 4], [v, s_ld[j % 4].t])
        h_ = hb_[:, (j % 2) * T:(j % 2 + 1) * T]
        v = V("scalar_tensor_tensor", h_, xj, cs_[:, j:j + 1], ac2, ALU.mult, ALU.mult, w=[t2, hf[j % 2]])
        a = A(h_, h_, AF.Identity, bias=mod[:, j, 0:1], w=[v])
        v = hf[j % 2] = split_x((j * S, j * S + T), h_, w=[a])
        hxk.append(v)
    for j in range(8):
        cj = cx[:, j * 256:(j + 1) * 256]
        if j == 0:
            t = A(rc_[:, 0:256], cj, AF.Square, w=[s_x.t])
        else:
            a = A(rc_[:, 256:512], cj, AF.Square, w=[dve.t])
            t = V("tensor_tensor", rc_[:, 0:256], rc_[:, 0:256], rc_[:, 256:512], ALU.add, w=[a])
    t = rstd_tail(rc_[:, 0:256], rc_[:, 512:768], 1024, 256, (4, 5), t)
    for j in range(8):
        cj = cx[:, j * 256:(j + 1) * 256]
        V("scalar_tensor_tensor", cj, cj, cs_[:, 8 + j:9 + j], rc_[:, 512:768], ALU.mult, ALU.mult, w=[t])
        v = V("tensor_scalar", cj, cj, mod[:, j, 1:2], None, ALU.add)
        hcx = split_x((j * S + T, j * S + S), cj, w=[v])

    def rms_chunks(chunks, n, sqt, acc_, r_, w):
        for j, cj in enumerate(chunks):
            if j == 0:
                t = A(acc_, cj, AF.Square, w=[dve.t, pe.t, *w(j)])
            else:
                a = A(sqt, cj, AF.Square, w=[dve.t, *w(j)])
                t = V("tensor_tensor", acc_, acc_, sqt, ALU.add, w=[a])
        return rstd_tail(acc_, r_, 1024, n, (4, 5), t)

    v_tok = {}

    def stream_g2():
        tiles = [(I["w_in2"][m], 8) for m in range(29)] + [(I["w_ada"][m], -8) for m in range(16, 48)]
        for m, w in enumerate(stream(tiles)):
            if m >= 29:
                ada_tile(m - 13, *w[1])
                yield
                continue
            i = m % 2
            dst = stg2[:, i * S:(i + 1) * S]
            es = []
            segs = [(0, 512), (512, 1024)] + ([(1024, 1280)] if m < 7 or 13 <= m < 21 else [])
            for h, (a, b_) in enumerate(segs):
                bk = h % 2
                yield from gemm_steps(w, 8, xs(S), (a, b_), bk, xk=hxk if m == 0 and h < 2 else None,
                                      xw=[hcx] if h == 2 else [])
                e = bank_free[bk] = evac(dst[:, a:b_], bank[bk][:, 0:b_ - a], [W["gemm"], s_st[i].t])
                es.append(e)
                yield
            n = segs[-1][1]
            v_tok[m] = P.dma(sp, D_v[m][:, 0:n], dst[:, 0:n], s_st[i], es)

    def needv(*ms):
        pull(v_tok, ms)
        return [v_tok[m] for m in ms]

    def head_out(h, o_, rr, sq_, gt_, gain, mean, gidx, slot, dslot):
        if mean:
            for k in range(2):
                b = B_S[1][k]
                hs = slice(k * 512, k * 512 + 512)
                t = mm(bank[b][:, :], ones, o_[:, hs], True, True, w=[dve.t, bank_free[b]], inc=True)
                bw(b, V("scalar_tensor_tensor", o_[:, hs], bank[b][:, :], -1.0 / 128, o_[:, hs], ALU.mult, ALU.add, w=[t]))
        t = A(sq_, o_, AF.Square, w=[dve.t, pe.t])
        t = rstd_tail(sq_, rr, 128, T, B_S[1], t)
        V("scalar_tensor_tensor", o_, o_, gain, rr, ALU.mult, ALU.mult, w=[t])
        t = P.dma(pool, gt_, D_v[gidx][:, 0:T], slot, [dve.t, *needv(gidx)])
        a = A(sq_, gt_, AF.Tanh, scale=0.5, w=[t, dve.t])
        V("scalar_tensor_tensor", sq_, sq_, 1.0, gt_, ALU.add, ALU.mult, w=[a])
        v = V("scalar_tensor_tensor", o_, o_, 0.5, sq_, ALU.mult, ALU.mult)
        P.dma(pool, D_o[h], o_, dslot, [v])

    def v3(a, n=128):
        return a.rearrange("p (c i) -> p c i", i=n)

    def mixer_gla(c):
        q_, k_ = c("gq", T), c("gk", S)
        vN = c("gvN", 10 * 256)
        b_ = c("gb", S)
        qJ = c("gqJ", 4 * T)
        kp, ke, keN = c("gkp", T), c("gke", S), c("gkeN", S)
        qe = c("gqe", T)
        Ss = c("gSs", 8 * 128)
        ST = c("gST", 2 * 512)
        o2 = aq2
        gw = stg[:, 0:512]
        sm = stg[:, 512:560]
        P.dma(pool, gw[0:32, :], I["gla_gw"], s_m[0])
        for rc in range(2):
            P.dma(pool, q_, D_v[7 + rc][:, 0:T], s_m[1], [dve.t, pe.t, act.t, *needv(7, 8)])
            P.dma(pool, k_, D_v[1 + rc], s_m[2], [dve.t, *needv(1, 2)])
            for a in range(2):
                t = P.dma(pool, ke, D_v[3 + 2 * rc + a], s_m[3], [dve.t, pe.t, *needv(3, 4, 5, 6)])
                for c0_ in range(0, 10, 4):
                    b = 6 + (c0_ // 4) % 2
                    n = min(4, 10 - c0_)
                    for cc in range(c0_, c0_ + n):
                        p_ = tr(bank[b][:, (cc - c0_) * 128:(cc - c0_) * 128 + 128], ke[:, cc * 128:cc * 128 + 128], ident,
                                w=[t, bank_free[b]] if cc == c0_ else (), inc=cc == c0_ + n - 1)
                    bw(b, A(vN.rearrange("p (c x) -> p c x", c=10)[:, c0_:c0_ + n, a * 128:a * 128 + 128],
                            v3(bank[b][:, 0:n * 128]), w=[p_]))
            yield
            V("tensor_scalar", q_, q_, 0.125, None, ALU.mult, w=[s_m[1].t])
            for d in range(2):
                gz = qJ[0:32, 0:S]
                tz = P.dma(pool, gz, D_v[0][0:32, :], s_m[4], [dve.t, pe.t, act.t, *needv(0)])
                for h, (a0, a1) in enumerate(((0, 512), (512, 1024), (1024, 1280))):
                    b = (2, 3, 4)[h]
                    p_ = mm(bank[b][:, 0:a1 - a0], gw[0:32, (2 * d + rc) * 128:(2 * d + rc) * 128 + 128],
                            gz[:, a0:a1], True, True, w=[tz, s_m[0].t, bank_free[b]], inc=True)
                    bw(b, A(b_[:, a0:a1], bank[b][:, 0:a1 - a0], AF.Identity, bias=pr("gate_b", 2 * d + rc), w=[p_, dve.t]))
                A(ke, b_, AF.Abs)
                A(ke, ke, AF.Exp, scale=-1.0)
                a = A(ke, ke, AF.Ln, bias=1.0)
                V("tensor_scalar", b_, b_, 0.0, None, ALU.min, w=[a])
                V("tensor_tensor", b_, b_, ke, ALU.subtract)
                V("tensor_scalar", keN, b_, 1.0 / 16, None, ALU.mult, w=[pe.t])
                for cc in range(10):
                    lo, hi = cc * 128, cc * 128 + 128
                    sl = slice(lo, hi) if d == 0 else slice(hi - 1, lo - 1 if lo else None, -1)
                    V("tensor_tensor_scan", b_[:, sl], keN[:, sl], keN[:, sl], 0.0, ALU.add, ALU.bypass)
                yield
                eo = 127 if d == 0 else 0
                ro = 15 if d == 0 else 16
                b3_ = v3(b_)
                bend = b3_[:, :, eo:eo + 1]
                V("tensor_tensor", v3(ke), b3_, bend.broadcast_to([128, 10, 128]), ALU.subtract)
                a = A(ke, ke, AF.Exp, scale=-1.0, w=[dve.t])
                aend = sm[:, d * 16:d * 16 + 10]
                A(aend.unsqueeze(2), bend, AF.Exp)
                v = V("tensor_tensor", ke, ke, k_, ALU.mult, w=[a, s_m[2].t])
                for c0_ in range(0, 10, 4):
                    b = 6 + (c0_ // 4) % 2
                    n = min(4, 10 - c0_)
                    for cc in range(c0_, c0_ + n):
                        p_ = tr(bank[b][:, (cc - c0_) * 128:(cc - c0_) * 128 + 128], ke[:, cc * 128:cc * 128 + 128], ident,
                                w=[v, bank_free[b]] if cc == c0_ else (), inc=cc == c0_ + n - 1)
                    bw(b, A(keN[:, c0_ * 128:(c0_ + n) * 128], bank[b][:, 0:n * 128], w=[p_, dve.t]))
                for J in range(4):
                    V("tensor_tensor", v3(qJ[:, J * T:(J + 1) * T]), b3_[:, 0:8, :],
                      b3_[:, 0:8, 32 * J + ro:32 * J + ro + 1].broadcast_to([128, 8, 128]), ALU.subtract, w=[pe.t])
                    V("tensor_scalar", qJ[:, J * T:(J + 1) * T], qJ[:, J * T:(J + 1) * T], 40.0, None, ALU.min)
                a = A(qJ, qJ, AF.Exp, w=[dve.t])
                kb = b_[:, 0:T].rearrange("p (m i) -> p m i", i=32)
                V("tensor_tensor", kp.rearrange("p (m i) -> p m i", i=32), kb,
                  kb[:, :, ro:ro + 1].broadcast_to([128, 32, 32]), ALU.subtract, w=[pe.t])
                v = V("tensor_scalar", kp, kp, -40.0, None, ALU.max)
                A(kp, kp, AF.Exp, scale=-1.0, w=[v])
                a2 = A(qe, b_[:, 0:T], AF.Exp, w=[v, pe.t])
                V("tensor_tensor", qJ.rearrange("p (j t) -> p j t", j=4), qJ.rearrange("p (j t) -> p j t", j=4),
                  q_.unsqueeze(1).broadcast_to([128, 4, T]), ALU.mult, w=[a])
                V("tensor_tensor", kp, kp, k_[:, 0:T], ALU.mult, w=[a2])
                vq = V("tensor_tensor", qe, qe, q_, ALU.mult)
                yield
                order = ([8, 9] + list(range(7))) if d == 0 else ([9, 8] + list(range(7, 0, -1)))
                nxt_of = {8: 9, 9: 0} if d == 0 else {9: 8, 8: 7}
                tmpS = ST[:, 0:128]
                tmpS2 = ST[:, 128:256]
                prev = None
                for n, cc in enumerate(order):
                    b = 6 + n % 2
                    for a in range(2):
                        p_ = mm(bank[b][a * 64:a * 64 + 64, 0:128], keN[:, cc * 128 + a * 64:cc * 128 + a * 64 + 64],
                                vN[:, cc * 256 + a * 128:cc * 256 + a * 128 + 128], True, True,
                                w=[act.t, bank_free[b]] if a == 0 else (), inc=a == 1)
                    if n == 0:
                        dstS = tmpS
                    elif n == 1:
                        i0 = 0 if d == 0 else 7
                        dstS = Ss[:, i0 * 128:i0 * 128 + 128]
                    else:
                        i0 = cc + 1 if d == 0 else cc - 1
                        dstS = Ss[:, i0 * 128:i0 * 128 + 128]
                    if n == 0:
                        bw(b, V("tensor_copy", dstS, bank[b][:, 0:128], w=[p_]))
                    else:
                        bw(b, V("scalar_tensor_tensor", dstS, prev, aend[:, cc:cc + 1], bank[b][:, 0:128], ALU.mult,
                                ALU.add, w=[p_]))
                    prev = dstS
                tS = dve.t
                yield
                mask = cn("mle") if d == 0 else cn("mge")
                stt_ = [None, None]
                for a in range(2):
                    rs = slice(a * 64, a * 64 + 64)
                    for k in range(2):
                        b = B_S[0][k]
                        for cc in range(4 * k, 4 * k + 4):
                            for J in range(4):
                                p_ = mm(bank[b][32 * J:32 * J + 32, (cc % 4) * 128:(cc % 4) * 128 + 128],
                                        kp[rs, cc * 128 + 32 * J:cc * 128 + 32 * J + 32],
                                        qJ[rs, J * T + cc * 128:J * T + cc * 128 + 128], True, True,
                                        w=[vq, bank_free[b]] if cc % 4 == 0 and J == 0 else (), inc=cc % 4 == 3 and J == 3)
                        sv = bw(b, V("tensor_tensor", v3(ST[:, k * 512:k * 512 + 512]), v3(bank[b][:, :]),
                                     mask.unsqueeze(1).broadcast_to([128, 4, 128]), ALU.mult, w=[p_, stt_[k]]))
                        b = B_S[1][k]
                        for cc in range(4 * k, 4 * k + 4):
                            reg = bank[b][:, (cc % 4) * 128:(cc % 4) * 128 + 128]
                            mm(reg, vN[:, cc * 256 + a * 128:cc * 256 + a * 128 + 128],
                               ST[:, cc * 128:cc * 128 + 128], True, False, w=[sv, bank_free[b], tS])
                            p_ = mm(reg, Ss[rs, cc * 128:cc * 128 + 128], qe[rs, cc * 128:cc * 128 + 128], False, True,
                                    inc=cc % 4 == 3)
                        stt_[k] = p_
                        dst = o2[:, a * T + k * 512:a * T + k * 512 + 512]
                        if d == 0:
                            bw(b, V("tensor_copy", dst, bank[b][:, :], w=[p_, s_m[5].t]))
                        else:
                            bw(b, V("tensor_tensor", dst, dst, bank[b][:, :], ALU.add, w=[p_]))
                    yield
            for a in range(2):
                h = 2 * rc + a
                head_out(h, o2[:, a * T:(a + 1) * T], kp, qe, ke[:, 0:T], pr("gla_norm", h), False, 9 + h, s_m[3], s_m[5])
                pool.wait([s_m[5].t])
                yield

    def mixer_ret(c):
        q_, k_ = c("rq", T), c("rk", S)
        vN, kN = c("rvN", S), c("rkN", S)
        keN = [c(f"rke{d}", S) for d in range(2)]
        qe = [c(f"rqe{d}", T) for d in range(2)]
        Ss = [c(f"rSs{d}", T) for d in range(2)]
        rC, rS = c("rC", T), c("rS", T)
        tm = c("rtm", S)
        o_, ST = acq, ac2
        Dm = c("rDm", 128 * 4)
        lg = c("rlg", 48)
        P.dma(pool, rC, I["rope2"][0], s_m[0])
        P.dma(pool, rS, I["rope2"][1], s_m[0])
        V("tensor_scalar", lg[:, 0:8], pr("ret_logit", 0, 8), -1.0, None, ALU.mult)
        log1p_exp(lg[:, 0:8], lg[:, 8:16], lg[:, 16:24], lg[:, 24:32], lg[:, 0:8])
        V("tensor_scalar", lg[:, 0:8], lg[:, 0:8], -1.0, None, ALU.mult)
        A(lg[:, 8:16], lg[:, 0:8], AF.Exp, scale=128.0, w=[dve.t])
        for d, nm in enumerate(("colf", "colb")):
            V("tensor_scalar", lg[:, 16 + 4 * d:20 + 4 * d], lg[:, 4 * d:4 * d + 4], cn(nm), None, ALU.mult)
        A(lg[:, 16:24], lg[:, 16:24], AF.Exp, w=[dve.t])
        for h in range(4):
            tq = P.dma(pool, q_, D_v[21 + h][:, 0:T], s_m[1], [dve.t, pe.t, act.t, *needv(21 + h)])
            tk = P.dma(pool, k_, D_v[13 + h], s_m[2], [dve.t, pe.t, *needv(13 + h)])
            tv = P.dma(pool, tm, D_v[17 + h], s_m[3], [dve.t, pe.t, *needv(17 + h)])
            pool.wait([tq, tk, tv])

            def turn(src, dst, w):
                for c0_ in range(0, 10, 4):
                    b = 6 + (c0_ // 4) % 2
                    n = min(4, 10 - c0_)
                    for cc in range(c0_, c0_ + n):
                        p_ = tr(bank[b][:, (cc - c0_) * 128:(cc - c0_) * 128 + 128], src[:, cc * 128:cc * 128 + 128], ident,
                                w=[w, bank_free[b]] if cc == c0_ else (), inc=cc == c0_ + n - 1)
                    bw(b, A(dst[:, c0_ * 128:(c0_ + n) * 128], bank[b][:, 0:n * 128], w=[p_, dve.t]))

            turn(tm, vN, tv)
            for d, (rel, mk) in enumerate((("relf", "mle"), ("relb", "mge"))):
                a = A(Dm[:, d * 128:d * 128 + 128], cn(rel), AF.Exp, scale=lg[:, 4 * d + h:4 * d + h + 1], w=[dve.t])
                V("tensor_tensor", Dm[:, d * 128:d * 128 + 128], Dm[:, d * 128:d * 128 + 128], cn(mk), ALU.mult, w=[a])
                A(Dm[:, 256 + d * 128:384 + d * 128], cn("posf" if d == 0 else "posb"), AF.Exp,
                  scale=lg[:, 4 * d + h:4 * d + h + 1])
            V("tensor_tensor", Dm[:, 0:128], Dm[:, 0:128], Dm[:, 128:256], ALU.add)
            sw = tm[:, 0:T]
            dve.wait([s_m[0].t, tq, tk, pe.t])
            for x_, sc in ((q_, 1.0), (k_, 128.0 ** -0.5)):
                xx = x_[:, 0:T]
                V("tensor_tensor", sw[0:64, :], xx[64:128, :], rS[64:128, :], ALU.mult)
                V("tensor_tensor", sw[64:128, :], xx[0:64, :], rS[0:64, :], ALU.mult)
                V("tensor_tensor", xx, xx, rC, ALU.mult)
                V("tensor_tensor", xx, xx, sw, ALU.add)
            v = V("tensor_scalar", k_, k_, 128.0 ** -0.5, None, ALU.mult)
            turn(k_, kN, v)
            yield
            for d in range(2):
                V("tensor_scalar", keN[d], kN, lg[:, 16 + 4 * d + h:17 + 4 * d + h], None, ALU.mult, w=[act.t, pe.t])
                V("tensor_tensor", v3(qe[d]), v3(q_), Dm[:, 256 + d * 128:384 + d * 128].unsqueeze(1).broadcast_to([128, 8, 128]),
                  ALU.mult)
            vk = dve.t
            orders = ([8, 9] + list(range(7)), [9, 8] + list(range(7, 0, -1)))
            prev = [None, None]
            for n in range(9):
                for d in range(2):
                    cc = orders[d][n]
                    b = 6 + d
                    p_ = mm(bank[b][:, 0:128], keN[d][:, cc * 128:cc * 128 + 128], vN[:, cc * 128:cc * 128 + 128],
                            True, True, w=[vk, bank_free[b]], inc=True)
                    if n == 0:
                        dstS = ST[:, d * 128:d * 128 + 128]
                        bw(b, V("tensor_copy", dstS, bank[b][:, 0:128], w=[p_]))
                    else:
                        i0 = (0 if d == 0 else 7) if n == 1 else (cc + 1 if d == 0 else cc - 1)
                        dstS = Ss[d][:, i0 * 128:i0 * 128 + 128]
                        bw(b, V("scalar_tensor_tensor", dstS, prev[d], lg[:, 8 + 4 * d + h:9 + 4 * d + h],
                                bank[b][:, 0:128], ALU.mult, ALU.add, w=[p_]))
                    prev[d] = dstS
                if n % 3 == 2:
                    yield
            for k in range(2):
                b = B_S[0][k]
                for cc in range(4 * k, 4 * k + 4):
                    p_ = mm(bank[b][:, (cc % 4) * 128:(cc % 4) * 128 + 128], k_[:, cc * 128:cc * 128 + 128],
                            q_[:, cc * 128:cc * 128 + 128], True, True, w=[bank_free[b]] if cc % 4 == 0 else (),
                            inc=cc % 4 == 3)
                sv = bw(b, V("tensor_tensor", v3(ST[:, k * 512:k * 512 + 512]), v3(bank[b][:, :]),
                             Dm[:, 0:128].unsqueeze(1).broadcast_to([128, 4, 128]), ALU.mult, w=[p_]))
                b = B_S[1][k]
                for cc in range(4 * k, 4 * k + 4):
                    reg = bank[b][:, (cc % 4) * 128:(cc % 4) * 128 + 128]
                    cs3 = slice(cc * 128, cc * 128 + 128)
                    mm(reg, vN[:, cs3], ST[:, cs3], True, False, w=[sv, bank_free[b]])
                    mm(reg, Ss[0][:, cs3], qe[0][:, cs3], False, False)
                    p_ = mm(reg, Ss[1][:, cs3], qe[1][:, cs3], False, True, inc=cc % 4 == 3)
                bw(b, V("tensor_copy", o_[:, k * 512:k * 512 + 512], bank[b][:, :], w=[p_, s_m[5].t]))
            yield
            head_out(4 + h, o_, qe[0], qe[1], tm[:, 0:T], pr("ret_norm", h), True, 25 + h, s_m[4], s_m[5])
            yield

    P.filler = stream_g2()
    pull(v_tok, range(3))
    P.barrier()
    c2.close()
    for f in (mixer_gla, mixer_ret):
        c = ExitStack()
        for _ in f(Region(c)):
            pass
        P.barrier()
        c.close()
    if P.filler is not None:
        rest, P.filler = P.filler, None
        for _ in rest:
            pass
    P.barrier()

    V("scalar_tensor_tensor", cs_[:, 16:24], mod[:, 32:40, 0], 1.0, pr("norm2", 0, 8), ALU.add, ALU.mult)
    v = V("tensor_copy", cf[:, 0:8], mod[:, 40:48, 0])
    p_ = tr(bank[0][0:8, 0:128], cf[:, 0:8], ident, w=[v, bank_free[0]], inc=True)
    v = bank_free[0] = V("tensor_copy", stg2[0:8, 2304:2432], bank[0][0:8, 0:128], w=[p_])
    P.dma(sp, D_m5.rearrange("o (a b) -> (o a) b", a=8), stg2[0:8, 2304:2432], s_x, [v])
    c2 = ExitStack()
    orw, wr_ = stg2[:, 0:2 * T], stg2[:, 2 * T:2 * T + 128]
    h2 = sb("h2", 8 * T, c=c2)
    for j in range(8):
        P.dma(sp, res[:, j * T:(j + 1) * T], D_xb[j], s_ld[0])
    P.dma(sp, wr_, I["w_router"], s_ld[1])
    xv = []
    for j in range(8):
        i = j % 2
        P.dma(pool, h2[:, j * T:(j + 1) * T], D_o[j], s_m[j % 4], [s_m[j % 4].t])
    for j in range(8):
        xv.append(split_x((j * T, (j + 1) * T), h2[:, j * T:(j + 1) * T], w=[Tok(s_m[j % 4].sem, s_m[j % 4].val - (16 if j < 4 else 0), s_m[j % 4].at)]))
    for m, w in enumerate(stream([(I["w_out2"][m], 8) for m in range(8)])):
        for h in range(2):
            bk = take_bank()
            t = gemm(w, 8, xs(T), (h * 512, h * 512 + 512), bk, xk=xv)
            rs = res[:, m * T + h * 512:m * T + h * 512 + 512]
            bw(bk, V("scalar_tensor_tensor", rs, bank[bk][:, :], mod[:, 16 + m, 0:1], rs, ALU.mult, ALU.add,
                     w=[t, s_ld[0].t]))
            sum_sq(m, h)
    xt2 = dve.t

    def turn_out(src, dram, w, slots):
        for tc in range(8):
            i = tc % 2
            for q in range(2):
                bk = take_bank()
                for j in range(4):
                    p_ = tr(bank[bk][:, j * 128:j * 128 + 128],
                            src[:, (4 * q + j) * T + tc * 128:(4 * q + j) * T + tc * 128 + 128], ident,
                            w=[w, bank_free[bk]] if j == 0 else (), inc=j == 3)
                e = bw(bk, A(orw[:, i * T + q * 512:i * T + q * 512 + 512], bank[bk][:, :], w=[p_, slots[i].t]))
            P.dma(sp, dram[tc * 128:tc * 128 + 128, :], orw[:, i * T:(i + 1) * T], slots[i], [e])

    t = rstd_tail(acq, acq, 1024, T, (6, 7), dve.t)
    for j in range(8):
        xj, hj = res[:, j * T:(j + 1) * T], h2[:, j * T:(j + 1) * T]
        v = V("scalar_tensor_tensor", hj, xj, cs_[:, 16 + j:17 + j], acq, ALU.mult, ALU.mult, w=[t])
        hv = A(hj, hj, AF.Identity, bias=mod[:, 24 + j, 0:1], w=[v])
    b = take_bank()
    for tc in range(8):
        for k in range(8):
            p_ = mm(bank[b][:, tc * 16:tc * 16 + 16], h2[:, k * T + tc * 128:k * T + tc * 128 + 128],
                    wr_[:, k * 16:k * 16 + 16], k == 0, k == 7, w=[hv, bank_free[b], s_ld[1].t] if k == 0 else (),
                    inc=k == 7 and tc == 7)
    af = stg[:, 0:128]
    l3 = bank[b][:, 0:128].rearrange("p (c e) -> p c e", e=16)
    a3 = af.rearrange("p (c e) -> p c e", e=16)
    mx = stg[:, 128:136]
    V("tensor_reduce", mx, l3, AX.X, ALU.max, w=[p_, act.t])
    bw(b, V("tensor_tensor", a3, l3, b3(mx, 16), ALU.subtract))
    a = A(af, af, AF.Exp, w=[dve.t])
    V("tensor_reduce", mx, a3, AX.X, ALU.add, w=[a])
    V("reciprocal", mx, mx)
    v = V("tensor_tensor", a3, a3, b3(mx, 16), ALU.mult)
    affT = stg[0:16, T:2 * T]
    for k in range(2):
        b = take_bank()
        for j in range(4):
            p_ = tr(bank[b][0:16, j * 128:j * 128 + 128], af[:, (4 * k + j) * 16:(4 * k + j) * 16 + 16], ident,
                    w=[v, bank_free[b]] if j == 0 else (), inc=j == 3)
        bw(b, V("tensor_copy", affT[:, k * 512:k * 512 + 512], bank[b][0:16, :], w=[p_]))
    turn_out(h2, D_h, hv, s_ld[2:4])
    turn_out(res, D_acc, xt2, s_ld[2:4])
    gv_, ix, ixf = stg[0:16, 256:384], stg[0:16, 384:512].bitcast(U32), stg[0:16, 512:640]
    for rd in range(16):
        g8 = gv_[:, rd * 8:rd * 8 + 8]
        V("max", g8, affT)
        V("max_index", ix[:, rd * 8:rd * 8 + 8], g8, affT)
        V("match_replace", affT, g8, affT, -1.0)
    V("tensor_copy", ixf, ix)
    P.barrier()
    c2.close()
    c1.close()

    c1 = ExitStack()
    gT = sb("gT", 16, c=c1)
    iT = sb("iT", 16, U32, c=c1)
    fnw, m5 = acq, ac2
    XEH, XEL = WH, WL
    HH, HL = sb("HH", 2 * 1408, F32R, c1), sb("HL", 2 * 1408, F32R, c1)
    NR, NS = 5, 3
    er = sb("ER", 2 * 3072, c=c1)
    ER = [er[:, i * 3072:(i + 1) * 3072] for i in range(2)] + [res[:, i * 3072:(i + 1) * 3072] for i in range(2)] + [WR]
    EH, EL = sb("EH", NS * 3072, F32R, c1), sb("EL", NS * 3072, F32R, c1)
    xe = res[:, 6 * T:8 * T]
    ye = stg[:, T:2 * T]
    hN = stg[:, 0:2 * 384]
    s_e = [P.slot(f"e{i}") for i in range(NR)]
    s_g = [P.slot(f"g{i}") for i in range(2)]
    s_acc, s_mf = P.slot("acc"), P.slot("mf")
    b = take_bank()
    tr(bank[b][:, 0:16], gv_, ident[0:16, 0:16], w=[bank_free[b]])
    p_ = tr(bank[b][:, 16:32], ixf, ident[0:16, 0:16], inc=True)
    V("tensor_copy", gT, bank[b][:, 0:16], w=[p_])
    tix = bw(b, V("tensor_copy", iT, bank[b][:, 16:32]))

    pieces = []
    for e in range(16):
        for q in range(4):
            n = 384 if q < 3 else 256
            pieces += [(e, 0, q, 8 * n), (e, 1, q, 8 * n)]
        pieces += [(e, 2, q, 11 * 256) for q in range(4)]
    p_raw, p_spl = [None] * NR, [None] * NS
    p_tok = {}

    def e_load(n):
        e, kind, q, size = pieces[n]
        i = n % NR
        src = I[("wg", "wu", "wd")[kind]][e]
        off = q * 8 * 384 if kind < 2 else q * 11 * 256
        p_tok[n] = P.dma(sp, ER[i][:, 0:size], src[:, off:off + size], s_e[i], [*(p_raw[i] or [])])

    def e_split(n):
        size = pieces[n][3]
        i, j = n % NR, n % NS
        raw = ER[i][:, 0:size]
        hi, lo = (t_[:, j * 3072:j * 3072 + size] for t_ in (EH, EL))
        cut = size // 2
        for c_ in (slice(0, cut), slice(cut, size)):
            a = A(hi[:, c_], raw[:, c_], w=[p_tok[n], p_spl[j]])
            v = V("tensor_tensor", lo[:, c_], raw[:, c_], hi[:, c_].bitcast(F32), ALU.subtract, w=[a])
        p_raw[i] = [a, v]
        return v

    for n in range(NR - 1):
        e_load(n)
    t = P.dma(act, fnw[:, :], I["fnorm"].broadcast_to([128, 1024]), s_mf)
    P.dma(act, m5[:, :], D_m5.broadcast_to([128, 1024]), s_mf)

    g_tok, xe_free, x_tok = {}, [None] * 2, {}

    def gather(e):
        g_tok[e] = P.idma(s_g[e % 2], [tix, xe_free[e % 2]], out=xe[:, (e % 2) * 1024:(e % 2 + 1) * 1024],
                          out_offset=None, in_=D_h[:, :],
                          in_offset=bass.IndirectOffsetOnAxis(ap=iT[:, e:e + 1], axis=0))

    xh_pe = [None] * 2

    def turn_x(e):
        i = e % 2
        for q in range(2):
            b = 6 + q
            for j in range(4):
                p_ = tr(bank[b][:, j * 128:j * 128 + 128],
                        xe[:, i * 1024 + (4 * q + j) * 128:i * 1024 + (4 * q + j) * 128 + 128], ident,
                        w=[g_tok[e], bank_free[b]] if j == 0 else (), inc=j == 3)
            s_ = slice(i * 1024 + q * 512, i * 1024 + q * 512 + 512)
            a = A(XEH[:, s_], bank[b][:, :], w=[p_, xh_pe[i]])
            v = bw(b, V("tensor_tensor", XEL[:, s_], bank[b][:, :], XEH[:, s_].bitcast(F32), ALU.subtract, w=[a]))
        xe_free[i] = p_
        x_tok[e] = v

    pend = []

    def egemm(n, b, col, width, K, L, ltok, at):
        j = n % NS
        for k in range(K):
            while pend and k == at:
                pend.pop(0)()
            lh, ll = L(k)
            rh = EH[:, j * 3072 + k * width:j * 3072 + (k + 1) * width]
            rl = EL[:, j * 3072 + k * width:j * 3072 + (k + 1) * width]
            mm(bank[b][:, col:col + width], lh, rh, k == 0, False, w=[*(ltok() if callable(ltok) else ltok), bank_free[b]] if k in (0, at) else ())
            mm(bank[b][:, col:col + width], lh, rl, False, False)
            p_ = mm(bank[b][:, col:col + width], ll, rh, False, k == K - 1, inc=k == K - 1)
        p_spl[j] = p_
        return p_

    gather(0)
    gather(1)
    turn_x(0)
    sp_tok = {0: e_split(0), 1: e_split(1)}
    hh_pe = [None] * 2
    hn_free = [None] * 2
    h_tok = [None]
    y_free = None
    NP_ = len(pieces)
    done = None
    for n in range(NP_):
        e, kind, q, size = pieces[n]
        if n + NR - 1 < NP_:
            e_load(n + NR - 1)
        if n + 2 < NP_:
            sp_tok[n + 2] = e_split(n + 2)
        i = e % 2
        if kind < 2:
            w_ = 384 if q < 3 else 256
            b = 2 * (q % 2) + kind
            t = egemm(n, b, 0, w_, 8, lambda k: (XEH[:, i * 1024 + k * 128:i * 1024 + k * 128 + 128],
                                                 XEL[:, i * 1024 + k * 128:i * 1024 + k * 128 + 128]),
                      [sp_tok[n], x_tok[e]], 4)
            if kind == 0:
                ta = t
            else:
                if q == 3:
                    xh_pe[i] = t
                hn = hN[:, (q % 2) * 384:(q % 2) * 384 + w_]
                a = A(hn, bank[b - 1][:, 0:w_], AF.Tanh, scale=0.5, w=[ta, hn_free[q % 2], dve.t])
                v = V("scalar_tensor_tensor", hn, hn, 1.0, bank[b - 1][:, 0:w_], ALU.add, ALU.mult, w=[a])
                bw(b - 1, v)
                v = bw(b, V("scalar_tensor_tensor", hn, hn, 0.5, bank[b][:, 0:w_], ALU.mult, ALU.mult, w=[t]))

                def turn_h(q=q, i=i, w_=w_, v=v, hn=hn):
                    bt = 4 + q % 2
                    for j in range(w_ // 128):
                        p_ = tr(bank[bt][:, j * 128:j * 128 + 128], hn[:, j * 128:j * 128 + 128], ident,
                                w=[v, bank_free[bt]] if j == 0 else (), inc=j == w_ // 128 - 1)
                    hn_free[q % 2] = p_
                    s_ = slice(i * 1408 + q * 384, i * 1408 + q * 384 + w_)
                    a = A(HH[:, s_], bank[bt][:, 0:w_], w=[p_, hh_pe[i]])
                    h_tok[0] = bw(bt, V("tensor_tensor", HL[:, s_], bank[bt][:, 0:w_], HH[:, s_].bitcast(F32),
                                        ALU.subtract, w=[a]))

                pend.append(turn_h)
        else:
            if q == 0 and e + 1 < 16:
                turn_x(e + 1)
                if e + 2 < 16:
                    gather(e + 2)
            b = 4 + q % 2
            t = egemm(n, b, 0, 256, 11, lambda k: (HH[:, i * 1408 + k * 128:i * 1408 + k * 128 + 128],
                                                   HL[:, i * 1408 + k * 128:i * 1408 + k * 128 + 128]),
                      lambda: [sp_tok[n], h_tok[0]], 4)
            if q == 3:
                hh_pe[i] = t
            v = bw(b, V("scalar_tensor_tensor", ye[:, q * 256:q * 256 + 256], bank[b][:, 0:256], gT[:, e:e + 1],
                        m5[:, q * 256:q * 256 + 256], ALU.mult, ALU.mult, w=[t, y_free, s_mf.t]))
            if q == 3:
                y_free = P.idma(s_acc, [v, s_acc.t], out=D_acc[:, :],
                                out_offset=bass.IndirectOffsetOnAxis(ap=iT[:, e:e + 1], axis=0),
                                in_=ye[:, :], in_offset=None, compute_op=ALU.add)
    fin = P.slot("fin")
    f_l = [P.slot(f"fl{i}") for i in range(4)]
    f_s = [P.slot(f"fs{i}") for i in range(4)]
    f_in = [s_acc.t, dve.t, act.t, pe.t]

    def row_load(tc):
        P.dma(sp, ER[tc % 4][:, 0:1024], D_acc[tc * 128:tc * 128 + 128, :], f_l[tc % 4], f_in)

    for tc in range(4):
        row_load(tc)
    for tc in range(8):
        i = tc % 4
        xr, yo = ER[i][:, 0:1024], ER[i][:, 1024:2048]
        ss = hN[:, i * 4:i * 4 + 1]
        a = A(yo, xr, AF.Square, accum_out=ss, w=[f_l[i].t, f_s[i].t])
        V("tensor_scalar", ss, ss, 1.0 / 1024, EPS, ALU.mult, ALU.add, w=[a])
        v = V("reciprocal", ss, ss)
        a = A(ss, ss, AF.Sqrt, w=[v])
        v = V("scalar_tensor_tensor", yo, xr, ss, fnw, ALU.mult, ALU.mult, w=[a, s_mf.t])
        P.dma(sp, out[tc * 128:tc * 128 + 128, :], yo, f_s[i], [v])
        if tc + 4 < 8:
            f_in = [v]
            row_load(tc + 4)
    sp.wait([s.t for s in P.slots])
    P.barrier()
    c1.close()

    block = ctx.enter_context(nc.Block())

    @block.tensor
    def _(e):
        pe.play(e)

    @block.scalar
    def _(e):
        act.play(e)

    @block.vector
    def _(e):
        dve.play(e)

    @block.gpsimd
    def _(e):
        pool.play(e)

    @block.sync
    def _(e):
        sp.play(e)

    ctx.close()


def chunks(w, cols):
    K = w.shape[0] // 128
    return w[:, cols].reshape(K, 128, -1).transpose(1, 0, 2)


def layout(x, **A):
    L = {}
    f = np.float32
    ar = np.arange
    L["xT"] = np.ascontiguousarray(x[0].T.reshape(8, 128, 1024))
    w = A["w_in"][0]
    pad = lambda *parts: np.concatenate(parts, 1)
    sw = np.r_[16:32, 0:16]
    kr = w[:, 640:672]
    z = lambda n: np.zeros((1024, n), f)
    krdt = np.concatenate([kr, w[:, 2464:2472], z(24), kr[:, sw], z(32)], 1)
    cols = [w[:, 0:640], krdt, w[:, 1696:2464], w[:, 2984:3496], w[:, 672:1184], w[:, 1184:1696],
            w[:, 2472:2984], w[:, 3496:7592]]
    w = np.concatenate(cols, 1)
    tile = lambda w: np.ascontiguousarray(
        w.reshape(w.shape[0] // 128, 128, w.shape[1] // 128, 128).transpose(2, 1, 0, 3)).reshape(
            w.shape[1] // 128, 128, -1)
    L["w_in"] = tile(w)
    uq = A["w_uq"][0].reshape(384, 8, 96)
    uq = np.concatenate([uq[:, :, :64].reshape(384, 512), uq[:, :, 64:].reshape(384, 256),
                         uq[:, :, 64:][:, :, sw].reshape(384, 256)], 1)
    L["w_uq"] = np.ascontiguousarray(tile(uq).transpose(1, 0, 2)).reshape(128, 8 * 384)
    ukv = A["w_ukv"][0].reshape(256, 8, 128)
    kn = tile(np.ascontiguousarray(ukv[:, :, :64]).reshape(256, 512)).transpose(1, 0, 2).reshape(128, 1024)
    vv = np.ascontiguousarray(ukv[:, :, 64:]).reshape(2, 128, 512).transpose(1, 0, 2).reshape(128, 1024)
    L["w_ukv"] = np.concatenate([kn, vv], 1)
    wl = np.zeros((2, 4, 128, 128), f)
    for s, n in enumerate(("lru_w_a", "lru_w_i")):
        for b in range(8):
            o = (b % 2) * 64
            wl[s, b // 2, o:o + 64, o:o + 64] = A[n][0, b]
    L["w_lru"] = np.ascontiguousarray(wl.reshape(8, 128, 128).transpose(1, 0, 2)).reshape(128, 1024)
    L["w_branch"] = np.concatenate([tile(A["w_branch"][0, b]) for b in range(4)])
    L["w_out"] = tile(A["w_out"][0])
    L["w_ff1"] = tile(A["w_ff1"][0])
    L["w_ff2"] = np.concatenate([tile(A["w_ff2"][0, q * 512:(q + 1) * 512]) for q in range(8)])
    L["w_ple_gate"] = tile(A["w_ple_gate"][0])
    L["w_ple"] = tile(A["w_ple"][0])
    L["pT"] = np.ascontiguousarray(A["p"][0, 0].T.reshape(2, 128, 1024).transpose(1, 0, 2)).reshape(128, 2048)
    L["w_ada"] = tile(A["w_ada_2"][0])
    L["fnorm"] = np.ascontiguousarray(A["final_norm_w_2"][None])
    L["ctxT"] = np.ascontiguousarray(A["ctx_2"][0].T.reshape(8, 128, 256).transpose(1, 0, 2)).reshape(128, 2048)
    w2 = A["w_in_2"][0]
    L["w_in2"] = tile(np.concatenate([w2[:, 1024:1056], np.zeros((1024, 96), f), w2[:, 256:512], w2[:, 512:1024],
                                      w2[:, 0:256], w2[:, 1056:1568], w2[:, 2080:2592], w2[:, 2592:3104],
                                      w2[:, 1568:2080], w2[:, 3104:3616]], 1))
    gw = np.zeros((32, 2, 256), f)
    for d in range(2):
        gw[16 * d:16 * d + 16, d] = A["gla_gate_w_2"][0, d]
    L["gla_gw"] = gw.reshape(32, 512)
    L["w_out2"] = tile(A["w_out_2"][0])
    L["w_router"] = np.ascontiguousarray(A["w_router_2"][0].reshape(8, 128, 16).transpose(1, 0, 2)).reshape(128, 128)
    row = np.broadcast_to(ar(16)[:, None], (16, 64)).reshape(-1).astype(f)
    cl = np.broadcast_to(ar(64)[None], (16, 64)).reshape(-1).astype(f)
    iv = (f(10000.0) ** (-ar(32, dtype=f) / f(32))).astype(f)
    ang = np.concatenate([iv[:, None] * row[None], iv[:, None] * cl[None]], 0).astype(f)
    L["rope2"] = np.stack([np.concatenate([np.cos(ang)] * 2), np.concatenate([np.sin(ang), -np.sin(ang)])]).astype(f)

    def cut(w, widths, K):
        w = w.reshape(16, K, 128, -1)
        out, at = [], 0
        for n in widths:
            out.append(w[:, :, :, at:at + n].transpose(0, 2, 1, 3).reshape(16, 128, K * n))
            at += n
        return np.concatenate(out, 2)

    L["wg"] = cut(A["w_exp_gate_2"][0], (384, 384, 384, 256), 8)
    L["wu"] = cut(A["w_exp_up_2"][0], (384, 384, 384, 256), 8)
    L["wd"] = cut(A["w_exp_down_2"][0], (256,) * 4, 11)
    L["w_pool"] = np.ascontiguousarray(A["w_pool"][0].transpose(1, 0, 2)).reshape(128, 512)
    L["positions"] = A["positions"]

    par = np.zeros((128, NPAR), f)

    def put(name, a):
        o, n = PO[name]
        par[:a.shape[0], o:o + n] = a

    col = lambda v: v.reshape(-1, 128).T
    put("g_mix", col(A["g_mix"][0]))
    put("q_norm", col(A["q_norm"][0]))
    put("kv_norm", col(A["kv_norm"][0]))
    put("pool_scale", col(A["pool_scale"][0]))
    put("conv_w", A["ssd_conv_w"][0].reshape(4, 6, 128).transpose(2, 1, 0).reshape(128, 24))
    put("conv_b", col(A["ssd_conv_b"][0]))
    put("ssd_norm", col(A["ssd_norm"][0]))
    put("ssd_d", col(np.repeat(A["ssd_d"][0], 64)))
    put("lconv_w", A["lru_conv_w"][0].reshape(4, 4, 128).transpose(2, 1, 0).reshape(128, 16))
    put("lconv_b", col(A["lru_conv_b"][0]))
    put("b_a", col(A["lru_b_a"][0]))
    put("b_i", col(A["lru_b_i"][0]))
    put("lam", col(A["lru_lambda"][0]))
    put("g_mlp", col(A["g_mlp"][0]))
    put("g_ple", col(A["g_ple"][0]))
    put("g_final", col(A["g_final"]))
    put("norm1", col(A["norm1_w_2"][0]))
    put("norm2", col(A["norm2_w_2"][0]))
    put("b_ada", col(A["b_ada_2"][0]))
    put("gate_b", col(A["gla_gate_b_2"][0].reshape(-1)))
    put("gla_norm", col(A["gla_norm_w_2"][0]))
    put("ret_norm", col(A["ret_norm_w_2"][0]))
    put("cc", np.stack([col(A["c_2"][0]), col(A["c_ctx_2"])], 2).reshape(128, 16))
    put("dt_bias", A["ssd_dt_bias"][0][:, None])
    put("a_log", A["ssd_a_log"][0][:, None])
    put("ret_logit", np.broadcast_to(A["ret_decay_logit_2"][0].reshape(1, 8), (128, 8)))
    L["par"] = par

    con = np.zeros((128, NCON), f)

    def putc(name, a):
        o, n = CO[name]
        con[:a.shape[0], o:o + n] = a

    p, q = ar(128)[:, None], ar(128)[None, :]
    putc("ident", np.eye(128, dtype=f))
    putc("ones", np.ones((128, 128), f))
    putc("mle", (p <= q).astype(f))
    putc("mge", (p >= q).astype(f))
    putc("mneg", np.where(q > p, f(-1e30), f(0)))
    inv = (f(1.0) / (f(10000.0) ** (ar(0, 32, 2, dtype=f) / f(32)))).astype(f)
    putc("inv", inv[ar(128) % 16][:, None])
    putc("sgn", np.where(ar(128) % 32 < 16, f(-1), f(1))[:, None])
    ic = np.concatenate([1.0 / np.minimum(ar(16) + 1, ww) for ww in (2, 4, 8, 16)])
    putc("icnt", np.broadcast_to(ic[None].astype(f), (128, 64)))
    putc("relf", np.maximum(q - p, 0).astype(f))
    putc("relb", np.maximum(p - q, 0).astype(f))
    putc("posf", np.broadcast_to((q + 1).astype(f), (128, 128)))
    putc("posb", np.broadcast_to((128 - q).astype(f), (128, 128)))
    putc("colf", (127 - p).astype(f))
    putc("colb", p.astype(f))
    s8 = np.zeros((8, 8, 128), f)
    s8[ar(8), ar(8)] = 1
    L["scon"] = np.stack([np.broadcast_to((ar(1024) % 128 != 0).astype(f)[None], (8, 1024)), s8.reshape(8, 1024)])
    L["con"] = con
    return L


def kernel(**inputs):
    import numpy as _np
    import concourse.bacc as _bacc
    from concourse import mybir as _mybir
    from concourse.bass_utils import run_bass_kernel_spmd as _run

    L = layout(**{k: _np.asarray(v) for k, v in inputs.items()})
    nc = _bacc.Bacc("TRN2", target_bir_lowering=False, num_devices=1)
    arrays, I = {}, {}
    for name, a in L.items():
        a = _np.ascontiguousarray(a)
        arrays[f"in_{name}_dram"] = a
        I[name] = nc.dram_tensor(f"in_{name}_dram", a.shape, _mybir.dt.from_np(a.dtype), kind="ExternalInput").ap()
    out = nc.dram_tensor("out_0_dram", (1024, 1024), F32, kind="ExternalOutput").ap()
    program(nc, I, out)
    r = _run(nc, [arrays], core_ids=[0])
    return r.results[0]["out_0_dram"].reshape(1, 1024, 1024)
```

```python
from contextlib import ExitStack

import numpy as np
import concourse.bass as bass
from concourse import mybir

F32 = mybir.dt.float32
F32R = mybir.dt.float32r
I32 = mybir.dt.int32
U32 = mybir.dt.uint32
ALU = mybir.AluOpType
AF = mybir.ActivationFunctionType
AX = mybir.AxisListType
EPS = 1e-6
T = 1024
H2 = 512

PAR = [("g_mix", 8), ("q_norm", 3), ("kv_norm", 2), ("pool_scale", 4), ("conv_w", 24), ("conv_b", 6),
       ("ssd_norm", 4), ("ssd_d", 4), ("lconv_w", 16), ("lconv_b", 4), ("b_a", 4), ("b_i", 4), ("lam", 4),
       ("g_mlp", 8), ("g_ple", 8), ("g_final", 8), ("norm1", 8), ("norm2", 8), ("b_ada", 48), ("gate_b", 4),
       ("gla_norm", 4), ("ret_norm", 4), ("cc", 16), ("dt_bias", 1), ("a_log", 1), ("ret_logit", 8)]
CON = [("ident", 128), ("ones", 128), ("mle", 128), ("mneg", 128), ("inv", 1), ("sgn", 1),
       ("icnt", 64), ("mge", 128), ("relf", 128), ("relb", 128), ("posf", 128), ("posb", 128), ("colf", 1), ("colb", 1)]


def offsets(table):
    out, at = {}, 0
    for name, n in table:
        out[name] = (at, n)
        at += n
    return out, at


PO, NPAR = offsets(PAR)
CO, NCON = offsets(CON)
NCON1 = CO["mge"][0]


class Tok:
    def __init__(self, sem, val, at=0.0):
        self.sem, self.val, self.at = sem, val, at


def width(ap):
    n = 1
    for x in ap.shape[1:]:
        n *= x
    return n


class Eng:

    def __init__(self, name, sem, prog):
        self.name, self.sem, self.n, self.list, self.seen = name, sem, 0, [], {}
        self.time, self.prog = 0.0, prog

    def wait(self, toks):
        for t in toks:
            if t is None:
                continue
            self.time = max(self.time, t.at + (0.1 if t.sem is not self.sem else 0.06))
            if self.seen.get(t.sem.name, 0) < t.val:
                self.seen[t.sem.name] = t.val
                self.list.append(("wait", t.sem, t.val))

    def put(self, method, args, kw, w=(), inc=True, dur=0.1):
        self.prog.fill_to(max([self.time] + [t.at for t in w if t is not None]))
        self.wait(w)
        self.time += dur
        if inc:
            self.n += 1
            self.last = self.time
        self.list.append(("op", method, args, kw, (self.sem, 1) if inc else None))
        return self.t

    @property
    def t(self):
        return Tok(self.sem, self.n, self.last) if self.n else None

    def play(self, eng):
        table = {"tensor_tensor": eng.tensor_tensor if self.name in ("dve", "pool") else None,
                 "wait_ge": eng.wait_ge, "dma_start": eng.dma_start}
        if self.name == "dve":
            table.update(tensor_scalar=eng.tensor_scalar, scalar_tensor_tensor=eng.scalar_tensor_tensor,
                         tensor_tensor_scan=eng.tensor_tensor_scan, tensor_copy=eng.tensor_copy,
                         memset=eng.memset, reciprocal=eng.reciprocal, tensor_reduce=eng.tensor_reduce,
                         max=eng.max, max_index=eng.max_index, match_replace=eng.match_replace)
        if self.name == "pool":
            table.update(tensor_scalar=eng.tensor_scalar, tensor_copy=eng.tensor_copy, memset=eng.memset,
                         indirect_dma_start=eng.indirect_dma_start)
        if self.name == "act":
            table.update(activation=eng.activation)
        if self.name == "pe":
            table.update(matmul=eng.matmul, transpose=eng.transpose)
        for item in self.list:
            if item[0] == "wait":
                eng.wait_ge(item[1], item[2])
            else:
                _, method, args, kw, inc = item
                ins = table[method](*args, **kw)
                if inc:
                    ins.then_inc(*inc)


class Slot:

    def __init__(self, sem):
        self.sem, self.val, self.at = sem, 0, 0.0

    def next(self, at):
        self.val += 16
        self.at = at
        return Tok(self.sem, self.val, at)

    @property
    def t(self):
        return Tok(self.sem, self.val, self.at) if self.val else None


class Prog:
    def __init__(self, nc, ctx):
        self.nc, self.ctx = nc, ctx
        self.pe, self.act, self.dve, self.pool, self.sp = (
            Eng(n, ctx.enter_context(nc.semaphore("c_" + n)), self) for n in ("pe", "act", "dve", "pool", "sp"))
        self.slots, self.filler, self.filling = [], None, False

    def fill_to(self, at):
        if self.filler is None or self.filling:
            return
        self.filling = True
        while self.pe.time + 0.6 < at:
            if next(self.filler, "end") == "end":
                self.filler = None
                break
        self.filling = False

    def slot(self, name):
        s = Slot(self.ctx.enter_context(self.nc.semaphore("d_" + name)))
        self.slots.append(s)
        return s

    def A(self, out, in_, f=AF.Copy, w=(), **kw):
        return self.act.put("activation", (out, in_, f), kw, [self.act.t, *w], dur=0.2 + width(out) / 1200)

    def V(self, method, *args, w=(), **kw):
        n = width(args[1] if method in ("tensor_reduce", "max", "max_index") else args[0])
        if method in ("reciprocal", "tensor_tensor_scan"):
            n *= 2
        if method in ("tensor_scalar", "memset"):
            n *= 0.6
        return self.dve.put(method, args, kw, [self.dve.t, *w], dur=0.07 + n / 960)

    def G(self, method, *args, w=(), **kw):
        return self.pool.put(method, args, kw, [self.pool.t, *w], dur=0.1 + width(args[0]) * 0.0024)

    def mm(self, out, l, r, start, stop, w=(), inc=False):
        n = width(out)
        d = n / 2350 if l.dtype == F32R else max(n, 64) / 580
        return self.pe.put("matmul", (out, l, r), dict(start=start, stop=stop), w, inc, dur=d)

    def tr(self, out, in_, ident, w=(), inc=False):
        return self.pe.put("transpose", (out, in_, ident), {}, w, inc, dur=0.06)

    def dma(self, eng, out, in_, slot, w=()):
        eng.wait(w)
        eng.time += 1.1 if eng is self.pool else 0.06
        t = slot.next(eng.time + 2.3 + out.shape[0] * width(out) * 4 / 300e3)
        eng.list.append(("op", "dma_start", (out, in_), {}, (slot.sem, 16)))
        return t

    def idma(self, slot, w=(), **kw):
        self.pool.wait(w)
        self.pool.time += 1.1
        t = slot.next(self.pool.time + 5.0)
        self.pool.list.append(("op", "indirect_dma_start", (), kw, (slot.sem, 16)))
        return t

    def barrier(self, but=()):
        toks = [e.t for e in (self.pe, self.act, self.dve, self.pool)] + [s.t for s in self.slots if s not in but]
        for e in (self.pe, self.act, self.dve, self.pool, self.sp):
            e.wait(toks)
        m = max(e.time for e in (self.pe, self.act, self.dve, self.pool))
        for e in (self.pe, self.act, self.dve, self.pool, self.sp):
            e.time = m


def program(nc, I, out, stop=99):
    ctx = ExitStack()
    P = Prog(nc, ctx)
    pe, act, dve, pool, sp = P.pe, P.act, P.dve, P.pool, P.sp
    A, V, G, mm, tr = P.A, P.V, P.G, P.mm, P.tr

    def sb(name, n, dt=F32, c=ctx, p=128):
        return c.enter_context(nc.sbuf_tensor(name, [p, n], dt))[:, :]

    def scratch(name, shape):
        return nc.dram_tensor(name, shape, F32, kind="Internal").ap()

    D_u = scratch("D_u", [22, 128, T])
    D_g = scratch("D_g", [32, 128, T])
    D_y = scratch("D_y", [16, 128, T])
    D_dt = scratch("D_dt", [8, T])
    D_xb = scratch("D_xb", [8, 128, T])
    D_v = scratch("D_v", [29, 128, 1280])
    D_o = scratch("D_o", [8, 128, T])
    D_h = scratch("D_h", [T, 1024])
    D_m5 = scratch("D_m5", [1, 1024])
    D_acc = scratch("D_acc", [T, 1024])

    par = sb("par", NPAR)
    con = sb("con", NCON1)
    con2 = [None]
    bank = [ctx.enter_context(nc.psum_tensor(f"bank{i}", [128, 512], F32))[:, :] for i in range(8)]

    def pr(name, i=0, n=1):
        return par[:, PO[name][0] + i:PO[name][0] + i + n]

    def cn(name, a=0, b=None):
        o, n = CO[name]
        src, o = (con, o) if o < NCON1 else (con2[0], o - NCON1)
        return src[:, o + a:o + (n if b is None else b)]

    ident, ones = cn("ident"), cn("ones")

    c1 = ExitStack()
    WH, WL = sb("WH", 2048, F32R), sb("WL", 2048, F32R)
    WR = sb("WR", 3 * 1024)
    stg = sb("stg", 2048)
    res = sb("res", 8 * T)
    aq2 = sb("aq2", 2 * T)
    acq, ac2 = aq2[:, 0:T], aq2[:, T:2 * T]
    md = sb("md", 96)
    mod = md.rearrange("p (m s) -> p m s", s=2)
    cs_ = sb("cs_", 24)
    cf = sb("cf", 16)
    XH, XL = sb("XH", 8 * T, F32R, c1), sb("XL", 8 * T, F32R, c1)
    s_par = P.slot("par")
    s_wr = [P.slot(f"wr{i}") for i in range(3)]
    s_ld = [P.slot(f"ld{i}") for i in range(4)]
    s_st = [P.slot(f"st{i}") for i in range(2)]
    s_x = P.slot("x")
    s_m = [P.slot(f"m{i}") for i in range(6)]

    P.dma(sp, par, I["par"], s_par)
    t_par = P.dma(sp, con, I["con"][:, 0:NCON1], s_par)

    W = dict(n=0, spl=0, gemm=None, loaded=[], raw_free=[None] * 3, spl_free=[None] * 2, halves=[None] * 2)

    def w_load(src, K):
        n = W["n"]
        W["n"] += 1
        i = n % 3
        t = P.dma(sp, WR[:, i * 1024:i * 1024 + K * 128], src, s_wr[i], [*(W["raw_free"][i] or [])])
        W["loaded"].append((n, K, t))

    def w_split(eng="pool"):
        n, K, t = W["loaded"].pop(0)
        i, j = n % 3, W["spl"] % 2
        W["spl"] += 1
        raw = WR[:, i * 1024:i * 1024 + K * 128]
        hi, lo = WH[:, j * 1024:j * 1024 + K * 128], WL[:, j * 1024:j * 1024 + K * 128]
        a = A(hi, raw, w=[t, W["spl_free"][j]])
        put = G if eng == "pool" else V
        b = put("tensor_tensor", lo, raw, hi.bitcast(F32), ALU.subtract, w=[t, a, W["spl_free"][j]])
        W["raw_free"][i] = [a, b]
        return j, [a, b]

    def stream(tiles, eng="pool"):
        tiles = list(tiles)
        for s, K in tiles[:2]:
            w_load(s, K)
        nxt = w_split(eng)
        for n, (s, K) in enumerate(tiles):
            if n + 2 < len(tiles):
                w_load(*tiles[n + 2])
            cur = nxt
            nxt = w_split(eng) if n + 1 < len(tiles) else None
            yield cur

    bank_free = [None] * 8

    def gemm_steps(w, K, x, cols, b, xw=(), xk=None):
        j, wt = w
        n = cols[1] - cols[0]
        first = True
        for k in range(K):
            whi = WH[:, j * 1024 + k * 128:j * 1024 + k * 128 + 128]
            wlo = WL[:, j * 1024 + k * 128:j * 1024 + k * 128 + 128]
            xhi, xlo = x(k, cols)
            for i, (l, r) in enumerate(((whi, xhi), (whi, xlo), (wlo, xhi))):
                last = k == K - 1 and l is wlo
                t = mm(bank[b][:, 0:n], l, r, first, last,
                       w=[*(wt + list(xw) + [bank_free[b]] if first else ()),
                          *([xk[k][cols[0] // 512]] if xk and i == 0 else ())], inc=last)
                first = False
            if not last:
                yield
        W["spl_free"][j] = t
        W["gemm"] = t

    def gemm(*args, **kw):
        for _ in gemm_steps(*args, **kw):
            pass
        return W["gemm"]

    def evac(out, in_, w):
        if act.time <= dve.time:
            return A(out, in_, w=w)
        return V("tensor_copy", out, in_, w=w)

    def xs(S):
        return lambda k, c: (XH[:, k * S + c[0]:k * S + c[1]], XL[:, k * S + c[0]:k * S + c[1]])

    def split_x(dst, src, w=(), pool_lo=False):
        hi, lo = XH[:, dst[0]:dst[1]], XL[:, dst[0]:dst[1]]
        a = A(hi, src, w=w)
        put = G if pool_lo else V
        return put("tensor_tensor", lo, src, hi.bitcast(F32), ALU.subtract, w=[a, *w])

    dve_t = [None, None]

    def xc(j):
        return res[:, j * T:(j + 1) * T]

    c0 = ExitStack()
    sq = sb("sq", 2 * T, c=c0)
    r = sb("r", T, c=c0)
    for j in range(4):
        P.dma(sp, res[:, 2 * j * T:(2 * j + 2) * T].rearrange("p (a t) -> p a t", a=2),
              I["xT"][2 * j:2 * j + 2].rearrange("a p t -> p a t"), s_ld[j])

    def rstd_tail(acc, r, D, n, banks, t, halves=None):
        for h in range(0, n, 512):
            b = banks[h // 512]
            m = min(512, n - h)
            t2 = mm(bank[b][:, 0:m], ones, acc[:, h:h + m], True, True, w=[t, bank_free[b], t_par], inc=True)
            v = V("tensor_scalar", r[:, h:h + m], bank[b][:, 0:m], 1.0 / D, EPS, ALU.mult, ALU.add,
                  w=[t2, act.t])
            bank_free[b] = v
            v = V("reciprocal", r[:, h:h + m], r[:, h:h + m])
            if halves is not None:
                halves.append(A(r[:, h:h + m], r[:, h:h + m], AF.Sqrt, w=[v]))
        return halves[-1] if halves is not None else A(r[:, 0:n], r[:, 0:n], AF.Sqrt, w=[dve.t])

    for j in range(8):
        if j == 0:
            t = A(acq, xc(0), AF.Square, w=[s_ld[0].t])
        else:
            q = sq[:, (j % 2) * T:(j % 2) * T + T]
            a = A(q, xc(j), AF.Square, w=[s_ld[j // 2].t, dve_t[j % 2]])
            t = dve_t[j % 2] = V("tensor_tensor", acq, acq, q, ALU.add, w=[a])
    th_ = []
    rstd_tail(acq, r, 1024, T, (0, 1), t, th_)
    hx = [[None, None] for _ in range(8)]
    for h in range(2):
        hs = slice(h * 512, h * 512 + 512)
        for j in range(8):
            v = V("scalar_tensor_tensor", xc(j)[:, hs], xc(j)[:, hs], pr("g_mix", j), r[:, hs], ALU.mult, ALU.mult,
                  w=[th_[h], t_par])
            hx[j][h] = split_x((j * T + h * 512, j * T + h * 512 + 512), xc(j)[:, hs], w=[v], pool_lo=j % 2 == 1)
    c0.close()

    u_tok = {}
    cM = ExitStack()
    cqv = sb("cqv", 6 * T, c=cM)

    class Region:

        def __init__(self, c):
            self.c, self.at = c, 0

        def __call__(self, name, n, c=None):
            if self.at + n <= 8 * T:
                self.at += n
                return res[:, self.at - n:self.at]
            return sb(name, n, c=self.c)

    A(cf, pr("cc", 0, 16), AF.Tanh, scale=0.5, w=[t_par])
    V("scalar_tensor_tensor", cf, cf, 1.0, pr("cc", 0, 16), ALU.add, ALU.mult, w=[act.t])
    cv = V("tensor_scalar", cf, cf, 0.5, None, ALU.mult)

    t_h = [dve.t, act.t]

    def stream_g():
        tiles = [(I["w_in"][m], 8) for m in range(60)]
        for m, w in enumerate(stream(tiles)):
            i = m % 2
            dst = cqv[:, m * T:(m + 1) * T] if m < 6 else stg[:, i * T:(i + 1) * T]
            es = []
            for h in range(2):
                yield from gemm_steps(w, 8, xs(T), (h * 512, h * 512 + 512), h, xk=hx if m == 0 else None)
                d = dst[:, h * 512:h * 512 + 512]
                ww = [W["gemm"]] + (t_h if m < 6 else [s_st[i].t])
                if m < 28:
                    e = evac(d, bank[h][:, :], ww)
                else:
                    e = A(d, bank[h][:, :], AF.Tanh, scale=0.5, w=ww)
                bank_free[h] = e
                es.append(e)
                yield
            if m < 6:
                u_tok[m] = es
            elif m < 28:
                u_tok[m] = [P.dma(sp, D_u[m - 6], dst, s_st[i], es)]
            else:
                u_tok[m] = [P.dma(sp, D_g[m - 28], dst, s_st[i], es)]

    def pull(table, ms):
        was, P.filling = P.filling, True
        while any(m not in table for m in ms):
            next(P.filler, None)
        P.filling = was

    def need(*ms):
        pull(u_tok, ms)
        return [t for m in ms for t in u_tok[m]]

    B_S = ((2, 3), (4, 5))
    B_T, B_O = 6, 7
    gbank = {}

    def bw(b, t):
        bank_free[b] = t
        return t

    def small_mm2(banks, parts, w=()):
        out = []
        for h in range(2):
            ps = parts(h)
            for n, (l, rr) in enumerate(ps):
                t = mm(bank[banks[h]][:, :] if l.shape[-1] == 128 else bank[banks[h]][0:l.shape[-1], :],
                       l, rr, n == 0, n == len(ps) - 1,
                       w=[*w, bank_free[banks[h]]] if n == 0 else (), inc=n == len(ps) - 1)
            out.append(t)
        return out

    def mixer_mla(c):
        vN = c("vN", 8 * 512)
        cs = c("cs", 2 * T)
        rp = c("rp", 2 * T)
        uq = c("uq", 4 * 384)
        ukv = ac2
        PT = c("PT", 8 * 512)
        uqr, vw = PT[:, 0:1536], PT[:, 1536:2560]
        cosT, sinT = cs[:, 0:T], cs[:, T:2 * T]
        yt = acq
        tA, tB = PT[:, 2560:3584], yt
        posr = vN[:, 0:T].bitcast(I32)
        P.dma(pool, uq, I["w_uq"][:, 0:1536], s_m[0])
        P.dma(pool, ukv, I["w_ukv"][:, 0:1024], s_m[1])
        P.dma(pool, uqr, I["w_uq"][:, 1536:3072], s_m[4])
        P.dma(pool, vw, I["w_ukv"][:, 1024:2048], s_m[5])
        P.dma(pool, posr[0:1, :], I["positions"], s_m[2])
        P.dma(pool, D_dt, cqv[32:40, 5 * T:6 * T], s_m[3], need(5))
        V("tensor_copy", tA[0:1, :], posr[0:1, :], w=[s_m[2].t])
        for h in range(2):
            t = mm(bank[2 + h][:, :], ones[0:1, :], tA[0:1, h * 512:h * 512 + 512], True, True,
                   w=[dve.t, bank_free[2 + h]], inc=True)
            v = V("tensor_scalar", tB[:, h * 512:h * 512 + 512], bank[2 + h][:, :], cn("inv"), None, ALU.mult, w=[t])
            bw(2 + h, v)
        V("tensor_scalar", cosT, tB, 1.0 / (2 * np.pi), 12582912.0, ALU.mult, ALU.add)
        V("tensor_scalar", cosT, cosT, -12582912.0, None, ALU.add)
        for cc in (6.28125, 0.0019350051879882812, 3.019916050561733e-07):
            V("scalar_tensor_tensor", tB, cosT, -cc, tB, ALU.mult, ALU.add)
        V("tensor_scalar", tB, tB, 3.1415925, -3.1415925, ALU.min, ALU.max)
        A(sinT, tB, AF.Sin, w=[dve.t])
        A(cosT, tB, AF.Sin, scale=0.5, w=[dve.t])
        V("tensor_scalar", sinT, sinT, cn("sgn"), None, ALU.mult, w=[act.t])
        V("tensor_tensor", cosT, cosT, cosT, ALU.mult)
        V("tensor_scalar", cosT, cosT, -2.0, 1.0, ALU.mult, ALU.add)
        yield
        cq = [cqv[:, j * T:(j + 1) * T] for j in range(3)]
        ckv = [cqv[:, j * T:(j + 1) * T] for j in range(3, 5)]
        krdt = cqv[:, 5 * T:6 * T]
        for seg, D, g in ((cq, 384, "q_norm"), (ckv, 256, "kv_norm")):
            for j, s in enumerate(seg):
                if j == 0:
                    t = A(tA, s, AF.Square, w=[dve.t, *need(0, 1, 2, 3, 4, 5)])
                else:
                    a = A(tB, s, AF.Square, w=[dve.t])
                    t = V("tensor_tensor", tA, tA, tB, ALU.add, w=[a])
            t = rstd_tail(tA, tB, D, T, (2, 3), t)
            for j, s in enumerate(seg):
                nt = V("scalar_tensor_tensor", s, s, pr(g, j), tB, ALU.mult, ALU.mult, w=[t])
            yield
        for g in range(2):
            for n, c0_ in enumerate((g, 2 + g)):
                ts = small_mm2(B_S[n], lambda h: [(uqr[:, c0_ * 384 + k * 128:c0_ * 384 + k * 128 + 128],
                                                   cq[k][:, h * 512:h * 512 + 512]) for k in range(3)],
                               w=[nt, s_m[4].t])
                for h in range(2):
                    hs = slice(h * 512, h * 512 + 512)
                    tab = (cosT, sinT)[n]
                    dst = (rp[:, g * T:(g + 1) * T], tA)[n]
                    bw(B_S[n][h], V("tensor_tensor", dst[:, hs], bank[B_S[n][h]][:, :], tab[:, hs], ALU.mult,
                                    w=[ts[h]]))
            V("tensor_tensor", rp[:, g * T:(g + 1) * T], rp[:, g * T:(g + 1) * T], tA, ALU.add)
            yield
        kr = krdt
        V("tensor_tensor", tA[64:96, :], krdt[0:32, :], cosT[0:32, :], ALU.mult)
        V("tensor_tensor", kr[64:96, :], krdt[64:96, :], sinT[64:96, :], ALU.mult)
        V("tensor_tensor", kr[64:96, :], kr[64:96, :], tA[64:96, :], ALU.add)
        for tc in range(8):
            b = B_S[tc % 2][0]
            for k in range(2):
                t = mm(bank[b][:, :], ckv[k][:, tc * 128:tc * 128 + 128], vw[:, k * 512:512 + k * 512],
                       k == 0, k == 1, w=[nt, s_m[5].t, bank_free[b]] if k == 0 else (), inc=k == 1)
            bw(b, A(vN[:, tc * 512:tc * 512 + 512], bank[b][:, :], w=[t]))
            if tc % 4 == 3:
                yield
        tv = act.t
        qk = c("qk", 4 * T)
        Pm = cs
        st = c("st", 32)
        SC = 96.0 ** -0.5
        ts_ = [None, None]
        pv_t = None
        for i in range(4):
            q_, k_ = [qk[:, a * T:(a + 1) * T] for a in range(2)], [qk[:, (2 + a) * T:(3 + a) * T] for a in range(2)]
            for n, (dst, chunk, K, wt, src) in enumerate(((q_, uq[:, i * 384:(i + 1) * 384], 3, s_m[0], cq),
                                                          (k_, ukv[:, i * 256:(i + 1) * 256], 2, s_m[1], ckv))):
                ts = small_mm2(B_S[n], lambda h: [(chunk[:, k * 128:k * 128 + 128],
                                                   src[k][:, h * 512:h * 512 + 512]) for k in range(K)],
                               w=[nt, wt.t])
                for h in range(2):
                    hs = slice(h * 512, h * 512 + 512)
                    b = B_S[n][h]
                    A(dst[0][0:64, hs], bank[b][0:64, :], w=[ts[h], pv_t])
                    bw(b, A(dst[1][0:64, hs], bank[b][64:128, :]))
            for a in range(2):
                hh = 2 * i + a
                A(q_[a][64:96, :], rp[32 * (hh % 4):32 * (hh % 4) + 32, (hh // 4) * T:(hh // 4 + 1) * T], w=[dve.t, pv_t])
                A(k_[a][64:96, :], kr[64:96, :], w=[pv_t])
            qk_t = act.t
            yield
            units = [(a, qb) for a in range(2) for qb in range(8)]
            state = {}

            def s1(u):
                a, qb = units[u]
                n = (qb + 1) * 128
                bs = B_S[u % 2]
                for h in range(0, n, 512):
                    b = bs[h // 512]
                    m = min(512, n - h)
                    t = mm(bank[b][:, 0:m], q_[a][0:96, qb * 128:qb * 128 + 128], k_[a][0:96, h:h + m], True, True,
                           w=[qk_t, bank_free[b]], inc=True)
                db = bs[(n - 1) // 512]
                o = (n - 128) % 512
                V("tensor_tensor", bank[db][:, o:o + 128], bank[db][:, o:o + 128], cn("mneg"), ALU.add, w=[t])
                c4 = (u % 4) * 8
                for h in range(0, n, 512):
                    b = bs[h // 512]
                    m = min(512, n - h)
                    V("tensor_reduce", st[:, c4 + h // 512:c4 + h // 512 + 1], bank[b][:, 0:m], AX.X, ALU.max)
                if n > 512:
                    V("tensor_tensor", st[:, c4:c4 + 1], st[:, c4:c4 + 1], st[:, c4 + 1:c4 + 2], ALU.max)
                v = V("tensor_scalar", st[:, c4 + 2:c4 + 3], st[:, c4:c4 + 1], -SC, None, ALU.mult)
                p = Pm[:, (u % 2) * T:(u % 2) * T + n]
                for h in range(0, n, 512):
                    b = bs[h // 512]
                    m = min(512, n - h)
                    e = A(p[:, h:h + m], bank[b][:, 0:m], AF.Exp, bias=st[:, c4 + 2:c4 + 3], scale=SC,
                          accum_out=st[:, c4 + 3 + h // 512:c4 + 4 + h // 512], w=[v, state.get(("tr", u - 2)), pool.t])
                    bw(b, e)
                state[u] = e

            def s2(u):
                a, qb = units[u]
                n = (qb + 1) * 128
                c4 = (u % 4) * 8
                p = Pm[:, (u % 2) * T:(u % 2) * T + n]
                w = [state[u]]
                if n > 512:
                    V("tensor_tensor", st[:, c4 + 3:c4 + 4], st[:, c4 + 3:c4 + 4], st[:, c4 + 4:c4 + 5], ALU.add, w=w)
                v = V("reciprocal", st[:, c4 + 5:c4 + 6], st[:, c4 + 3:c4 + 4], w=w)
                g = V("tensor_scalar", p, p, st[:, c4 + 5:c4 + 6], None, ALU.mult, w=[v, *w])
                qh, ql = qb // 4, qb % 4
                for k0 in range(0, qb + 1, 4):
                    kn = min(4, qb + 1 - k0)
                    for k in range(k0, k0 + kn):
                        t = tr(bank[B_T][:, (k - k0) * 128:(k - k0) * 128 + 128], p[:, k * 128:k * 128 + 128], ident,
                               w=[g, bank_free[B_T]] if k == k0 else (), inc=k == k0 + kn - 1)
                    bw(B_T, A(PT[:, :].rearrange("p (k q) -> p k q", k=8)[:, k0:k0 + kn, ql * 128:ql * 128 + 128],
                              bank[B_T][:, 0:kn * 128].rearrange("p (k q) -> p k q", q=128),
                              w=[t, state.get("pv")]))
                state[("tr", u)] = t
                if ql == 3:
                    hh = 2 * i + a
                    kc = qb + 1
                    for k in range(kc):
                        o = max(0, (k - 4 * qh) * 128)
                        t = mm(bank[B_O][a * 64:a * 64 + 64, o:512], vN[:, k * 512 + hh * 64:k * 512 + hh * 64 + 64],
                               PT[:, k * 512 + o:k * 512 + 512], k == 0, k == kc - 1,
                               w=[act.t, tv, bank_free[B_O]] if k == 0 else (), inc=k == kc - 1)
                    state["pv"] = t
                    bw(B_O, V("tensor_copy", yt[a * 64:a * 64 + 64, qh * 512:qh * 512 + 512],
                              bank[B_O][a * 64:a * 64 + 64, :], w=[t, s_m[3].t]))

            s1(0)
            for u in range(16):
                if u + 1 < 16:
                    s1(u + 1)
                s2(u)
                if u % 2:
                    yield
            pv_t = state["pv"]
            P.dma(pool, D_y[i], yt, s_m[3], [dve.t])

    def log1p_exp(v, t1, t2, t3, out):
        A(t1, v, AF.Abs, w=[dve.t])
        A(t1, t1, AF.Exp, scale=-1.0)
        V("tensor_scalar", t2, t1, 2.0, None, ALU.add, w=[act.t])
        V("reciprocal", t2, t2)
        V("tensor_tensor", t1, t1, t2, ALU.mult)
        V("tensor_tensor", t2, t1, t1, ALU.mult)
        V("tensor_scalar", t3, t2, 1.0 / 17, None, ALU.mult)
        for k in (15, 13, 11, 9, 7, 5, 3):
            V("scalar_tensor_tensor", t3, t3, 1.0 / k, t2, ALU.add, ALU.mult)
        V("scalar_tensor_tensor", t3, t3, 1.0, t1, ALU.add, ALU.mult)
        V("tensor_scalar", t2, v, 0.0, None, ALU.max)
        return V("scalar_tensor_tensor", out, t3, 2.0, t2, ALU.mult, ALU.add)

    def conv(dst, raw, wt, bias):
        V("tensor_scalar", dst, raw[:, 3:3 + T], wt[:, 3:4], bias, ALU.mult, ALU.add)
        for k in range(3):
            t = V("scalar_tensor_tensor", dst, raw[:, k:k + T], wt[:, k:k + 1], dst, ALU.mult, ALU.add)
        return t

    def b3(a, n):
        return a.unsqueeze(2).broadcast_to([a.shape[0], a.shape[1], n])

    def mixer_ssd(c):
        xb = c("xb", 6 * T)
        xdt = c("xdt", 8 * 512)
        CB = c("CB", 2 * T)
        Hs = c("Hs", 8 * 256)
        Lb = c("Lb", 2 * T)
        Mb = c("Mb", 2 * T)
        Eb = c("Eb", T)
        raws = c("raws", 2 * 1028)
        bmN = c("bmN", 8 * 128)
        xd = c("xd", 512)
        hw = c("hw", 32)
        smal = c("smal", 64 * 4 + 32)
        dtN, acN, deN, la = (smal[:, i * 64:(i + 1) * 64] for i in range(4))
        eD = smal[:, 256:288]
        dt8, ac8, r8, sel8 = (Lb[0:8, 0:T], Lb[0:8, T:2 * T], Mb[0:8, 0:T], Mb[0:8, T:2 * T])
        acs_t = acq
        sel_t = ac2
        P.dma(pool, r8, I["scon"][0], s_m[0])
        P.dma(pool, sel_t[0:8, :], I["scon"][1], s_m[0])
        P.dma(pool, dt8, D_dt, s_m[1])
        for i in range(2):
            V("memset", raws[:, i * 1028:i * 1028 + 3], 0.0)
        mset = dve.t
        V("tensor_scalar", hw, par[:, PO["conv_w"][0]:PO["conv_w"][0] + 32], 0.5, None, ALU.mult)
        raw_t = [None, None]

        def load_raw(n, src, w=()):
            i = n % 2
            P.dma(pool, raws[:, i * 1028 + 3:i * 1028 + 3 + T], src, s_m[2 + i], [mset, raw_t[i], *w])

        load_raw(0, D_u[4], need(10))
        load_raw(1, D_u[5], need(11))
        V("tensor_scalar", dt8, dt8, par[0:8, PO["dt_bias"][0]:PO["dt_bias"][0] + 1], None, ALU.add, w=[s_m[1].t])
        log1p_exp(dt8, Eb[0:8, :], xdt[0:8, 0:T], xdt[0:8, T:2 * T], dt8)
        A(smal[0:8, 256:257], par[0:8, PO["a_log"][0]:PO["a_log"][0] + 1], AF.Exp)
        V("tensor_scalar", Eb[0:8, :], dt8, smal[0:8, 256:257], -1.0, ALU.mult, ALU.mult, w=[act.t])
        ta = V("tensor_tensor_scan", acs_t[0:8, :], r8, Eb[0:8, :], 0.0, ALU.mult, ALU.add, w=[s_m[0].t])
        yield
        for cc in range(8):
            tr(bank[6][:, cc * 8:cc * 8 + 8], dt8[:, cc * 128:cc * 128 + 128], ident[0:8, 0:8],
               w=[ta, bank_free[6]] if cc == 0 else ())
            t = tr(bank[6][:, 64 + cc * 8:72 + cc * 8], acs_t[0:8, cc * 128:cc * 128 + 128], ident[0:8, 0:8], inc=cc == 7)
        V("tensor_copy", dtN, bank[6][:, 0:64], w=[t])
        bw(6, V("tensor_copy", acN, bank[6][:, 64:128]))
        for h in range(8):
            t = mm(bank[7][:, h * 8:h * 8 + 8], sel_t[0:8, h * 128:h * 128 + 128], acs_t[0:8, 127::128], True, True,
                   w=[bank_free[7], s_m[0].t] if h == 0 else (), inc=h == 7)
        v = V("tensor_tensor", deN.rearrange("p (c h) -> p c h", c=8), bank[7][:, 0:64].rearrange("p (h c) -> p c h", h=8),
              acN.rearrange("p (c h) -> p c h", c=8), ALU.subtract, w=[t])
        A(deN, deN, AF.Exp, w=[v])
        for g in range(2):
            A(eD[g * 64:g * 64 + 64, :].rearrange("p (c r) -> p c r", c=8),
              bank[7][g * 64:g * 64 + 64, g * 32:g * 32 + 32].rearrange("p (r c) -> p c r", c=8), AF.Exp)
        bw(7, act.t)
        order = (4, 5, 0, 1, 2, 3)
        for n, j in enumerate(order):
            i = n % 2
            dst = xb[:, j * T:(j + 1) * T]
            dve.wait([s_m[2 + i].t])
            raw_t[i] = conv(dst, raws[:, i * 1028:(i + 1) * 1028], hw[:, 4 * j:4 * j + 4], hw[:, 24 + j:25 + j])
            if n + 2 < 6:
                jj = order[n + 2]
                load_raw(n + 2, D_u[jj], need(6 + jj))
            a = A(Eb, dst, AF.Tanh, w=[dve.t])
            V("scalar_tensor_tensor", dst, Eb, 1.0, dst, ALU.add, ALU.mult, w=[a])
            yield
        bm, cm = xb[:, 4 * T:5 * T], xb[:, 5 * T:6 * T]
        txb = dve.t
        for cc in range(8):
            b = 6 + cc % 2
            t = tr(bank[b][:, 0:128], bm[:, cc * 128:cc * 128 + 128], ident, w=[txb, bank_free[b]], inc=True)
            bw(b, A(bmN[:, cc * 128:cc * 128 + 128], bank[b][:, 0:128], w=[t]))
            b = B_S[0][cc % 2]
            for j in range(4):
                t = tr(bank[b][:, j * 128:j * 128 + 128], xb[:, j * T + cc * 128:j * T + cc * 128 + 128], ident,
                       w=[bank_free[b]] if j == 0 else (), inc=j == 3)
            bw(b, V("tensor_tensor", xdt[:, cc * 512:cc * 512 + 512].rearrange("p (h e) -> p h e", h=8),
                    bank[b][:, :].rearrange("p (h e) -> p h e", h=8), b3(dtN[:, cc * 8:cc * 8 + 8], 64), ALU.mult, w=[t]))
        yield
        for g in range(2):
            for cc in range(8):
                b = B_S[1][cc // 4]
                t = mm(bank[b][:, (cc % 4) * 128:(cc % 4) * 128 + 128], bm[g * 64:g * 64 + 64, cc * 128:cc * 128 + 128],
                       cm[g * 64:g * 64 + 64, cc * 128:cc * 128 + 128], True, True, w=[bank_free[b]] if cc % 4 == 0 else (),
                       inc=cc % 4 == 3)
                if cc % 4 == 3:
                    o = g * T + (cc // 4) * 512
                    bw(b, V("tensor_tensor", CB[:, o:o + 512].rearrange("p (c l) -> p c l", c=4),
                            bank[b][:, :].rearrange("p (c l) -> p c l", c=4),
                            cn("mle").unsqueeze(1).broadcast_to([128, 4, 128]), ALU.mult, w=[t]))
        th = V("memset", Hs[:, 0:256], 0.0)
        xt = None
        for cc in range(7):
            b = 6 + cc % 2
            v = V("tensor_tensor", xd.rearrange("p (h e) -> p h e", h=8),
                  xdt[:, cc * 512:cc * 512 + 512].rearrange("p (h e) -> p h e", h=8), b3(deN[:, cc * 8:cc * 8 + 8], 64),
                  ALU.mult, w=[act.t, xt])
            for g in range(2):
                xt = mm(bank[b][g * 64:g * 64 + 64, 0:256], bmN[:, cc * 128 + g * 64:cc * 128 + g * 64 + 64],
                        xd[:, g * 256:g * 256 + 256], True, True, w=[v, bank_free[b]] if g == 0 else (), inc=g == 1)
            V("tensor_tensor", Hs[:, (cc + 1) * 256:(cc + 2) * 256].rearrange("p (r e) -> p r e", r=4),
              Hs[:, cc * 256:(cc + 1) * 256].rearrange("p (r e) -> p r e", r=4), b3(eD[:, cc * 4:cc * 4 + 4], 64), ALU.mult)
            th = bw(b, V("tensor_tensor", Hs[:, (cc + 1) * 256:(cc + 2) * 256], Hs[:, (cc + 1) * 256:(cc + 2) * 256],
                         bank[b][:, 0:256], ALU.add, w=[xt]))
            if cc % 3 == 2:
                yield
        Mt = [None, None]

        def pre(h):
            g, i = h // 4, h % 2
            Lh, Mh = Lb[:, i * T:(i + 1) * T], Mb[:, i * T:(i + 1) * T]
            for k in range(2):
                b = B_S[0][k]
                t = mm(bank[b][:, :], sel_t[0:8, h * 128:h * 128 + 128], acs_t[0:8, k * 512:k * 512 + 512], True, True,
                       w=[bank_free[b]], inc=True)
                for cc in range(4 * k, 4 * k + 4):
                    V("tensor_scalar", Lh[:, cc * 128:cc * 128 + 128], bank[b][:, (cc % 4) * 128:(cc % 4) * 128 + 128],
                      acN[:, cc * 8 + h:cc * 8 + h + 1], 0.0, ALU.subtract, ALU.min, w=[t, Mt[i]])
                e = A(Mh[g * 64:g * 64 + 64, k * 512:k * 512 + 512], bank[b][g * 64:g * 64 + 64, :], AF.Exp, w=[dve.t, Mt[i]])
                bw(b, V("tensor_tensor", Mh[g * 64:g * 64 + 64, k * 512:k * 512 + 512],
                        Mh[g * 64:g * 64 + 64, k * 512:k * 512 + 512],
                        cm[g * 64:g * 64 + 64, k * 512:k * 512 + 512], ALU.mult, w=[e]))
            a = A(Lh, Lh, AF.Exp, w=[dve.t])
            return V("tensor_tensor", Lh, Lh, CB[:, g * T:(g + 1) * T], ALU.mult, w=[a])

        nxt = pre(0)
        for h in range(8):
            g, i, r_, j = h // 4, h % 2, h % 4, h // 2
            cur = nxt
            if h + 1 < 8:
                nxt = pre(h + 1)
            Lh, Mh = Lb[:, i * T:(i + 1) * T], Mb[:, i * T:(i + 1) * T]
            o = (h % 2) * 64
            for cc in range(8):
                b = B_S[1][cc // 4]
                reg = bank[b][o:o + 64, (cc % 4) * 128:(cc % 4) * 128 + 128]
                mm(reg, xdt[:, cc * 512 + h * 64:cc * 512 + h * 64 + 64], Lh[:, cc * 128:cc * 128 + 128], True, False,
                   w=[cur, bank_free[b], th])
                Mt[i] = mm(reg, Hs[g * 64:g * 64 + 64, cc * 256 + r_ * 64:cc * 256 + r_ * 64 + 64],
                           Mh[g * 64:g * 64 + 64, cc * 128:cc * 128 + 128], False, True, inc=cc == 7)
            if i:
                for k in range(2):
                    xj = xb[:, j * T + k * 512:j * T + k * 512 + 512]
                    bw(B_S[1][k], V("scalar_tensor_tensor", xj, xj, pr("ssd_d", j), bank[B_S[1][k]][:, :], ALU.mult,
                                    ALU.add, w=[Mt[i]]))
            yield
        zt = None
        for j in range(4):
            z_, xj = CB[:, (j % 2) * T:(j % 2) * T + T], xb[:, j * T:(j + 1) * T]
            t = P.dma(pool, z_, D_u[14 + j], s_m[4 + j % 2], [dve.t, *need(20 + j)])
            a = A(Lb[:, 0:T], z_, AF.Tanh, scale=0.5, w=[t, dve.t])
            V("scalar_tensor_tensor", z_, Lb[:, 0:T], 1.0, z_, ALU.add, ALU.mult, w=[a])
            V("scalar_tensor_tensor", xj, xj, 0.5, z_, ALU.mult, ALU.mult)
            if j == 0:
                t = A(Mb[:, 0:T], xj, AF.Square, w=[dve.t])
            else:
                a = A(Lb[:, T:2 * T], xj, AF.Square, w=[dve.t])
                t = V("tensor_tensor", Mb[:, 0:T], Mb[:, 0:T], Lb[:, T:2 * T], ALU.add, w=[a])
        t = rstd_tail(Mb[:, 0:T], Eb, 512, T, (2, 3), t)
        for j in range(4):
            xj = xb[:, j * T:(j + 1) * T]
            v = V("scalar_tensor_tensor", xj, xj, pr("ssd_norm", j), Eb, ALU.mult, ALU.mult, w=[t])
            P.dma(pool, D_y[8 + j], xj, s_m[j], [v])
        yield

    def mixer_lru(c):
        av, mv, uv = c("av", 4 * T), c("mv", 4 * T), c("uv", 4 * T)
        raws = c("raws2", 2 * 1028)
        t1, t2 = c("lt1", T), c("lt2", T)
        wai = c("wai", 8 * 128)
        hb = c("hb", 24)
        P.dma(pool, wai, I["w_lru"], s_m[5])
        for i in range(2):
            V("memset", raws[:, i * 1028:i * 1028 + 3], 0.0)
        mset = dve.t
        raw_t = [None, None]

        def load_raw(n, j):
            P.dma(pool, raws[:, (n % 2) * 1028 + 3:(n % 2) * 1028 + 3 + T], D_u[6 + j], s_m[n % 2],
                  [mset, raw_t[n % 2], *need(12 + j)])

        load_raw(0, 0)
        load_raw(1, 1)
        V("tensor_scalar", hb[:, 0:8], par[:, PO["b_a"][0]:PO["b_a"][0] + 8], 0.5, None, ALU.mult)
        V("tensor_scalar", hb[:, 8:12], pr("lam", 0, 4), -1.0, None, ALU.mult)
        log1p_exp(hb[:, 8:12], hb[:, 12:16], hb[:, 16:20], hb[:, 20:24], hb[:, 8:12])
        V("tensor_scalar", hb[:, 8:12], hb[:, 8:12], -4.0, None, ALU.mult)
        for j in range(4):
            a_, m_, u_ = av[:, j * T:(j + 1) * T], mv[:, j * T:(j + 1) * T], uv[:, j * T:(j + 1) * T]
            dve.wait([s_m[j % 2].t])
            xct = raw_t[j % 2] = conv(u_, raws[:, (j % 2) * 1028:(j % 2 + 1) * 1028], pr("lconv_w", 4 * j, 4), pr("lconv_b", j))
            if j + 2 < 4:
                load_raw(j + 2, j + 2)
            for s, dst in enumerate((t1, t2)):
                for k in range(2):
                    b = B_S[s][k]
                    t = mm(bank[b][:, :], wai[:, (s * 4 + j) * 128:(s * 4 + j + 1) * 128], u_[:, k * 512:k * 512 + 512],
                           True, True, w=[xct, bank_free[b], s_m[5].t], inc=True)
                    bw(b, A(dst[:, k * 512:k * 512 + 512], bank[b][:, :], AF.Tanh, scale=0.5, bias=hb[:, 4 * s + j:4 * s + j + 1],
                            w=[t, xct]))
            ta = act.t
            V("tensor_scalar", t1, t1, 1.0, hb[:, 8 + j:9 + j], ALU.add, ALU.mult, w=[ta])
            v = V("tensor_scalar", t2, t2, 0.5, 0.5, ALU.mult, ALU.add)
            A(a_, t1, AF.Exp, w=[v])
            a = A(m_, t1, AF.Tanh, scale=-1.0)
            V("tensor_tensor", u_, u_, t2, ALU.mult, w=[pe.t])
            V("tensor_tensor", t2, a_, a_, ALU.mult, w=[a])
            V("scalar_tensor_tensor", m_, t2, 1.0, m_, ALU.add, ALU.mult)
            yield
        for j in range(4):
            a = A(mv[:, j * T:(j + 1) * T], mv[:, j * T:(j + 1) * T], AF.Sqrt, w=[dve.t])
        for j in range(4):
            m_ = mv[:, j * T:(j + 1) * T]
            V("tensor_tensor", uv[:, j * T:(j + 1) * T], uv[:, j * T:(j + 1) * T], m_, ALU.mult, w=[a])
            V("tensor_tensor_scan", m_, av[:, j * T:(j + 1) * T], uv[:, j * T:(j + 1) * T], 0.0, ALU.mult, ALU.add)
            yield
        for j in range(4):
            g_, m_ = av[:, j * T:(j + 1) * T], mv[:, j * T:(j + 1) * T]
            t = P.dma(pool, g_, D_u[18 + j], s_m[2 + j % 2], [dve.t, *need(24 + j)])
            a = A(t1, g_, AF.Square, w=[t, dve.t])
            V("tensor_scalar", t1, t1, 0.044715, 1.0, ALU.mult, ALU.add, w=[a])
            v = V("tensor_tensor", t1, t1, g_, ALU.mult)
            a = A(t1, t1, AF.Tanh, scale=0.7978845608028654, w=[v])
            V("scalar_tensor_tensor", t1, t1, 1.0, g_, ALU.add, ALU.mult, w=[a])
            v = V("scalar_tensor_tensor", m_, m_, 0.5, t1, ALU.mult, ALU.mult)
            P.dma(pool, D_y[12 + j], m_, s_m[4], [v, s_m[4].t])
            yield

    def mixer_pool(c):
        raw = c("praw", 2 * 1040)
        tmp = c("ptmp", 2 * 1040)
        wp = c("wp", 512)
        yo = c("yo", 2 * T)
        P.dma(pool, wp, I["w_pool"], s_m[5])
        for a in (raw, tmp):
            for i in range(2):
                V("memset", a[:, i * 1040:i * 1040 + 16], 0.0)
        mset = dve.t
        used = [None, None]
        for g in range(4):
            i = g % 2
            rw = raw[:, i * 1040:(i + 1) * 1040]
            t = P.dma(pool, rw[:, 16:], D_u[10 + g], s_m[i], [mset, used[i], *need(16 + g)])
            cur, n = rw, 0
            for st_ in (1, 2, 4, 8)[:g + 1]:
                nx = tmp[:, n * 1040:(n + 1) * 1040]
                V("tensor_tensor", nx[:, 16:], cur[:, 16:], cur[:, 16 - st_:1040 - st_], ALU.add, w=[t, pe.t])
                cur, n = nx, 1 - n
            wd = 2 << g
            d = tmp[:, n * 1040:(n + 1) * 1040]
            V("tensor_tensor", d[:, 16:32], cur[:, 16:32], cn("icnt", 16 * g, 16 * g + 16), ALU.mult)
            V("tensor_tensor", d[:, 16:32], d[:, 16:32], rw[:, 16:32], ALU.subtract)
            v = used[i] = V("scalar_tensor_tensor", d[:, 32:], cur[:, 32:], 1.0 / wd, rw[:, 32:], ALU.mult, ALU.subtract)
            for k in range(2):
                b = B_S[g % 2][k]
                t = mm(bank[b][:, :], wp[:, g * 128:g * 128 + 128], d[:, 16 + k * 512:16 + k * 512 + 512], True, True,
                       w=[v, bank_free[b], s_m[5].t], inc=True)
                a = bw(b, A(yo[:, i * T + k * 512:i * T + k * 512 + 512], bank[b][:, :], scale=pr("pool_scale", g),
                            w=[t, s_m[2 + i].t]))
            P.dma(pool, D_y[4 + g], yo[:, i * T:(i + 1) * T], s_m[2 + i], [a])
            yield

    def run_m():
        for f in (mixer_mla, mixer_ssd, mixer_lru, mixer_pool):
            c = ExitStack()
            yield from f(Region(c))
            P.barrier()
            c.close()
            if f is mixer_mla:
                cM.close()

    P.filler = stream_g()
    pull(u_tok, range(6))
    for _ in run_m():
        pass
    if P.filler is not None:
        rest, P.filler = P.filler, None
        for _ in rest:
            pass
    P.barrier()
    nb = [0]

    qf = [None] * 4
    nq = [0]

    def q_slot():
        i = nq[0] = (nq[0] + 1) % 4
        return i, stg[:, i * 512:i * 512 + 512]

    def sum_sq(m, h, acc=None, scale=1.0):
        acc = acq if acc is None else acc
        rs, ac = res[:, m * T + h * 512:m * T + h * 512 + 512], acc[:, h * 512:h * 512 + 512]
        if m == 0:
            return A(ac, rs, AF.Square, scale=scale, w=[dve.t, pe.t])
        i, q = q_slot()
        a = A(q, rs, AF.Square, scale=scale, w=[dve.t, qf[i]])
        qf[i] = V("tensor_tensor", ac, ac, q, ALU.add, w=[a])

    def take_bank():
        b = nb[0] % 8
        nb[0] += 1
        return b

    c2 = ExitStack()
    mrg = sb("mrg", 8 * T, c=c2)
    yr = sb("yr", 2 * T, c=c2)
    gr = sb("gr", 3 * T, c=c2)
    y_pe = [None] * 4

    yt_ = [None] * 2

    def dma_y(b, j):
        i = j % 2
        yt_[i] = P.dma(pool, yr[:, i * T:(i + 1) * T], D_y[4 * b + j], s_m[i], [dve.t, act.t])

    def split_y(b, j):
        i = j % 2
        o = ((b % 2) * 4 + j) * T
        return split_x((o, o + T), yr[:, i * T:(i + 1) * T], w=[yt_[i], y_pe[b - 2] if b > 1 else None])

    tiles = [(I["w_branch"][m], 4) for m in range(32)] + [(I["w_out"][m], 8) for m in range(8)]
    for f in range(9):
        tiles += [(I["w_ff1"][4 * f + j], 8) for j in range(4)] if f < 8 else []
        tiles += [(I["w_ff2"][8 * (f - 1) + m], 4) for m in range(8)] if f else []
    tiles += [x_ for m in range(8) for x_ in ((I["w_ple_gate"][m], 8), (I["w_ple"][m], 2))]
    order = [7, 9, 10, 11, 1, 3, 4, 0, 8, 2, 5, 6, *range(12, 29)]
    tiles += [(I["w_in2"][m], 8) for m in order] + [(I["w_out2"][m], 8) for m in range(8)]
    ws = stream(tiles)
    gt, gfree = [None] * 3, [None] * 3

    def load_g(n):
        b, m = divmod(n, 8)
        gt[n % 3] = P.dma(sp, gr[:, (n % 3) * T:(n % 3 + 1) * T], D_g[n], s_ld[n % 3], [gfree[n % 3]])

    load_g(0)
    load_g(1)
    for j in range(2):
        dma_y(0, j)
    for j in range(4):
        yv = split_y(0, j)
        if j < 2:
            dma_y(0, j + 2)
    for n in range(32):
        w = next(ws)
        b, m = divmod(n, 8)
        if n + 2 < 32:
            load_g(n + 2)
        if b < 3 and m in (1, 3, 5):
            for j in range(2):
                if m > 1:
                    yn = split_y(b + 1, m - 3 + j)
                if m < 5:
                    dma_y(b + 1, m - 1 + j)
        g_ = gr[:, (n % 3) * T:(n % 3 + 1) * T]
        for h in range(2):
            bk = take_bank()
            hs = slice(h * 512, h * 512 + 512)
            off = (b % 2) * 4 * T
            t = gemm(w, 4, lambda k, c_: (XH[:, off + k * T + c_[0]:off + k * T + c_[1]],
                                          XL[:, off + k * T + c_[0]:off + k * T + c_[1]]),
                     (h * 512, h * 512 + 512), bk, xw=[yv])
            dst = mrg[:, m * T + h * 512:m * T + h * 512 + 512]
            if b == 0:
                gfree[n % 3] = bw(bk, V("scalar_tensor_tensor", dst, g_[:, hs], 1.0, bank[bk][:, :], ALU.add, ALU.mult,
                                        w=[t, gt[n % 3]]))
            else:
                gfree[n % 3] = bw(bk, V("scalar_tensor_tensor", g_[:, hs], g_[:, hs], 1.0, bank[bk][:, :], ALU.add,
                                        ALU.mult, w=[t, gt[n % 3]]))
                gfree[n % 3] = V("tensor_tensor", dst, dst, g_[:, hs], ALU.add)
        if m == 7:
            y_pe[b] = t
            if b < 3:
                yv = yn
    m_t = dve.t
    xv = [[None, None] for _ in range(8)]
    for h in range(2):
        for j in range(8):
            o = j * T + h * 512
            xv[j][h] = split_x((o, o + 512), mrg[:, o:o + 512], w=[m_t, W["gemm"]], pool_lo=j % 2 == 1)
    xt_ = [None] * 2
    for m in range(2):
        xt_[m] = P.dma(sp, yr[:, m * T:(m + 1) * T], I["xT"][m], s_x if m else s_ld[3], [dve.t])
    for m in range(8):
        w = next(ws)
        for h in range(2):
            bk = take_bank()
            t = gemm(w, 8, xs(T), (h * 512, h * 512 + 512), bk, xk=xv)
            v = bw(bk, V("scalar_tensor_tensor", res[:, m * T + h * 512:m * T + h * 512 + 512], bank[bk][:, :], 0.5,
                         yr[:, (m % 2) * T + h * 512:(m % 2) * T + h * 512 + 512], ALU.mult, ALU.add,
                         w=[t, xt_[m % 2]]))
            sum_sq(m, h)
        if m + 2 < 8:
            xt_[m % 2] = P.dma(sp, yr[:, (m % 2) * T:(m % 2 + 1) * T], I["xT"][m + 2], s_x if m % 2 else s_ld[3], [v])
    P.barrier()
    c2.close()

    def norm_x(gain):
        th = []
        rstd_tail(acq, acq, 1024, T, (6, 7), dve.t, th)
        out = [[None, None] for _ in range(8)]
        for h in range(2):
            for j in range(8):
                i, q = q_slot()
                v = V("scalar_tensor_tensor", q, res[:, j * T + h * 512:j * T + h * 512 + 512], pr(gain, j),
                      acq[:, h * 512:h * 512 + 512], ALU.mult, ALU.mult, w=[th[h], qf[i]])
                qf[i] = out[j][h] = split_x((j * T + h * 512, j * T + h * 512 + 512), q, w=[v, W["gemm"]],
                                            pool_lo=j % 2 == 1)
        return out

    xv = norm_x("g_mlp")
    ada = dict(m=0)
    ada_t, ada_pe = [None] * 2, [None] * 2
    ada_free = [x_ for p_ in xv for x_ in p_]

    def ada_load(m):
        if m < 48:
            ada_t[m % 2] = P.dma(sp, (ac2, acq)[m % 2], I["w_ada"][m], s_ld[m % 2], [ada_pe[m % 2], *ada_free])

    def ada_tile():
        m = ada["m"]
        if m == 48:
            return
        ada["m"] += 1
        raw, b = (ac2, acq)[m % 2], take_bank()
        for k in range(8):
            p_ = mm(bank[b][:, 0:2], raw[:, k * 128:k * 128 + 128], cf[:, 2 * k:2 * k + 2],
                    k == 0, k == 7, w=[ada_t[m % 2], cv, bank_free[b]] if k == 0 else (), inc=k == 7)
        ada_pe[m % 2] = p_
        ada_load(m + 2)
        bw(b, V("tensor_scalar", mod[:, m, :], bank[b][:, 0:2], pr("b_ada", m), None, ALU.add, w=[p_]))

    c2 = ExitStack()
    FH, FL = sb("FH", 8 * T, F32R, c2), sb("FL", 8 * T, F32R, c2)

    def fx(o):
        return lambda k, c_: (FH[:, o + k * T + c_[0]:o + k * T + c_[1]], FL[:, o + k * T + c_[0]:o + k * T + c_[1]])

    nff = [0]
    ada_load(0)
    ada_load(1)

    def ff_tile():
        nff[0] += 1
        if nff[0] % 3:
            ada_tile()
        return next(ws)

    f_pe, f_v = [None] * 2, [None] * 2
    for f in range(9):
        if f < 8:
            o = (f % 2) * 4 * T
            for j in range(4):
                w = ff_tile()
                for h in range(2):
                    bk = take_bank()
                    t = gemm(w, 8, xs(T), (h * 512, h * 512 + 512), bk, xk=xv)
                    i, q = q_slot()
                    bw(bk, A(q, bank[bk][:, :], AF.Relu, w=[t, qf[i], f_pe[f % 2]]))
                    v = V("tensor_tensor", q, q, q, ALU.mult, w=[act.t])
                    s_ = slice(o + j * T + h * 512, o + j * T + h * 512 + 512)
                    a = A(FH[:, s_], q, w=[v])
                    qf[i] = f_v[f % 2] = V("tensor_tensor", FL[:, s_], q, FH[:, s_].bitcast(F32), ALU.subtract, w=[a])
        if f:
            o = ((f - 1) % 2) * 4 * T
            for m in range(8):
                w = ff_tile()
                for h in range(2):
                    bk = take_bank()
                    t = gemm(w, 4, fx(o), (h * 512, h * 512 + 512), bk, xw=[f_v[(f - 1) % 2]])
                    rs = res[:, m * T + h * 512:m * T + h * 512 + 512]
                    bw(bk, V("tensor_tensor", rs, rs, bank[bk][:, :], ALU.add, w=[t]))
                    if f == 8:
                        sum_sq(m, h)
            f_pe[(f - 1) % 2] = t
    for q in range(2):
        V("scalar_tensor_tensor", cs_[:, q * 8:q * 8 + 8], mod[:, 8:16, q], 1.0, pr("norm1", 0, 8), ALU.add, ALU.mult)
    P.barrier()
    c2.close()
    c2 = ExitStack()
    FH, FL = sb("PH", 2 * T, F32R, c2), sb("PL", 2 * T, F32R, c2)
    pT = sb("pT", 2 * T, c=c2)
    tp = P.dma(sp, pT, I["pT"], s_x)
    xv = norm_x("g_ple")
    for h in range(4):
        hs = slice(h * 512, h * 512 + 512)
        a = A(FH[:, hs], pT[:, hs], w=[tp])
        pv = V("tensor_tensor", FL[:, hs], pT[:, hs], FH[:, hs].bitcast(F32), ALU.subtract, w=[a])
    for m in range(8):
        w = next(ws)
        bs = [take_bank(), take_bank()]
        ts = [gemm(w, 8, xs(T), (h * 512, h * 512 + 512), bs[h], xk=xv) for h in range(2)]
        w = next(ws)
        for h in range(2):
            i, q = q_slot()
            a = bw(bs[h], A(q, bank[bs[h]][:, :], AF.Tanh, scale=0.5, w=[ts[h], qf[i]]))
            bk = take_bank()
            t = gemm(w, 2, fx(0), (h * 512, h * 512 + 512), bk, xw=[pv])
            bw(bk, V("scalar_tensor_tensor", q, q, 1.0, bank[bk][:, :], ALU.add, ALU.mult, w=[a, t]))
            rs = res[:, m * T + h * 512:m * T + h * 512 + 512]
            qf[i] = V("scalar_tensor_tensor", rs, q, 0.5, rs, ALU.mult, ALU.add)
            sum_sq(m, h)
            sum_sq(m, h, ac2, pr("g_final", m))
    P.barrier()
    c2.close()
    c1.close()

    S = 1280
    c1, cX = ExitStack(), ExitStack()
    stg2 = sb("stg2", 2 * S, c=c1)
    con2[0] = sb("con2", NCON - NCON1, c=c1)
    XH, XL = sb("XH2", 8 * S, F32R, cX), sb("XL2", 8 * S, F32R, cX)
    P.dma(sp, con2[0], I["con"][:, NCON1:], s_par)
    c2 = ExitStack()
    hb_ = sb("hb_", 2 * T, c=c2)
    cx = sb("cx", 8 * 256, c=c2)
    rc_ = sb("rc_", 768, c=c2)
    rr_ = sb("rr_", T, c=c2)
    gc = sb("gc", 8, c=c2)
    P.dma(sp, cx, I["ctxT"], s_x)
    tc_ = V("tensor_tensor", gc, cs_[:, 0:8], pr("g_final", 0, 8), ALU.mult)
    th = []
    rstd_tail(acq, acq, 1024, T, (6, 7), dve.t, th)
    hxk = [[None, None] for _ in range(8)]
    hf = [None] * 4
    t2 = [None] * 2
    for h in range(2):
        hs = slice(h * 512, h * 512 + 512)
        rq = rr_[:, hs]
        V("tensor_tensor", rq, acq[:, hs], acq[:, hs], ALU.mult, w=[th[h]])
        p_ = mm(bank[4 + h][:, :], ones, ac2[:, hs], True, True, w=[bank_free[4 + h]], inc=True)
        bw(4 + h, V("scalar_tensor_tensor", rq, bank[4 + h][:, :], 1.0 / 1024, rq, ALU.mult, ALU.mult, w=[p_]))
        V("tensor_scalar", rq, rq, EPS, None, ALU.add)
        v = V("reciprocal", rq, rq)
        a = A(rq, rq, AF.Sqrt, w=[v])
        t2[h] = V("tensor_tensor", ac2[:, hs], rq, acq[:, hs], ALU.mult, w=[a])
    n = 0
    for h in range(2):
        for j in range(8):
            hs = slice(j * T + h * 512, j * T + h * 512 + 512)
            h_ = hb_[:, (n % 4) * 512:(n % 4) * 512 + 512]
            v = V("scalar_tensor_tensor", h_, res[:, hs], gc[:, j:j + 1], ac2[:, h * 512:h * 512 + 512], ALU.mult,
                  ALU.mult, w=[t2[h], hf[n % 4], tc_])
            o = j * S + h * 512
            a = A(XH[:, o:o + 512], h_, AF.Identity, bias=mod[:, j, 0:1], w=[v])
            hxk[j][h] = hf[n % 4] = V("scalar_tensor_tensor", XL[:, o:o + 512], h_, mod[:, j, 0:1],
                                      XH[:, o:o + 512].bitcast(F32), ALU.add, ALU.subtract, w=[a])
            n += 1
    s_ri = [[P.slot(f"r{i}_{k}") for k in range(5)] for i in range(2)]

    v_tok, ctx_t = {}, [None]

    def stream_g2():
        for n_ in range(29):
            w = next(ws)
            m = order[n_]
            i = n_ % 2
            dst = stg2[:, i * S:(i + 1) * S]
            es = []
            segs = [(0, 512), (512, 1024)] + ([(1024, 1280)] if m < 7 or 13 <= m < 21 else [])
            for h, (a, b_) in enumerate(segs):
                bk = h % 2
                yield from gemm_steps(w, 8, xs(S), (a, b_), bk, xk=hxk if n_ == 0 and h < 2 else None,
                                      xw=[ctx_t[0]] if h == 2 else [])
                e = bank_free[bk] = evac(dst[:, a:b_], bank[bk][:, 0:b_ - a], [W["gemm"], s_st[i].t])
                es.append(e)
                yield
            n = segs[-1][1]
            v_tok[m] = P.dma(sp, D_v[m][:, 0:n], dst[:, 0:n], s_st[i], es)

    def needv(*ms):
        pull(v_tok, ms)
        return [v_tok[m] for m in ms]

    def head_out(h, o_, rr, sq_, gt_, gain, mean, gidx, slot, dslot, tg=None):
        if mean:
            for k in range(2):
                b = B_S[1][k]
                hs = slice(k * 512, k * 512 + 512)
                t = mm(bank[b][:, :], ones, o_[:, hs], True, True, w=[dve.t, bank_free[b]], inc=True)
                bw(b, V("scalar_tensor_tensor", o_[:, hs], bank[b][:, :], -1.0 / 128, o_[:, hs], ALU.mult, ALU.add, w=[t]))
            yield
        t = A(sq_, o_, AF.Square, w=[dve.t, pe.t])
        yield
        t = rstd_tail(sq_, rr, 128, T, B_S[1], t)
        yield
        V("scalar_tensor_tensor", o_, o_, gain, rr, ALU.mult, ALU.mult, w=[t])
        if tg is None:
            tg = P.dma(pool, gt_, D_v[gidx][:, 0:T], slot, [dve.t, *needv(gidx)])
        a = A(sq_, gt_, AF.Tanh, scale=0.5, w=[tg, dve.t])
        V("scalar_tensor_tensor", sq_, sq_, 1.0, gt_, ALU.add, ALU.mult, w=[a])
        v = V("scalar_tensor_tensor", o_, o_, 0.5, sq_, ALU.mult, ALU.mult)
        P.dma(pool, D_o[h], o_, dslot, [v])

    def v3(a, n=128):
        return a.rearrange("p (c i) -> p c i", i=n)

    def mixer_gla(c):
        q_, k_ = c("gq", T), c("gk", S)
        vN = c("gvN", 10 * 256)
        b_ = c("gb", S)
        qJ = c("gqJ", 4 * T)
        kp, ke, keN = c("gkp", T), c("gke", S), c("gkeN", S)
        qe = c("gqe", T)
        Ss = c("gSs", 8 * 128)
        ST = c("gST", 2 * 512)
        o2 = aq2
        gw = stg[:, 0:512]
        sm = stg[:, 512:560]
        P.dma(pool, gw[0:32, :], I["gla_gw"], s_m[0])
        for rc in range(2):
            P.dma(pool, q_, D_v[7 + rc][:, 0:T], s_m[1], [dve.t, pe.t, act.t, *needv(7 + rc)])
            P.dma(pool, k_, D_v[1 + rc], s_m[2], [dve.t, *needv(1 + rc)])
            for a in range(2):
                t = P.dma(pool, ke, D_v[3 + 2 * rc + a], s_m[3], [dve.t, pe.t, *needv(3 + 2 * rc + a)])
                for c0_ in range(0, 10, 4):
                    b = 6 + (c0_ // 4) % 2
                    n = min(4, 10 - c0_)
                    for cc in range(c0_, c0_ + n):
                        p_ = tr(bank[b][:, (cc - c0_) * 128:(cc - c0_) * 128 + 128], ke[:, cc * 128:cc * 128 + 128], ident,
                                w=[t, bank_free[b]] if cc == c0_ else (), inc=cc == c0_ + n - 1)
                    bw(b, A(vN.rearrange("p (c x) -> p c x", c=10)[:, c0_:c0_ + n, a * 128:a * 128 + 128],
                            v3(bank[b][:, 0:n * 128]), w=[p_]))
            yield
            V("tensor_scalar", q_, q_, 0.125, None, ALU.mult, w=[s_m[1].t])
            for d in range(2):
                gz = qJ[0:32, 0:S]
                tz = P.dma(pool, gz, D_v[0][0:32, :], s_m[4], [dve.t, pe.t, act.t, *needv(0)])
                for h, (a0, a1) in enumerate(((0, 512), (512, 1024), (1024, 1280))):
                    b = (2, 3, 4)[h]
                    p_ = mm(bank[b][:, 0:a1 - a0], gw[0:32, (2 * d + rc) * 128:(2 * d + rc) * 128 + 128],
                            gz[:, a0:a1], True, True, w=[tz, s_m[0].t, bank_free[b]], inc=True)
                    bw(b, A(b_[:, a0:a1], bank[b][:, 0:a1 - a0], AF.Identity, bias=pr("gate_b", 2 * d + rc), w=[p_, dve.t]))
                A(ke, b_, AF.Abs)
                A(ke, ke, AF.Exp, scale=-1.0)
                a = A(ke, ke, AF.Ln, bias=1.0)
                V("tensor_scalar", b_, b_, 0.0, None, ALU.min, w=[a])
                V("tensor_tensor", b_, b_, ke, ALU.subtract)
                V("tensor_scalar", keN, b_, 1.0 / 16, None, ALU.mult, w=[pe.t])
                for cc in range(10):
                    lo, hi = cc * 128, cc * 128 + 128
                    sl = slice(lo, hi) if d == 0 else slice(hi - 1, lo - 1 if lo else None, -1)
                    V("tensor_tensor_scan", b_[:, sl], keN[:, sl], keN[:, sl], 0.0, ALU.add, ALU.bypass)
                yield
                eo = 127 if d == 0 else 0
                ro = 15 if d == 0 else 16
                b3_ = v3(b_)
                bend = b3_[:, :, eo:eo + 1]
                V("tensor_tensor", v3(ke), b3_, bend.broadcast_to([128, 10, 128]), ALU.subtract)
                a = A(ke, ke, AF.Exp, scale=-1.0, w=[dve.t])
                aend = sm[:, d * 16:d * 16 + 10]
                A(aend.unsqueeze(2), bend, AF.Exp)
                v = V("tensor_tensor", ke, ke, k_, ALU.mult, w=[a, s_m[2].t])
                for c0_ in range(0, 10, 4):
                    b = 6 + (c0_ // 4) % 2
                    n = min(4, 10 - c0_)
                    for cc in range(c0_, c0_ + n):
                        p_ = tr(bank[b][:, (cc - c0_) * 128:(cc - c0_) * 128 + 128], ke[:, cc * 128:cc * 128 + 128], ident,
                                w=[v, bank_free[b]] if cc == c0_ else (), inc=cc == c0_ + n - 1)
                    bw(b, A(keN[:, c0_ * 128:(c0_ + n) * 128], bank[b][:, 0:n * 128], w=[p_, dve.t]))
                for J in range(4):
                    V("tensor_tensor", v3(qJ[:, J * T:(J + 1) * T]), b3_[:, 0:8, :],
                      b3_[:, 0:8, 32 * J + ro:32 * J + ro + 1].broadcast_to([128, 8, 128]), ALU.subtract, w=[pe.t])
                    V("tensor_scalar", qJ[:, J * T:(J + 1) * T], qJ[:, J * T:(J + 1) * T], 40.0, None, ALU.min)
                a = A(qJ, qJ, AF.Exp, w=[dve.t])
                kb = b_[:, 0:T].rearrange("p (m i) -> p m i", i=32)
                V("tensor_tensor", kp.rearrange("p (m i) -> p m i", i=32), kb,
                  kb[:, :, ro:ro + 1].broadcast_to([128, 32, 32]), ALU.subtract, w=[pe.t])
                v = V("tensor_scalar", kp, kp, -40.0, None, ALU.max)
                A(kp, kp, AF.Exp, scale=-1.0, w=[v])
                a2 = A(qe, b_[:, 0:T], AF.Exp, w=[v, pe.t])
                V("tensor_tensor", qJ.rearrange("p (j t) -> p j t", j=4), qJ.rearrange("p (j t) -> p j t", j=4),
                  q_.unsqueeze(1).broadcast_to([128, 4, T]), ALU.mult, w=[a])
                V("tensor_tensor", kp, kp, k_[:, 0:T], ALU.mult, w=[a2])
                vq = V("tensor_tensor", qe, qe, q_, ALU.mult)
                yield
                order = ([8, 9] + list(range(7))) if d == 0 else ([9, 8] + list(range(7, 0, -1)))
                nxt_of = {8: 9, 9: 0} if d == 0 else {9: 8, 8: 7}
                tmpS = ST[:, 0:128]
                tmpS2 = ST[:, 128:256]
                prev = None
                for n0 in range(0, 9, 4):
                    b = 6 + (n0 // 4) % 2
                    m_ = min(4, 9 - n0)
                    for n in range(n0, n0 + m_):
                        cc = order[n]
                        for a in range(2):
                            p_ = mm(bank[b][a * 64:a * 64 + 64, (n - n0) * 128:(n - n0) * 128 + 128],
                                    keN[:, cc * 128 + a * 64:cc * 128 + a * 64 + 64],
                                    vN[:, cc * 256 + a * 128:cc * 256 + a * 128 + 128], True, True,
                                    w=[act.t, bank_free[b]] if n == n0 and a == 0 else (),
                                    inc=n == n0 + m_ - 1 and a == 1)
                    for n in range(n0, n0 + m_):
                        cc = order[n]
                        if n == 0:
                            dstS = tmpS
                        elif n == 1:
                            i0 = 0 if d == 0 else 7
                            dstS = Ss[:, i0 * 128:i0 * 128 + 128]
                        else:
                            i0 = cc + 1 if d == 0 else cc - 1
                            dstS = Ss[:, i0 * 128:i0 * 128 + 128]
                        u_ = bank[b][:, (n - n0) * 128:(n - n0) * 128 + 128]
                        if n == 0:
                            V("tensor_copy", dstS, u_, w=[p_])
                        else:
                            V("scalar_tensor_tensor", dstS, prev, aend[:, cc:cc + 1], u_, ALU.mult, ALU.add, w=[p_])
                        prev = dstS
                    bw(b, dve.t)
                tS = dve.t
                yield
                mask = cn("mle") if d == 0 else cn("mge")
                stt_ = [None, None]
                for a in range(2):
                    rs = slice(a * 64, a * 64 + 64)
                    for k in range(2):
                        b = B_S[0][k]
                        for cc in range(4 * k, 4 * k + 4):
                            for J in range(4):
                                p_ = mm(bank[b][32 * J:32 * J + 32, (cc % 4) * 128:(cc % 4) * 128 + 128],
                                        kp[rs, cc * 128 + 32 * J:cc * 128 + 32 * J + 32],
                                        qJ[rs, J * T + cc * 128:J * T + cc * 128 + 128], True, True,
                                        w=[vq, bank_free[b]] if cc % 4 == 0 and J == 0 else (), inc=cc % 4 == 3 and J == 3)
                        sv = bw(b, V("tensor_tensor", v3(ST[:, k * 512:k * 512 + 512]), v3(bank[b][:, :]),
                                     mask.unsqueeze(1).broadcast_to([128, 4, 128]), ALU.mult, w=[p_, stt_[k]]))
                        b = B_S[1][k]
                        for cc in range(4 * k, 4 * k + 4):
                            reg = bank[b][:, (cc % 4) * 128:(cc % 4) * 128 + 128]
                            mm(reg, vN[:, cc * 256 + a * 128:cc * 256 + a * 128 + 128],
                               ST[:, cc * 128:cc * 128 + 128], True, False, w=[sv, bank_free[b], tS])
                            p_ = mm(reg, Ss[rs, cc * 128:cc * 128 + 128], qe[rs, cc * 128:cc * 128 + 128], False, True,
                                    inc=cc % 4 == 3)
                        stt_[k] = p_
                        dst = o2[:, a * T + k * 512:a * T + k * 512 + 512]
                        if d == 0:
                            bw(b, V("tensor_copy", dst, bank[b][:, :], w=[p_, s_m[5].t]))
                        else:
                            bw(b, V("tensor_tensor", dst, dst, bank[b][:, :], ALU.add, w=[p_]))
                    yield
            for a in range(2):
                h = 2 * rc + a
                yield from head_out(h, o2[:, a * T:(a + 1) * T], kp, qe, ke[:, 0:T], pr("gla_norm", h), False, 9 + h, s_m[3], s_m[5])
                pool.wait([s_m[5].t])
                yield

    def mixer_ret(c):
        rC, rS = c("rC", T), c("rS", T)
        lg = c("rlg", 48)
        P.dma(pool, rC, I["rope2"][0], s_m[0])
        P.dma(pool, rS, I["rope2"][1], s_m[0])
        V("tensor_scalar", lg[:, 0:8], pr("ret_logit", 0, 8), -1.0, None, ALU.mult)
        log1p_exp(lg[:, 0:8], lg[:, 8:16], lg[:, 16:24], lg[:, 24:32], lg[:, 0:8])
        V("tensor_scalar", lg[:, 0:8], lg[:, 0:8], -1.0, None, ALU.mult)
        A(lg[:, 8:16], lg[:, 0:8], AF.Exp, scale=128.0, w=[dve.t])
        for d, nm in enumerate(("colf", "colb")):
            V("tensor_scalar", lg[:, 16 + 4 * d:20 + 4 * d], lg[:, 4 * d:4 * d + 4], cn(nm), None, ALU.mult)
        A(lg[:, 16:24], lg[:, 16:24], AF.Exp, w=[dve.t])
        runs = [ret_heads(c, i, rC, rS, lg) for i in range(2)]
        next(runs[1])
        for _ in range(2):
            next(runs[0])
        while runs:
            for g_ in list(runs):
                if next(g_, "end") == "end":
                    runs.remove(g_)

    def ret_heads(c, inst, rC, rS, lg):
        nm_ = f"r{inst}"
        q_, k_ = c(nm_ + "q", T), c(nm_ + "k", S)
        keN = [c(nm_ + f"ke{d}", S) for d in range(2)]
        vN, kN = c(nm_ + "vN", S), c(nm_ + "kN", S)
        qe = [c(nm_ + f"qe{d}", T) for d in range(2)]
        Ss = [c(nm_ + f"Ss{d}", T) for d in range(2)]
        tm = c(nm_ + "tm", S)
        Dm = c(nm_ + "Dm", 128 * 4)
        o_, ST = (acq, ac2) if inst else (c(nm_ + "o", T), c(nm_ + "ST", T))
        s_n = s_ri[inst]
        loc = []
        tq = P.dma(pool, q_, D_v[21 + inst][:, 0:T], s_n[0])
        tk = P.dma(pool, k_, D_v[13 + inst], s_n[1])
        tv = P.dma(pool, tm, D_v[17 + inst], s_n[2])
        yield
        for h in (inst, inst + 2):

            def turn(src, dst, w):
                for c0_ in range(0, 10, 4):
                    b = 6 + (c0_ // 4) % 2
                    n = min(4, 10 - c0_)
                    for cc in range(c0_, c0_ + n):
                        p_ = tr(bank[b][:, (cc - c0_) * 128:(cc - c0_) * 128 + 128], src[:, cc * 128:cc * 128 + 128], ident,
                                w=[w, bank_free[b]] if cc == c0_ else (), inc=cc == c0_ + n - 1)
                    bw(b, A(dst[:, c0_ * 128:(c0_ + n) * 128], bank[b][:, 0:n * 128], w=[p_, *loc]))
                return p_, act.t

            pv_, av_ = turn(tm, vN, tv)
            yield
            for d, (rel, mk) in enumerate((("relf", "mle"), ("relb", "mge"))):
                a = A(Dm[:, d * 128:d * 128 + 128], cn(rel), AF.Exp, scale=lg[:, 4 * d + h:4 * d + h + 1], w=loc)
                V("tensor_tensor", Dm[:, d * 128:d * 128 + 128], Dm[:, d * 128:d * 128 + 128], cn(mk), ALU.mult, w=[a])
                A(Dm[:, 256 + d * 128:384 + d * 128], cn("posf" if d == 0 else "posb"), AF.Exp,
                  scale=lg[:, 4 * d + h:4 * d + h + 1])
            V("tensor_tensor", Dm[:, 0:128], Dm[:, 0:128], Dm[:, 128:256], ALU.add)
            sw = tm[:, 0:T]
            dve.wait([s_m[0].t, tq, tk, pv_])
            for x_, sc in ((q_, 1.0), (k_, 128.0 ** -0.5)):
                xx = x_[:, 0:T]
                V("tensor_tensor", sw[0:64, :], xx[64:128, :], rS[64:128, :], ALU.mult)
                V("tensor_tensor", sw[64:128, :], xx[0:64, :], rS[0:64, :], ALU.mult)
                V("tensor_tensor", xx, xx, rC, ALU.mult)
                V("tensor_tensor", xx, xx, sw, ALU.add)
                yield
            v = V("tensor_scalar", k_, k_, 128.0 ** -0.5, None, ALU.mult)
            tg = P.dma(pool, tm[:, 0:T], D_v[25 + h][:, 0:T], s_n[3], [v])
            yield
            _, ak_ = turn(k_, kN, v)
            yield
            for d in range(2):
                V("tensor_scalar", keN[d], kN, lg[:, 16 + 4 * d + h:17 + 4 * d + h], None, ALU.mult, w=[ak_, *loc])
                V("tensor_tensor", v3(qe[d]), v3(q_), Dm[:, 256 + d * 128:384 + d * 128].unsqueeze(1).broadcast_to([128, 8, 128]),
                  ALU.mult)
            vk = dve.t
            yield
            orders = ([8, 9] + list(range(7)), [9, 8] + list(range(7, 0, -1)))
            prev = [None, None]
            for n0 in range(0, 9, 4):
                m_ = min(4, 9 - n0)
                for d in range(2):
                    b = 6 + d
                    for n in range(n0, n0 + m_):
                        cc = orders[d][n]
                        p_ = mm(bank[b][:, (n - n0) * 128:(n - n0) * 128 + 128], keN[d][:, cc * 128:cc * 128 + 128],
                                vN[:, cc * 128:cc * 128 + 128], True, True, w=[vk, bank_free[b]] if n == n0 else (),
                                inc=n == n0 + m_ - 1)
                    for n in range(n0, n0 + m_):
                        cc = orders[d][n]
                        u_ = bank[b][:, (n - n0) * 128:(n - n0) * 128 + 128]
                        if n == 0:
                            dstS = ST[:, d * 128:d * 128 + 128]
                            V("tensor_copy", dstS, u_, w=[p_])
                        else:
                            i0 = (0 if d == 0 else 7) if n == 1 else (cc + 1 if d == 0 else cc - 1)
                            dstS = Ss[d][:, i0 * 128:i0 * 128 + 128]
                            V("scalar_tensor_tensor", dstS, prev[d], lg[:, 8 + 4 * d + h:9 + 4 * d + h], u_, ALU.mult,
                              ALU.add, w=[p_])
                        prev[d] = dstS
                    bw(b, dve.t)
                yield
            for k in range(2):
                b = B_S[0][k]
                for cc in range(4 * k, 4 * k + 4):
                    p_ = mm(bank[b][:, (cc % 4) * 128:(cc % 4) * 128 + 128], k_[:, cc * 128:cc * 128 + 128],
                            q_[:, cc * 128:cc * 128 + 128], True, True, w=[bank_free[b]] if cc % 4 == 0 else (),
                            inc=cc % 4 == 3)
                sv = bw(b, V("tensor_tensor", v3(ST[:, k * 512:k * 512 + 512]), v3(bank[b][:, :]),
                             Dm[:, 0:128].unsqueeze(1).broadcast_to([128, 4, 128]), ALU.mult, w=[p_]))
                b = B_S[1][k]
                for cc in range(4 * k, 4 * k + 4):
                    reg = bank[b][:, (cc % 4) * 128:(cc % 4) * 128 + 128]
                    cs3 = slice(cc * 128, cc * 128 + 128)
                    mm(reg, vN[:, cs3], ST[:, cs3], True, False, w=[sv, bank_free[b]])
                    mm(reg, Ss[0][:, cs3], qe[0][:, cs3], False, False)
                    p_ = mm(reg, Ss[1][:, cs3], qe[1][:, cs3], False, True, inc=cc % 4 == 3)
                bw(b, V("tensor_copy", o_[:, k * 512:k * 512 + 512], bank[b][:, :], w=[p_, s_n[4].t]))
                yield
            if h < 2:
                tq = P.dma(pool, q_, D_v[23 + h][:, 0:T], s_n[0], [p_])
                tk = P.dma(pool, k_, D_v[15 + h], s_n[1], [p_])
            yield from head_out(4 + h, o_, qe[0], qe[1], tm[:, 0:T], pr("ret_norm", h), True, 25 + h, s_n[3], s_n[4], tg)
            loc = [dve.t, pe.t, act.t]
            if h < 2:
                tv = P.dma(pool, tm, D_v[19 + h], s_n[2], [dve.t])
            yield

    P.filler = stream_g2()
    pull(v_tok, (7,))
    P.filling = True

    def more(n):
        for _ in range(n):
            if 11 not in v_tok:
                next(P.filler, None)

    for j in range(8):
        cj = cx[:, j * 256:(j + 1) * 256]
        if j == 0:
            t = A(rc_[:, 0:256], cj, AF.Square, w=[s_x.t])
        else:
            a = A(rc_[:, 256:512], cj, AF.Square, w=[dve.t])
            t = V("tensor_tensor", rc_[:, 0:256], rc_[:, 0:256], rc_[:, 256:512], ALU.add, w=[a])
    t = rstd_tail(rc_[:, 0:256], rc_[:, 512:768], 1024, 256, (4, 5), t)
    for j in range(8):
        cj = cx[:, j * 256:(j + 1) * 256]
        more(2)
        V("scalar_tensor_tensor", cj, cj, cs_[:, 8 + j:9 + j], rc_[:, 512:768], ALU.mult, ALU.mult, w=[t])
        v = V("tensor_scalar", cj, cj, mod[:, j, 1:2], None, ALU.add)
        ctx_t[0] = split_x((j * S + T, j * S + S), cj, w=[v])
    for j in range(8):
        more(3)
        xj = res[:, j * T:(j + 1) * T]
        v = V("scalar_tensor_tensor", xj, xj, pr("g_final", j), acq, ALU.mult, ALU.mult)
        P.dma(sp, D_xb[j], xj, s_ld[j % 4], [v, s_ld[j % 4].t])
    P.filling = False
    P.barrier()
    c2.close()
    c = ExitStack()
    for _ in mixer_gla(Region(c)):
        pass
    needv(28)
    P.barrier()
    c.close()
    cX.close()
    c = ExitStack()
    mixer_ret(Region(c))
    P.barrier()
    c.close()
    if P.filler is not None:
        rest, P.filler = P.filler, None
        for _ in rest:
            pass
    P.barrier()

    V("scalar_tensor_tensor", cs_[:, 16:24], mod[:, 32:40, 0], 1.0, pr("norm2", 0, 8), ALU.add, ALU.mult)
    v = V("tensor_copy", cf[:, 0:8], mod[:, 40:48, 0])
    p_ = tr(bank[0][0:8, 0:128], cf[:, 0:8], ident, w=[v, bank_free[0]], inc=True)
    v = bank_free[0] = V("tensor_copy", ac2[0:8, 0:128], bank[0][0:8, 0:128], w=[p_])
    P.dma(sp, D_m5.rearrange("o (a b) -> (o a) b", a=8), ac2[0:8, 0:128], s_x, [v])
    c1.close()
    c1, c2 = ExitStack(), ExitStack()
    er = sb("ER", 3072, c=c1)
    XH, XL = sb("XH3", 8 * T, F32R, c2), sb("XL3", 8 * T, F32R, c2)
    h2 = sb("h2", 8 * T, c=c2)
    NR, NS = 4, 4
    s_e = [P.slot(f"e{i}") for i in range(NR)]
    ER = [er] + [res[:, i * 3072:(i + 1) * 3072] for i in range(2)] + [WR]
    pieces = []
    for e in range(16):
        for q in range(4):
            n = 384 if q < 3 else 256
            pieces += [(e, 0, q, 8 * n), (e, 1, q, 8 * n)]
        pieces += [(e, 2, q, 11 * 256) for q in range(4)]
    p_raw, p_spl = [None] * NR, [None] * NS
    p_tok = {}

    def e_load(n):
        e, kind, q, size = pieces[n]
        i = n % NR
        src = I[("wg", "wu", "wd")[kind]][e]
        off = q * 8 * 384 if kind < 2 else q * 11 * 256
        p_tok[n] = P.dma(sp, ER[i][:, 0:size], src[:, off:off + size], s_e[i], [*(p_raw[i] or [])])

    o_t = []
    for j in range(8):
        o_t.append(P.dma(pool, h2[:, j * T:(j + 1) * T], D_o[j], s_m[j % 4], [s_m[j % 4].t]))
    xv = [[None, None] for _ in range(8)]
    for h in range(2):
        for j in range(8):
            o = j * T + h * 512
            xv[j][h] = split_x((o, o + 512), h2[:, o:o + 512], w=[o_t[j]], pool_lo=j % 2 == 1)
    for m in range(8):
        w = next(ws)
        if m == 0:
            for j in range(8):
                P.dma(act, res[:, j * T:(j + 1) * T], D_xb[j], s_ld[0])
        for h in range(2):
            bk = take_bank()
            t = gemm(w, 8, xs(T), (h * 512, h * 512 + 512), bk, xk=xv)
            rs = res[:, m * T + h * 512:m * T + h * 512 + 512]
            bw(bk, V("scalar_tensor_tensor", rs, bank[bk][:, :], mod[:, 16 + m, 0:1], rs, ALU.mult, ALU.add,
                     w=[t, s_ld[0].t]))
            sum_sq(m, h)
    next(ws, None)
    orw, wr_ = WR[:, 0:2 * T], WR[:, 2 * T:2 * T + 128]
    o_w = [x_ for f_ in W["raw_free"] for x_ in f_]
    P.dma(sp, wr_, I["w_router"], s_ld[1], o_w)
    e_load(0)
    xt2 = dve.t

    def turn_out(src, dram, w, slots):
        for tc in range(8):
            i = tc % 2
            for q in range(2):
                bk = take_bank()
                for j in range(4):
                    p_ = tr(bank[bk][:, j * 128:j * 128 + 128],
                            src[:, (4 * q + j) * T + tc * 128:(4 * q + j) * T + tc * 128 + 128], ident,
                            w=[w, bank_free[bk]] if j == 0 else (), inc=j == 3)
                e = bw(bk, A(orw[:, i * T + q * 512:i * T + q * 512 + 512], bank[bk][:, :], w=[p_, slots[i].t, *o_w]))
            P.dma(sp, dram[tc * 128:tc * 128 + 128, :], orw[:, i * T:(i + 1) * T], slots[i], [e])

    t = rstd_tail(acq, acq, 1024, T, (6, 7), dve.t)
    lb = [take_bank(), take_bank()]
    for j in range(8):
        xj, hj = res[:, j * T:(j + 1) * T], h2[:, j * T:(j + 1) * T]
        v = V("scalar_tensor_tensor", hj, xj, cs_[:, 16 + j:17 + j], acq, ALU.mult, ALU.mult, w=[t, pe.t] if j == 0 else ())
        hv = A(hj, hj, AF.Identity, bias=mod[:, 24 + j, 0:1], w=[v])
        for h in range(2):
            p_ = mm(bank[lb[h]][0:16, :], wr_[:, j * 16:j * 16 + 16], hj[:, h * 512:h * 512 + 512], j == 0, j == 7,
                    w=[hv, bank_free[lb[h]], s_ld[1].t], inc=True)
    lgt = stg[0:16, T:2 * T]
    for h in range(2):
        v = bw(lb[h], V("tensor_copy", lgt[:, h * 512:h * 512 + 512], bank[lb[h]][0:16, :], w=[p_, act.t]))
    b = take_bank()
    for tc in range(8):
        p_ = tr(bank[b][:, tc * 16:tc * 16 + 16], lgt[:, tc * 128:tc * 128 + 128], ident[0:16, 0:16],
                w=[v, bank_free[b]] if tc == 0 else (), inc=tc == 7)
    af = stg[:, 0:128]
    l3 = bank[b][:, 0:128].rearrange("p (c e) -> p c e", e=16)
    a3 = af.rearrange("p (c e) -> p c e", e=16)
    mx = stg[:, 128:136]
    V("tensor_reduce", mx, l3, AX.X, ALU.max, w=[p_, act.t])
    bw(b, V("tensor_tensor", a3, l3, b3(mx, 16), ALU.subtract))
    a = A(af, af, AF.Exp, w=[dve.t])
    V("tensor_reduce", mx, a3, AX.X, ALU.add, w=[a])
    V("reciprocal", mx, mx)
    v = V("tensor_tensor", a3, a3, b3(mx, 16), ALU.mult)
    affT = stg[0:16, T:2 * T]
    for k in range(2):
        b = take_bank()
        for j in range(4):
            p_ = tr(bank[b][0:16, j * 128:j * 128 + 128], af[:, (4 * k + j) * 16:(4 * k + j) * 16 + 16], ident,
                    w=[v, bank_free[b]] if j == 0 else (), inc=j == 3)
        bw(b, V("tensor_copy", affT[:, k * 512:k * 512 + 512], bank[b][0:16, :], w=[p_]))
    turn_out(h2, D_h, hv, s_ld[2:4])
    turn_out(res, D_acc, xt2, s_ld[2:4])
    tr_res = pe.t
    gv_, ix, ixf = stg[0:16, 256:384], stg[0:16, 384:512].bitcast(U32), stg[0:16, 512:640]
    for rd in range(16):
        g8 = gv_[:, rd * 8:rd * 8 + 8]
        V("max", g8, affT)
        V("max_index", ix[:, rd * 8:rd * 8 + 8], g8, affT)
        V("match_replace", affT, g8, affT, -1.0)
    V("tensor_copy", ixf, ix)
    p_raw[1] = p_raw[2] = [tr_res]
    p_raw[3] = [s_ld[2].t, s_ld[3].t]
    for n in range(1, NR):
        e_load(n)
    P.barrier(but=s_e)
    c2.close()

    gT = sb("gT", 16, c=c1)
    iT = sb("iT", 16, U32, c=c1)
    fnw, m5 = acq, ac2
    XEH, XEL = WH, WL
    HH, HL = sb("HH", 1408, F32R, c1), sb("HL", 1408, F32R, c1)
    EH, EL = sb("EH", NS * 3072, F32R, c1), sb("EL", NS * 3072, F32R, c1)
    xe = res[:, 6 * T:8 * T]
    ye = stg[:, T:2 * T]
    hN = stg[:, 0:2 * 384]
    s_g = [P.slot(f"g{i}") for i in range(2)]
    s_acc, s_mf = P.slot("acc"), P.slot("mf")
    b = take_bank()
    tr(bank[b][:, 0:16], gv_, ident[0:16, 0:16], w=[bank_free[b]])
    p_ = tr(bank[b][:, 16:32], ixf, ident[0:16, 0:16], inc=True)
    V("tensor_copy", gT, bank[b][:, 0:16], w=[p_])
    tix = bw(b, V("tensor_copy", iT, bank[b][:, 16:32]))

    def e_split(n):
        size = pieces[n][3]
        i, j = n % NR, n % NS
        raw = ER[i][:, 0:size]
        hi, lo = (t_[:, j * 3072:j * 3072 + size] for t_ in (EH, EL))
        cut = int(size * 0.45) // 128 * 128
        c_, d_ = slice(0, cut), slice(cut, size)
        a = A(hi[:, d_], raw[:, d_], w=[p_tok[n], p_spl[j]])
        g = G("tensor_tensor", lo[:, d_], raw[:, d_], hi[:, d_].bitcast(F32), ALU.subtract, w=[a])
        a = A(hi[:, c_], raw[:, c_])
        v = V("tensor_tensor", lo[:, c_], raw[:, c_], hi[:, c_].bitcast(F32), ALU.subtract, w=[a])
        p_raw[i] = [a, v, g]
        return [v, g]

    P.dma(act, fnw[:, :], I["fnorm"].broadcast_to([128, 1024]), s_mf)
    P.dma(act, m5[:, :], D_m5.broadcast_to([128, 1024]), s_mf)

    g_tok, xe_free, x_tok = {}, [None] * 2, {}

    def gather(e):
        g_tok[e] = P.idma(s_g[e % 2], [tix, xe_free[e % 2]], out=xe[:, (e % 2) * 1024:(e % 2 + 1) * 1024],
                          out_offset=None, in_=D_h[:, :],
                          in_offset=bass.IndirectOffsetOnAxis(ap=iT[:, e:e + 1], axis=0))

    xh_pe = [None] * 2

    def turn_x(e):
        i = e % 2
        for q in range(2):
            b = 6 + q
            for j in range(4):
                p_ = tr(bank[b][:, j * 128:j * 128 + 128],
                        xe[:, i * 1024 + (4 * q + j) * 128:i * 1024 + (4 * q + j) * 128 + 128], ident,
                        w=[g_tok[e], bank_free[b]] if j == 0 else (), inc=j == 3)
            s_ = slice(i * 1024 + q * 512, i * 1024 + q * 512 + 512)
            a = A(XEH[:, s_], bank[b][:, :], w=[p_, xh_pe[i]])
            v = bw(b, V("tensor_tensor", XEL[:, s_], bank[b][:, :], XEH[:, s_].bitcast(F32), ALU.subtract, w=[a]))
        xe_free[i] = p_
        x_tok[e] = v

    pend = []

    def egemm(n, b, col, width, K, L, ltok, at, late=()):
        j = n % NS
        for k in range(K):
            while pend and k == at:
                pend.pop(0)()
            lh, ll = L(k)
            rh = EH[:, j * 3072 + k * width:j * 3072 + (k + 1) * width]
            rl = EL[:, j * 3072 + k * width:j * 3072 + (k + 1) * width]
            mm(bank[b][:, col:col + width], lh, rh, k == 0, False, w=[*ltok, bank_free[b]] if k == 0 else late() if k == 9 else ())
            mm(bank[b][:, col:col + width], lh, rl, False, False)
            p_ = mm(bank[b][:, col:col + width], ll, rh, False, k == K - 1, inc=k == K - 1)
        p_spl[j] = p_
        return p_

    gather(0)
    gather(1)
    turn_x(0)
    sp_tok = {n: e_split(n) for n in range(NS - 1)}
    for n in range(NR, NR + NS - 1):
        e_load(n)
    hh_pe = None
    hn_free = [None] * 2
    h_tok = [None]
    y_free = None
    NP_ = len(pieces)
    for n in range(NP_):
        e, kind, q, size = pieces[n]
        if n + NS - 1 < NP_:
            sp_tok[n + NS - 1] = e_split(n + NS - 1)
        if n + NS - 1 + NR < NP_:
            e_load(n + NS - 1 + NR)
        i = e % 2
        if kind < 2:
            w_ = 384 if q < 3 else 256
            b = 2 * (q % 2) + kind
            t = egemm(n, b, 0, w_, 8, lambda k: (XEH[:, i * 1024 + k * 128:i * 1024 + k * 128 + 128],
                                                 XEL[:, i * 1024 + k * 128:i * 1024 + k * 128 + 128]),
                      [*sp_tok[n], x_tok[e]], 4)
            if kind == 0:
                ta = t
            else:
                if q == 3:
                    xh_pe[i] = t
                hn = hN[:, (q % 2) * 384:(q % 2) * 384 + w_]
                a = A(hn, bank[b - 1][:, 0:w_], AF.Tanh, scale=0.5, w=[ta, hn_free[q % 2], dve.t])
                v = V("scalar_tensor_tensor", hn, hn, 1.0, bank[b - 1][:, 0:w_], ALU.add, ALU.mult, w=[a])
                bw(b - 1, v)
                v = bw(b, V("scalar_tensor_tensor", hn, hn, 0.5, bank[b][:, 0:w_], ALU.mult, ALU.mult, w=[t]))

                def turn_h(q=q, w_=w_, v=v, hn=hn, hh_pe=hh_pe):
                    bt = 4 + q % 2
                    for j in range(w_ // 128):
                        p_ = tr(bank[bt][:, j * 128:j * 128 + 128], hn[:, j * 128:j * 128 + 128], ident,
                                w=[v, bank_free[bt]] if j == 0 else (), inc=j == w_ // 128 - 1)
                    hn_free[q % 2] = p_
                    s_ = slice(q * 384, q * 384 + w_)
                    a = A(HH[:, s_], bank[bt][:, 0:w_], w=[p_, hh_pe])
                    h_tok[0] = bw(bt, V("tensor_tensor", HL[:, s_], bank[bt][:, 0:w_], HH[:, s_].bitcast(F32),
                                        ALU.subtract, w=[a]))

                pend.append(turn_h)
        else:
            if q == 2 and e + 1 < 16:
                turn_x(e + 1)
                if e + 2 < 16:
                    gather(e + 2)
            b = 4 + q % 2
            t = egemm(n, b, 0, 256, 11, lambda k: (HH[:, k * 128:k * 128 + 128], HL[:, k * 128:k * 128 + 128]),
                      [*sp_tok[n], h_tok[0]], 7, lambda: [h_tok[0]])
            if q == 3:
                hh_pe = t
            v = bw(b, V("scalar_tensor_tensor", ye[:, q * 256:q * 256 + 256], bank[b][:, 0:256], gT[:, e:e + 1],
                        m5[:, q * 256:q * 256 + 256], ALU.mult, ALU.mult, w=[t, y_free, s_mf.t]))
            if q == 3:
                y_free = P.idma(s_acc, [v, s_acc.t], out=D_acc[:, :],
                                out_offset=bass.IndirectOffsetOnAxis(ap=iT[:, e:e + 1], axis=0),
                                in_=ye[:, :], in_offset=None, compute_op=ALU.add)
    f_l = [P.slot(f"fl{i}") for i in range(4)]
    f_s = [P.slot(f"fs{i}") for i in range(4)]
    f_in = [s_acc.t, dve.t, act.t, pe.t]

    def row_load(tc):
        P.dma(sp, ER[tc % 4][:, 0:1024], D_acc[tc * 128:tc * 128 + 128, :], f_l[tc % 4], f_in)

    for tc in range(4):
        row_load(tc)
    for tc in range(8):
        i = tc % 4
        xr, yo = ER[i][:, 0:1024], ER[i][:, 1024:2048]
        ss = hN[:, i * 4:i * 4 + 1]
        a = A(yo, xr, AF.Square, accum_out=ss, w=[f_l[i].t, f_s[i].t])
        V("tensor_scalar", ss, ss, 1.0 / 1024, EPS, ALU.mult, ALU.add, w=[a])
        v = V("reciprocal", ss, ss)
        a = A(ss, ss, AF.Sqrt, w=[v])
        v = V("scalar_tensor_tensor", yo, xr, ss, fnw, ALU.mult, ALU.mult, w=[a, s_mf.t])
        P.dma(sp, out[tc * 128:tc * 128 + 128, :], yo, f_s[i], [v])
        if tc + 4 < 8:
            f_in = [v]
            row_load(tc + 4)
    sp.wait([s.t for s in P.slots])
    P.barrier()
    c1.close()

    block = ctx.enter_context(nc.Block())

    @block.tensor
    def _(e):
        pe.play(e)

    @block.scalar
    def _(e):
        act.play(e)

    @block.vector
    def _(e):
        dve.play(e)

    @block.gpsimd
    def _(e):
        pool.play(e)

    @block.sync
    def _(e):
        sp.play(e)

    ctx.close()


def chunks(w, cols):
    K = w.shape[0] // 128
    return w[:, cols].reshape(K, 128, -1).transpose(1, 0, 2)


def layout(x, **A):
    L = {}
    f = np.float32
    ar = np.arange
    L["xT"] = np.ascontiguousarray(x[0].T.reshape(8, 128, 1024))
    w = A["w_in"][0]
    pad = lambda *parts: np.concatenate(parts, 1)
    sw = np.r_[16:32, 0:16]
    kr = w[:, 640:672]
    z = lambda n: np.zeros((1024, n), f)
    krdt = np.concatenate([kr, w[:, 2464:2472], z(24), kr[:, sw], z(32)], 1)
    cols = [w[:, 0:640], krdt, w[:, 1696:2464], w[:, 2984:3496], w[:, 672:1184], w[:, 1184:1696],
            w[:, 2472:2984], w[:, 3496:7592]]
    w = np.concatenate(cols, 1)
    tile = lambda w: np.ascontiguousarray(
        w.reshape(w.shape[0] // 128, 128, w.shape[1] // 128, 128).transpose(2, 1, 0, 3)).reshape(
            w.shape[1] // 128, 128, -1)
    L["w_in"] = tile(w)
    uq = A["w_uq"][0].reshape(384, 8, 96)
    uq = np.concatenate([uq[:, :, :64].reshape(384, 512), uq[:, :, 64:].reshape(384, 256),
                         uq[:, :, 64:][:, :, sw].reshape(384, 256)], 1)
    L["w_uq"] = np.ascontiguousarray(tile(uq).transpose(1, 0, 2)).reshape(128, 8 * 384)
    ukv = A["w_ukv"][0].reshape(256, 8, 128)
    kn = tile(np.ascontiguousarray(ukv[:, :, :64]).reshape(256, 512)).transpose(1, 0, 2).reshape(128, 1024)
    vv = np.ascontiguousarray(ukv[:, :, 64:]).reshape(2, 128, 512).transpose(1, 0, 2).reshape(128, 1024)
    L["w_ukv"] = np.concatenate([kn, vv], 1)
    wl = np.zeros((2, 4, 128, 128), f)
    for s, n in enumerate(("lru_w_a", "lru_w_i")):
        for b in range(8):
            o = (b % 2) * 64
            wl[s, b // 2, o:o + 64, o:o + 64] = A[n][0, b]
    L["w_lru"] = np.ascontiguousarray(wl.reshape(8, 128, 128).transpose(1, 0, 2)).reshape(128, 1024)
    L["w_branch"] = np.concatenate([tile(A["w_branch"][0, b]) for b in range(4)])
    L["w_out"] = tile(A["w_out"][0])
    L["w_ff1"] = tile(A["w_ff1"][0])
    L["w_ff2"] = np.concatenate([tile(A["w_ff2"][0, q * 512:(q + 1) * 512]) for q in range(8)])
    L["w_ple_gate"] = tile(A["w_ple_gate"][0])
    L["w_ple"] = tile(A["w_ple"][0])
    L["pT"] = np.ascontiguousarray(A["p"][0, 0].T.reshape(2, 128, 1024).transpose(1, 0, 2)).reshape(128, 2048)
    L["w_ada"] = tile(A["w_ada_2"][0])
    L["fnorm"] = np.ascontiguousarray(A["final_norm_w_2"][None])
    L["ctxT"] = np.ascontiguousarray(A["ctx_2"][0].T.reshape(8, 128, 256).transpose(1, 0, 2)).reshape(128, 2048)
    w2 = A["w_in_2"][0]
    L["w_in2"] = tile(np.concatenate([w2[:, 1024:1056], np.zeros((1024, 96), f), w2[:, 256:512], w2[:, 512:1024],
                                      w2[:, 0:256], w2[:, 1056:1568], w2[:, 2080:2592], w2[:, 2592:3104],
                                      w2[:, 1568:2080], w2[:, 3104:3616]], 1))
    gw = np.zeros((32, 2, 256), f)
    for d in range(2):
        gw[16 * d:16 * d + 16, d] = A["gla_gate_w_2"][0, d]
    L["gla_gw"] = gw.reshape(32, 512)
    L["w_out2"] = tile(A["w_out_2"][0])
    L["w_router"] = np.ascontiguousarray(A["w_router_2"][0].reshape(8, 128, 16).transpose(1, 0, 2)).reshape(128, 128)
    row = np.broadcast_to(ar(16)[:, None], (16, 64)).reshape(-1).astype(f)
    cl = np.broadcast_to(ar(64)[None], (16, 64)).reshape(-1).astype(f)
    iv = (f(10000.0) ** (-ar(32, dtype=f) / f(32))).astype(f)
    ang = np.concatenate([iv[:, None] * row[None], iv[:, None] * cl[None]], 0).astype(f)
    L["rope2"] = np.stack([np.concatenate([np.cos(ang)] * 2), np.concatenate([np.sin(ang), -np.sin(ang)])]).astype(f)

    def cut(w, widths, K):
        w = w.reshape(16, K, 128, -1)
        out, at = [], 0
        for n in widths:
            out.append(w[:, :, :, at:at + n].transpose(0, 2, 1, 3).reshape(16, 128, K * n))
            at += n
        return np.concatenate(out, 2)

    L["wg"] = cut(A["w_exp_gate_2"][0], (384, 384, 384, 256), 8)
    L["wu"] = cut(A["w_exp_up_2"][0], (384, 384, 384, 256), 8)
    L["wd"] = cut(A["w_exp_down_2"][0], (256,) * 4, 11)
    L["w_pool"] = np.ascontiguousarray(A["w_pool"][0].transpose(1, 0, 2)).reshape(128, 512)
    L["positions"] = A["positions"]

    par = np.zeros((128, NPAR), f)

    def put(name, a):
        o, n = PO[name]
        par[:a.shape[0], o:o + n] = a

    col = lambda v: v.reshape(-1, 128).T
    put("g_mix", col(A["g_mix"][0]))
    put("q_norm", col(A["q_norm"][0]))
    put("kv_norm", col(A["kv_norm"][0]))
    put("pool_scale", col(A["pool_scale"][0]))
    put("conv_w", A["ssd_conv_w"][0].reshape(4, 6, 128).transpose(2, 1, 0).reshape(128, 24))
    put("conv_b", col(A["ssd_conv_b"][0]))
    put("ssd_norm", col(A["ssd_norm"][0]))
    put("ssd_d", col(np.repeat(A["ssd_d"][0], 64)))
    put("lconv_w", A["lru_conv_w"][0].reshape(4, 4, 128).transpose(2, 1, 0).reshape(128, 16))
    put("lconv_b", col(A["lru_conv_b"][0]))
    put("b_a", col(A["lru_b_a"][0]))
    put("b_i", col(A["lru_b_i"][0]))
    put("lam", col(A["lru_lambda"][0]))
    put("g_mlp", col(A["g_mlp"][0]))
    put("g_ple", col(A["g_ple"][0]))
    put("g_final", col(A["g_final"]))
    put("norm1", col(A["norm1_w_2"][0]))
    put("norm2", col(A["norm2_w_2"][0]))
    put("b_ada", col(A["b_ada_2"][0]))
    put("gate_b", col(A["gla_gate_b_2"][0].reshape(-1)))
    put("gla_norm", col(A["gla_norm_w_2"][0]))
    put("ret_norm", col(A["ret_norm_w_2"][0]))
    put("cc", np.stack([col(A["c_2"][0]), col(A["c_ctx_2"])], 2).reshape(128, 16))
    put("dt_bias", A["ssd_dt_bias"][0][:, None])
    put("a_log", A["ssd_a_log"][0][:, None])
    put("ret_logit", np.broadcast_to(A["ret_decay_logit_2"][0].reshape(1, 8), (128, 8)))
    L["par"] = par

    con = np.zeros((128, NCON), f)

    def putc(name, a):
        o, n = CO[name]
        con[:a.shape[0], o:o + n] = a

    p, q = ar(128)[:, None], ar(128)[None, :]
    putc("ident", np.eye(128, dtype=f))
    putc("ones", np.ones((128, 128), f))
    putc("mle", (p <= q).astype(f))
    putc("mge", (p >= q).astype(f))
    putc("mneg", np.where(q > p, f(-1e30), f(0)))
    inv = (f(1.0) / (f(10000.0) ** (ar(0, 32, 2, dtype=f) / f(32)))).astype(f)
    putc("inv", inv[ar(128) % 16][:, None])
    putc("sgn", np.where(ar(128) % 32 < 16, f(-1), f(1))[:, None])
    ic = np.concatenate([1.0 / np.minimum(ar(16) + 1, ww) for ww in (2, 4, 8, 16)])
    putc("icnt", np.broadcast_to(ic[None].astype(f), (128, 64)))
    putc("relf", np.maximum(q - p, 0).astype(f))
    putc("relb", np.maximum(p - q, 0).astype(f))
    putc("posf", np.broadcast_to((q + 1).astype(f), (128, 128)))
    putc("posb", np.broadcast_to((128 - q).astype(f), (128, 128)))
    putc("colf", (127 - p).astype(f))
    putc("colb", p.astype(f))
    s8 = np.zeros((8, 8, 128), f)
    s8[ar(8), ar(8)] = 1
    L["scon"] = np.stack([np.broadcast_to((ar(1024) % 128 != 0).astype(f)[None], (8, 1024)), s8.reshape(8, 1024)])
    L["con"] = con
    return L


def kernel(**inputs):
    import numpy as _np
    import concourse.bacc as _bacc
    from concourse import mybir as _mybir
    from concourse.bass_utils import run_bass_kernel_spmd as _run

    L = layout(**{k: _np.asarray(v) for k, v in inputs.items()})
    nc = _bacc.Bacc("TRN2", target_bir_lowering=False, num_devices=1)
    arrays, I = {}, {}
    for name, a in L.items():
        a = _np.ascontiguousarray(a)
        arrays[f"in_{name}_dram"] = a
        I[name] = nc.dram_tensor(f"in_{name}_dram", a.shape, _mybir.dt.from_np(a.dtype), kind="ExternalInput").ap()
    out = nc.dram_tensor("out_0_dram", (1024, 1024), F32, kind="ExternalOutput").ap()
    program(nc, I, out)
    r = _run(nc, [arrays], core_ids=[0])
    return r.results[0]["out_0_dram"].reshape(1, 1024, 1024)
```
